# Optimizing a Trainium2 kernel written in Bass

```python
import jax, jax.numpy as jnp
from jax import lax
import numpy as np
import math

D_MODEL = 1024
BATCH = 1
SEQ = 256
DEPTH = 2

GRID_W = 64
WIN_H_MAX = 8
WIN_W = 16
COL_BLOCK = 16
COL_SLAB = 32
NA_HEADS = 8
NA_HEAD_DIM = 64
NA_WIDTH = NA_HEADS * NA_HEAD_DIM
GLA_HEADS = 4
GLA_DK = 64
GLA_DV = 128
GLA_QK_WIDTH = GLA_HEADS * GLA_DK
GLA_V_WIDTH = GLA_HEADS * GLA_DV
GLA_GATE_RANK = 16
GLA_TAU = 16.0
GLA_CHUNK = 64
MIX_WIDTH = NA_WIDTH + GLA_V_WIDTH
IN_SPLITS = (NA_WIDTH, NA_WIDTH, NA_WIDTH,
             GLA_QK_WIDTH, GLA_QK_WIDTH,
             GLA_V_WIDTH, GLA_V_WIDTH,
             GLA_GATE_RANK, GLA_GATE_RANK)
IN_WIDTH = sum(IN_SPLITS)
D_FF = 2816
EPS = 1e-6
NEG_INF = -1e30


def rmsnorm(x, g):
    xf = x.astype(jnp.float32)
    y = xf * lax.rsqrt(jnp.mean(xf * xf, axis=-1, keepdims=True) + EPS)
    return (y * g.astype(jnp.float32)).astype(x.dtype)

def swiglu(h, w_gate, w_up, w_down):
    return (jax.nn.silu(h @ w_gate) * (h @ w_up)) @ w_down

def split_heads(a, n):
    b, s, w = a.shape
    return a.reshape(b, s, n, w // n).transpose(0, 2, 1, 3)

def merge_heads(a):
    b, n, s, d = a.shape
    return a.transpose(0, 2, 1, 3).reshape(b, s, n * d)

def neighbourhood_attention(q, k, v, rpb):
    B, H, S, d = q.shape
    rows = S // GRID_W
    wh = min(WIN_H_MAX, rows)
    q = q.reshape(B, H, rows, GRID_W, d)
    k = k.reshape(B, H, rows, GRID_W, d)
    v = v.reshape(B, H, rows, GRID_W, d)
    r = np.arange(rows)
    row_start = np.clip(r - wh // 2, 0, rows - wh)
    key_rows = row_start[:, None] + np.arange(wh)[None, :]
    dr = key_rows - r[:, None] + (WIN_H_MAX - 1)
    scale = NA_HEAD_DIM ** -0.5
    outs = []
    for j in range(GRID_W // COL_BLOCK):
        qc = np.arange(j * COL_BLOCK, (j + 1) * COL_BLOCK)
        col_start = np.clip(qc - WIN_W // 2, 0, GRID_W - WIN_W)
        c0 = int(np.clip(j * COL_BLOCK - WIN_W // 2, 0, GRID_W - COL_SLAB))
        kc = c0 + np.arange(COL_SLAB)
        valid = (kc[None, :] >= col_start[:, None]) & (kc[None, :] < col_start[:, None] + WIN_W)
        dc = np.clip(kc[None, :] - qc[:, None] + (WIN_W - 1), 0, 2 * WIN_W - 2)
        qb = q[:, :, :, j * COL_BLOCK:(j + 1) * COL_BLOCK]
        kb = k[:, :, :, c0:c0 + COL_SLAB][:, :, key_rows]
        vb = v[:, :, :, c0:c0 + COL_SLAB][:, :, key_rows]
        s = jnp.einsum('bhrqd,bhrwkd->bhrqwk', qb, kb).astype(jnp.float32) * scale
        bias = rpb[:, dr[:, None, :, None], dc[None, :, None, :]]
        s = s + bias[None].astype(jnp.float32)
        s = jnp.where(valid[:, None, :], s, NEG_INF)
        p = jax.nn.softmax(s.reshape(B, H, rows, COL_BLOCK, wh * COL_SLAB), axis=-1)
        p = p.reshape(B, H, rows, COL_BLOCK, wh, COL_SLAB).astype(v.dtype)
        outs.append(jnp.einsum('bhrqwk,bhrwkd->bhrqd', p, vb))
    o = jnp.concatenate(outs, axis=3)
    return o.reshape(B, H, S, d)

def gla_chunked(q, k, v, g, include_diag):
    B, H, T, dk = q.shape
    dv = v.shape[-1]
    n = T // GLA_CHUNK

    def to_chunks(a):
        return jnp.moveaxis(a.reshape(B, H, n, GLA_CHUNK, a.shape[-1]), 2, 0)

    t = np.arange(GLA_CHUNK)
    mask = (t[:, None] >= t[None, :]) if include_diag else (t[:, None] > t[None, :])

    def step(state, inp):
        qi, ki, vi, gi = inp
        b = jnp.cumsum(gi, axis=-2)
        inter = jnp.einsum('bhtd,bhde->bhte', qi * jnp.exp(b), state)
        diff = b[:, :, :, None, :] - b[:, :, None, :, :]
        decay = jnp.exp(jnp.where(mask[:, :, None], diff, -jnp.inf))
        a = jnp.einsum('bhtd,bhsd,bhtsd->bhts', qi, ki, decay)
        intra = jnp.einsum('bhts,bhse->bhte', a, vi)
        b_last = b[:, :, -1:, :]
        state = (jnp.exp(b_last[:, :, 0, :])[..., None] * state
                 + jnp.einsum('bhsd,bhse->bhde', ki * jnp.exp(b_last - b), vi))
        return state, inter + intra

    s0 = jnp.zeros((B, H, dk, dv), jnp.float32)
    _, o = lax.scan(step, s0, (to_chunks(q), to_chunks(k), to_chunks(v), to_chunks(g)))
    return jnp.moveaxis(o, 0, 2).reshape(B, H, T, dv)

def hybrid_layer(x, ffn1_norm, ffn1_wg, ffn1_wu, ffn1_wd, mix_norm, w_in, na_rpb, na_gain,
                 w_gate_f, b_gate_f, w_gate_b, b_gate_b, gla_gain, w_out,
                 ffn2_norm, ffn2_wg, ffn2_wu, ffn2_wd):
    x = x + 0.5 * swiglu(rmsnorm(x, ffn1_norm), ffn1_wg, ffn1_wu, ffn1_wd)

    h = rmsnorm(x, mix_norm)
    proj = h @ w_in
    offsets = list(np.cumsum(IN_SPLITS)[:-1])
    na_q, na_k, na_v, g_q, g_k, g_v, g_r, gf_code, gb_code = jnp.split(proj, offsets, axis=-1)

    na_o = neighbourhood_attention(split_heads(na_q, NA_HEADS), split_heads(na_k, NA_HEADS),
                                   split_heads(na_v, NA_HEADS), na_rpb)
    na_o = rmsnorm(merge_heads(na_o), na_gain)

    f32 = jnp.float32
    qg = split_heads(g_q, GLA_HEADS).astype(f32) * (GLA_DK ** -0.5)
    kg = split_heads(g_k, GLA_HEADS).astype(f32)
    vg = split_heads(g_v, GLA_HEADS).astype(f32)
    log_gf = jax.nn.log_sigmoid((gf_code @ w_gate_f + b_gate_f).astype(f32)) / GLA_TAU
    log_gb = jax.nn.log_sigmoid((gb_code @ w_gate_b + b_gate_b).astype(f32)) / GLA_TAU
    log_gf = split_heads(log_gf, GLA_HEADS)
    log_gb = split_heads(log_gb, GLA_HEADS)
    o_fwd = gla_chunked(qg, kg, vg, log_gf, True)
    flip = lambda a: jnp.flip(a, axis=2)
    o_bwd = flip(gla_chunked(flip(qg), flip(kg), flip(vg), flip(log_gb), False))
    gla_o = rmsnorm(o_fwd + o_bwd, gla_gain).astype(x.dtype)
    gla_o = merge_heads(gla_o) * jax.nn.silu(g_r)

    x = x + jnp.concatenate([na_o, gla_o], axis=-1) @ w_out

    x = x + 0.5 * swiglu(rmsnorm(x, ffn2_norm), ffn2_wg, ffn2_wu, ffn2_wd)
    return x

def first_inputs(seed: int = 0) -> dict:
    key = jax.random.key(seed)
    ks = iter(jax.random.split(key, 32))
    nrm = lambda shape, s: jax.random.normal(next(ks), shape, jnp.float32) * s
    gain = lambda shape: 1.0 + nrm(shape, 0.02)
    L, D = DEPTH, D_MODEL
    return {
        "x": nrm((BATCH, SEQ, D), 1.0),
        "ffn1_norm": gain((L, D)),
        "ffn1_wg": nrm((L, D, D_FF), D ** -0.5),
        "ffn1_wu": nrm((L, D, D_FF), D ** -0.5),
        "ffn1_wd": nrm((L, D_FF, D), D_FF ** -0.5),
        "mix_norm": gain((L, D)),
        "w_in": nrm((L, D, IN_WIDTH), D ** -0.5),
        "na_rpb": nrm((L, NA_HEADS, 2 * WIN_H_MAX - 1, 2 * WIN_W - 1), 0.1),
        "na_gain": gain((L, NA_WIDTH)),
        "w_gate_f": nrm((L, GLA_GATE_RANK, GLA_QK_WIDTH), GLA_GATE_RANK ** -0.5),
        "b_gate_f": nrm((L, GLA_QK_WIDTH), 0.1),
        "w_gate_b": nrm((L, GLA_GATE_RANK, GLA_QK_WIDTH), GLA_GATE_RANK ** -0.5),
        "b_gate_b": nrm((L, GLA_QK_WIDTH), 0.1),
        "gla_gain": gain((L, GLA_DV)),
        "w_out": nrm((L, MIX_WIDTH, D), MIX_WIDTH ** -0.5),
        "ffn2_norm": gain((L, D)),
        "ffn2_wg": nrm((L, D, D_FF), D ** -0.5),
        "ffn2_wu": nrm((L, D, D_FF), D ** -0.5),
        "ffn2_wd": nrm((L, D_FF, D), D_FF ** -0.5),
        "final_norm": gain((D,)),
    }

def first_block(x, ffn1_norm, ffn1_wg, ffn1_wu, ffn1_wd, mix_norm, w_in, na_rpb, na_gain,
              w_gate_f, b_gate_f, w_gate_b, b_gate_b, gla_gain, w_out,
              ffn2_norm, ffn2_wg, ffn2_wu, ffn2_wd, final_norm):
    for l in range(DEPTH):
        x = hybrid_layer(x, ffn1_norm[l], ffn1_wg[l], ffn1_wu[l], ffn1_wd[l], mix_norm[l], w_in[l],
                         na_rpb[l], na_gain[l], w_gate_f[l], b_gate_f[l], w_gate_b[l], b_gate_b[l],
                         gla_gain[l], w_out[l], ffn2_norm[l], ffn2_wg[l], ffn2_wu[l], ffn2_wd[l])
    return rmsnorm(x, final_norm)


N_EVEN = (DEPTH + 1) // 2
N_ODD = DEPTH // 2
ROPE_THETA = 500000.0
HEAD_DIM = 64
ROT_DIM = HEAD_DIM // 4
Q_BLOCK = 128
NEG = -1e30
BIG = 1e30

LRU_WIDTH = D_MODEL // 2
LRU_BLOCKS = 8
LRU_BLOCK_DIM = LRU_WIDTH // LRU_BLOCKS
CONV_WIDTH = 4
LRU_C = 8.0
MOBA_HEADS = (D_MODEL // 2) // HEAD_DIM
MOBA_WIDTH = MOBA_HEADS * HEAD_DIM
MOBA_BLOCK = 256
MOBA_TOPK = 3
IN0_WIDTH = 2 * LRU_WIDTH + 3 * MOBA_WIDTH
MIX0_WIDTH = LRU_WIDTH + MOBA_WIDTH

NSA_HEADS = D_MODEL // HEAD_DIM
NSA_KV_GROUPS = 2
NSA_HPG = NSA_HEADS // NSA_KV_GROUPS
CMP_LEN = 32
CMP_STRIDE = 16
SEL_BLOCK = 64
SEL_TOPK = 16
WINDOW = 512
CMP_HIDDEN = 128
NSA_QD = NSA_HEADS * HEAD_DIM
NSA_KVD = NSA_KV_GROUPS * HEAD_DIM
IN1_WIDTH = NSA_QD + 6 * NSA_KVD + 3 * NSA_HEADS
MIX1_WIDTH = NSA_QD


def rmsnorm_2(x, g):
    xf = x.astype(jnp.float32)
    y = xf * lax.rsqrt(jnp.mean(xf * xf, axis=-1, keepdims=True) + EPS)
    return (y * g.astype(jnp.float32)).astype(x.dtype)

def modulate(h, shift, scale):
    return h * (1.0 + scale[:, None, :]) + shift[:, None, :]

def swiglu_2(h, w1, w2):
    a, b = jnp.split(h @ w1, 2, axis=-1)
    return (jax.nn.silu(a) * b) @ w2

def rope_partial(x, pos):
    half = ROT_DIM // 2
    freqs = ROPE_THETA ** (-jnp.arange(half, dtype=jnp.float32) * 2.0 / ROT_DIM)
    ang = pos[:, None] * freqs[None, :]
    cos = jnp.cos(ang).astype(x.dtype)
    sin = jnp.sin(ang).astype(x.dtype)
    x1 = x[..., :half]
    x2 = x[..., half:ROT_DIM]
    return jnp.concatenate([x1 * cos - x2 * sin, x2 * cos + x1 * sin, x[..., ROT_DIM:]], axis=-1)

def masked_softmax(logits, mask):
    p = jax.nn.softmax(jnp.where(mask, logits, NEG), axis=-1)
    return jnp.where(mask, p, 0.0)

def causal_depthwise_conv(x, w, b):
    y = lax.conv_general_dilated(x, w[:, None, :], window_strides=(1,),
                                 padding=((CONV_WIDTH - 1, 0),),
                                 dimension_numbers=('NWC', 'WIO', 'NWC'),
                                 feature_group_count=x.shape[-1])
    return y + b

def rg_lru(x, wa, ba, wx, bx, lam):
    B, S, C = x.shape
    xb = x.reshape(B, S, LRU_BLOCKS, LRU_BLOCK_DIM)
    r = jax.nn.sigmoid(jnp.einsum('bsni,nij->bsnj', xb, wa) + ba).reshape(B, S, C)
    i = jax.nn.sigmoid(jnp.einsum('bsni,nij->bsnj', xb, wx) + bx).reshape(B, S, C)
    log_a = -LRU_C * r.astype(jnp.float32) * jax.nn.softplus(-lam.astype(jnp.float32))
    a = jnp.exp(log_a)
    mult = jnp.sqrt(-jnp.expm1(2.0 * log_a))
    bterm = mult * (i * x).astype(jnp.float32)

    def combine(left, right):
        a_l, b_l = left
        a_r, b_r = right
        return a_l * a_r, a_r * b_l + b_r

    _, h = lax.associative_scan(combine, (a, bterm), axis=1)
    return h.astype(x.dtype)

def moba_attention(q, k, v):
    B, H, S, dh = q.shape
    scale = dh ** -0.5
    nb = -(-S // MOBA_BLOCK)
    pad = nb * MOBA_BLOCK - S
    kp = jnp.pad(k, ((0, 0), (0, 0), (0, pad), (0, 0))).reshape(B, H, nb, MOBA_BLOCK, dh)
    vp = jnp.pad(v, ((0, 0), (0, 0), (0, pad), (0, 0))).reshape(B, H, nb, MOBA_BLOCK, dh)
    centroid = jnp.mean(kp.astype(jnp.float32), axis=3)
    t = jnp.arange(S)
    qblk = t // MOBA_BLOCK
    gate = jnp.einsum('bhsd,bhnd->bhsn', q.astype(jnp.float32), centroid)
    past = jnp.arange(nb)[None, :] < qblk[:, None]
    gate = jnp.where(past, gate, -jnp.inf)
    _, top_idx = lax.top_k(gate, min(MOBA_TOPK, nb))
    own = jnp.broadcast_to(qblk[:, None], (B, H, S, 1)).astype(top_idx.dtype)
    sel_idx = jnp.concatenate([top_idx, own], axis=-1)
    sel_valid = jnp.concatenate([top_idx < qblk[:, None], jnp.ones((B, H, S, 1), bool)], axis=-1)

    nq = S // Q_BLOCK

    def to_blocks(a):
        return jnp.moveaxis(a.reshape(B, H, nq, Q_BLOCK, *a.shape[3:]), 2, 0)

    b_ix = jnp.arange(B)[:, None, None, None]
    h_ix = jnp.arange(H)[None, :, None, None]
    offs = jnp.arange(MOBA_BLOCK)

    def step(args):
        qb, idx, valid, t0 = args
        kg = kp[b_ix, h_ix, idx]
        vg = vp[b_ix, h_ix, idx]
        s = jnp.einsum('bhqd,bhqnkd->bhqnk', qb, kg).astype(jnp.float32) * scale
        tq = t0 + jnp.arange(Q_BLOCK)
        kpos = idx[..., None] * MOBA_BLOCK + offs
        mask = valid[..., None] & (kpos <= tq[:, None, None])
        p = masked_softmax(s.reshape(B, H, Q_BLOCK, -1), mask.reshape(B, H, Q_BLOCK, -1)).reshape(s.shape)
        return jnp.einsum('bhqnk,bhqnkd->bhqd', p.astype(v.dtype), vg)

    out = lax.map(step, (to_blocks(q), to_blocks(sel_idx), to_blocks(sel_valid), jnp.arange(nq) * Q_BLOCK))
    return jnp.moveaxis(out, 0, 2).reshape(B, H, S, dh)

def mixer_lru_moba(h, in_w, conv_w, conv_b, wa, ba, wx, bx, lam, out_w, pos):
    B, S, _ = h.shape
    u = h @ in_w
    o1 = LRU_WIDTH
    o2 = 2 * LRU_WIDTH
    x_lru, g_lru, q, k, v = jnp.split(u, [o1, o2, o2 + MOBA_WIDTH, o2 + 2 * MOBA_WIDTH], axis=-1)
    xc = causal_depthwise_conv(x_lru, conv_w, conv_b)
    y_lru = rg_lru(xc, wa, ba, wx, bx, lam) * jax.nn.gelu(g_lru)

    def heads(a):
        return a.reshape(B, S, MOBA_HEADS, HEAD_DIM).transpose(0, 2, 1, 3)

    q = rope_partial(heads(q), pos)
    k = rope_partial(heads(k), pos)
    y_att = moba_attention(q, k, heads(v)).transpose(0, 2, 1, 3).reshape(B, S, MOBA_WIDTH)
    return jnp.concatenate([y_lru, y_att], axis=-1) @ out_w

def compress(kv, pos_emb, w1, w2):
    B, G, S, dh = kv.shape
    c = kv.reshape(B, G, S // CMP_STRIDE, CMP_STRIDE, dh)
    blocks = jnp.concatenate([c[:, :, :-1], c[:, :, 1:]], axis=3)
    nc = blocks.shape[2]
    blocks = (blocks + pos_emb).reshape(B, G, nc, CMP_LEN * dh)
    return jax.nn.gelu(blocks @ w1) @ w2

def mixer_nsa(h, in_w, cmp_pos, cmp_w1, cmp_w2, out_w, pos):
    B, S, _ = h.shape
    G, R, dh = NSA_KV_GROUPS, NSA_HPG, HEAD_DIM
    scale = dh ** -0.5
    u = h @ in_w
    cuts = [NSA_QD + i * NSA_KVD for i in range(7)]
    q, kc, vc, ks, vs, kw, vw, gl = jnp.split(u, cuts, axis=-1)
    q = q.reshape(B, S, G, R, dh).transpose(0, 2, 3, 1, 4)

    def kvh(a):
        return a.reshape(B, S, G, dh).transpose(0, 2, 1, 3)

    q_rope = rope_partial(q, pos)
    kcmp = compress(kvh(kc), cmp_pos[0], cmp_w1[0], cmp_w2[0])
    vcmp = compress(kvh(vc), cmp_pos[1], cmp_w1[1], cmp_w2[1])
    nc = kcmp.shape[2]
    ns = S // SEL_BLOCK
    ks_blocks = rope_partial(kvh(ks), pos).reshape(B, G, ns, SEL_BLOCK, dh)
    vs_blocks = kvh(vs).reshape(B, G, ns, SEL_BLOCK, dh)
    kw_pad = jnp.pad(rope_partial(kvh(kw), pos), ((0, 0), (0, 0), (WINDOW, 0), (0, 0)))
    vw_pad = jnp.pad(kvh(vw), ((0, 0), (0, 0), (WINDOW, 0), (0, 0)))
    gates = jax.nn.sigmoid(gl).reshape(B, S, NSA_HEADS, 3)

    cmp_end = jnp.arange(nc) * CMP_STRIDE + CMP_LEN - 1
    ci = jnp.arange(nc)[:, None] * CMP_STRIDE
    sj = jnp.arange(ns)[None, :] * SEL_BLOCK
    overlap = jnp.clip(jnp.minimum(ci + CMP_LEN, sj + SEL_BLOCK) - jnp.maximum(ci, sj), 0, None).astype(jnp.float32) / CMP_LEN
    n_sel = min(SEL_TOPK, ns)
    b_ix = jnp.arange(B)[:, None, None, None]
    g_ix = jnp.arange(G)[None, :, None, None]
    offs = jnp.arange(SEL_BLOCK)
    jn = jnp.arange(ns)
    nq = S // Q_BLOCK

    def to_blocks(a):
        return jnp.moveaxis(a.reshape(B, G, R, nq, Q_BLOCK, dh), 3, 0)

    def step(args):
        qn, qr, t0 = args
        tq = t0 + jnp.arange(Q_BLOCK)
        s_c = jnp.einsum('bgrqd,bgcd->bgrqc', qn, kcmp).astype(jnp.float32) * scale
        p_c = masked_softmax(s_c, cmp_end[None, :] <= tq[:, None])
        o_c = jnp.einsum('bgrqc,bgcd->bgrqd', p_c.astype(vcmp.dtype), vcmp)
        imp = jnp.einsum('bgrqc,cn->bgqn', p_c, overlap)
        blk_t = tq // SEL_BLOCK
        forced = (jn[None, :] == 0) | (jn[None, :] == blk_t[:, None]) | (jn[None, :] == blk_t[:, None] - 1)
        imp = jnp.where(forced, BIG, imp)
        imp = jnp.where(jn[None, :] <= blk_t[:, None], imp, -jnp.inf)
        _, idx = lax.top_k(imp, n_sel)
        kg = ks_blocks[b_ix, g_ix, idx]
        vg = vs_blocks[b_ix, g_ix, idx]
        s_s = jnp.einsum('bgrqd,bgqnkd->bgrqnk', qr, kg).astype(jnp.float32) * scale
        kpos = idx[..., None] * SEL_BLOCK + offs
        m_s = (kpos <= tq[:, None, None])[:, :, None]
        p_s = masked_softmax(s_s.reshape(B, G, R, Q_BLOCK, -1), m_s.reshape(B, G, 1, Q_BLOCK, -1)).reshape(s_s.shape)
        o_s = jnp.einsum('bgrqnk,bgqnkd->bgrqd', p_s.astype(vg.dtype), vg)
        kwb = lax.dynamic_slice_in_dim(kw_pad, t0, Q_BLOCK + WINDOW, axis=2)
        vwb = lax.dynamic_slice_in_dim(vw_pad, t0, Q_BLOCK + WINDOW, axis=2)
        s_w = jnp.einsum('bgrqd,bgkd->bgrqk', qr, kwb).astype(jnp.float32) * scale
        kpos_w = t0 - WINDOW + jnp.arange(Q_BLOCK + WINDOW)
        diff = tq[:, None] - kpos_w[None, :]
        m_w = (diff >= 0) & (diff < WINDOW) & (kpos_w[None, :] >= 0)
        p_w = masked_softmax(s_w, m_w)
        o_w = jnp.einsum('bgrqk,bgkd->bgrqd', p_w.astype(vwb.dtype), vwb)
        return jnp.stack([o_c, o_s, o_w], axis=-2)

    out = lax.map(step, (to_blocks(q), to_blocks(q_rope), jnp.arange(nq) * Q_BLOCK))
    out = out.transpose(1, 0, 4, 2, 3, 5, 6).reshape(B, S, NSA_HEADS, 3, dh)
    y = jnp.einsum('bshc,bshcd->bshd', gates, out).reshape(B, S, MIX1_WIDTH)
    return y @ out_w

def second_inputs(seed: int = 0) -> dict:
    key = jax.random.key(seed)
    ks = jax.random.split(key, 24)
    f32 = jnp.float32
    D = D_MODEL

    def nrm(k, shape, s):
        return s * jax.random.normal(k, shape, f32)

    a8 = jax.random.uniform(ks[14], (N_EVEN, LRU_WIDTH), f32, 0.9, 0.999)
    sig = a8 ** (1.0 / LRU_C)
    return {
        "x": nrm(ks[0], (BATCH, SEQ, D), 1.0),
        "c": nrm(ks[1], (BATCH, D), 1.0),
        "mod_w": nrm(ks[2], (DEPTH, D, 9 * D), 0.5 * D ** -0.5),
        "mod_b": nrm(ks[3], (DEPTH, 9 * D), 0.02),
        "norm_g": 1.0 + nrm(ks[4], (DEPTH, 3, D), 0.05),
        "ffn_w1": nrm(ks[5], (DEPTH, 2, D, 2 * D_FF), D ** -0.5),
        "ffn_w2": nrm(ks[6], (DEPTH, 2, D_FF, D), D_FF ** -0.5),
        "mix0_in_w": nrm(ks[7], (N_EVEN, D, IN0_WIDTH), D ** -0.5),
        "lru_conv_w": nrm(ks[8], (N_EVEN, CONV_WIDTH, LRU_WIDTH), CONV_WIDTH ** -0.5),
        "lru_conv_b": nrm(ks[9], (N_EVEN, LRU_WIDTH), 0.02),
        "lru_wa": nrm(ks[10], (N_EVEN, LRU_BLOCKS, LRU_BLOCK_DIM, LRU_BLOCK_DIM), LRU_BLOCK_DIM ** -0.5),
        "lru_ba": nrm(ks[11], (N_EVEN, LRU_BLOCKS, LRU_BLOCK_DIM), 0.02),
        "lru_wx": nrm(ks[12], (N_EVEN, LRU_BLOCKS, LRU_BLOCK_DIM, LRU_BLOCK_DIM), LRU_BLOCK_DIM ** -0.5),
        "lru_bx": nrm(ks[13], (N_EVEN, LRU_BLOCKS, LRU_BLOCK_DIM), 0.02),
        "lru_lambda": jnp.log(sig) - jnp.log1p(-sig),
        "mix0_out_w": nrm(ks[15], (N_EVEN, MIX0_WIDTH, D), MIX0_WIDTH ** -0.5),
        "mix1_in_w": nrm(ks[16], (N_ODD, D, IN1_WIDTH), D ** -0.5),
        "cmp_pos": nrm(ks[17], (N_ODD, 2, CMP_LEN, HEAD_DIM), 0.1),
        "cmp_w1": nrm(ks[18], (N_ODD, 2, CMP_LEN * HEAD_DIM, CMP_HIDDEN), (CMP_LEN * HEAD_DIM) ** -0.5),
        "cmp_w2": nrm(ks[19], (N_ODD, 2, CMP_HIDDEN, HEAD_DIM), CMP_HIDDEN ** -0.5),
        "mix1_out_w": nrm(ks[20], (N_ODD, MIX1_WIDTH, D), MIX1_WIDTH ** -0.5),
        "final_norm_g": 1.0 + nrm(ks[21], (D,), 0.05),
    }

def second_block(x, c, mod_w, mod_b, norm_g, ffn_w1, ffn_w2, mix0_in_w, lru_conv_w, lru_conv_b,
              lru_wa, lru_ba, lru_wx, lru_bx, lru_lambda, mix0_out_w, mix1_in_w, cmp_pos,
              cmp_w1, cmp_w2, mix1_out_w, final_norm_g):
    B, S, D = x.shape
    pos = jnp.arange(S, dtype=jnp.float32)
    cond = jax.nn.silu(c)
    for l in range(DEPTH):
        mod = (cond @ mod_w[l] + mod_b[l]).reshape(B, 9, D)
        h = modulate(rmsnorm_2(x, norm_g[l, 0]), mod[:, 0], mod[:, 1])
        x = x + 0.5 * mod[:, 2][:, None, :] * swiglu_2(h, ffn_w1[l, 0], ffn_w2[l, 0])
        h = modulate(rmsnorm_2(x, norm_g[l, 1]), mod[:, 3], mod[:, 4])
        j = l // 2
        if l % 2 == 0:
            y = mixer_lru_moba(h, mix0_in_w[j], lru_conv_w[j], lru_conv_b[j], lru_wa[j], lru_ba[j],
                               lru_wx[j], lru_bx[j], lru_lambda[j], mix0_out_w[j], pos)
        else:
            y = mixer_nsa(h, mix1_in_w[j], cmp_pos[j], cmp_w1[j], cmp_w2[j], mix1_out_w[j], pos)
        x = x + mod[:, 5][:, None, :] * y
        h = modulate(rmsnorm_2(x, norm_g[l, 2]), mod[:, 6], mod[:, 7])
        x = x + 0.5 * mod[:, 8][:, None, :] * swiglu_2(h, ffn_w1[l, 1], ffn_w2[l, 1])
    return rmsnorm_2(x, final_norm_g)


def setup_inputs(seed=0):
    out = dict(first_inputs(seed))
    for name, value in second_inputs(seed + 1).items():
        if name != "x":
            out[name + "_2"] = value
    return out


def reference(
    x, ffn1_norm, ffn1_wg, ffn1_wu, ffn1_wd, mix_norm, w_in, na_rpb, na_gain, w_gate_f,
    b_gate_f, w_gate_b, b_gate_b, gla_gain, w_out, ffn2_norm, ffn2_wg, ffn2_wu, ffn2_wd,
    final_norm, c_2, mod_w_2, mod_b_2, norm_g_2, ffn_w1_2, ffn_w2_2, mix0_in_w_2, lru_conv_w_2,
    lru_conv_b_2, lru_wa_2, lru_ba_2, lru_wx_2, lru_bx_2, lru_lambda_2, mix0_out_w_2,
    mix1_in_w_2, cmp_pos_2, cmp_w1_2, cmp_w2_2, mix1_out_w_2, final_norm_g_2,
):
    x = first_block(
        x, ffn1_norm, ffn1_wg, ffn1_wu, ffn1_wd, mix_norm, w_in, na_rpb, na_gain, w_gate_f,
        b_gate_f, w_gate_b, b_gate_b, gla_gain, w_out, ffn2_norm, ffn2_wg, ffn2_wu, ffn2_wd,
        final_norm,
    )
    return second_block(
        x, c_2, mod_w_2, mod_b_2, norm_g_2, ffn_w1_2, ffn_w2_2, mix0_in_w_2, lru_conv_w_2,
        lru_conv_b_2, lru_wa_2, lru_ba_2, lru_wx_2, lru_bx_2, lru_lambda_2, mix0_out_w_2,
        mix1_in_w_2, cmp_pos_2, cmp_w1_2, cmp_w2_2, mix1_out_w_2, final_norm_g_2,
    )


_drawn_inputs = setup_inputs


def setup_inputs(seed=0):
    import zlib

    import numpy as np

    out = dict(_drawn_inputs(seed))
    spreads = {}
    factors = {'ffn1_norm': 3.652,
     'na_gain': 13.404,
     'b_gate_f': 3.888,
     'b_gate_b': 4.094,
     'gla_gain': 19.523,
     'ffn2_norm': 6.053,
     'final_norm': 7.857,
     'lru_conv_b_2': 41.88,
     'lru_ba_2': 200.0,
     'lru_bx_2': 200.0,
     'cmp_pos_2': 23.129,
     'mod_b_2': 5.027,
     'norm_g_2': 6.82,
     'lru_wa_2': 4.7,
     'lru_lambda_2': 2.78}
    for name, (base, spread) in spreads.items():
        noise = np.random.default_rng([zlib.crc32(name.encode()), seed]).standard_normal(out[name].shape)
        drawn = base * np.exp(spread * noise) if base else spread * noise
        out[name] = __import__('jax').numpy.asarray(drawn.astype(out[name].dtype))
    for name, factor in factors.items():
        out[name] = (out[name] * factor).astype(out[name].dtype)
    return out
```

```python
from contextlib import ExitStack, contextmanager

import numpy as np

import concourse.bass as bass
from concourse import mybir

F32 = mybir.dt.float32
U32 = mybir.dt.uint32
ALU = mybir.AluOpType
ACT = mybir.ActivationFunctionType
AXX = mybir.AxisListType.X

P = 128
S = 256
TB = S // P
D = 1024
KC = D // P
FF = 2816
FC = FF // P
LAYERS = 2
FFNS = 2 * 2 * LAYERS
EPS = 1e-6
NEG = -1e30
RING = 2
SLOT = 2 * KC * P

GRID_W, ROWS, WIN_H, WIN_W = 64, S // 64, 8, 16
NA_HEADS, DH = 8, 64
GLA_HEADS, GLA_TAU, GLA_RANK = 4, 16.0, 16
SCALE = DH ** -0.5
NSA_HEADS, NSA_GROUPS = 16, 2
CMP_LEN, CMP_STRIDE = 32, 16
NCMP = S // CMP_STRIDE - 1
CMP_PAIRS = CMP_LEN // 2

M1_SLOTS = 12
M2_SLOTS = 10
M3_SLOTS = 10
OUT_SLOTS = D // (2 * P)
TOTAL_SLOTS = FFNS * FC + LAYERS * (M1_SLOTS + OUT_SLOTS) + M2_SLOTS + M3_SLOTS + 2 * OUT_SLOTS
GLA_LEVELS = [256, 128, 64, 32, 16, 8, 4, 2]
MOD_CHUNKS = LAYERS * 9 * KC
MOD_GROUPS = 4
MOD_GROUP = MOD_CHUNKS // MOD_GROUPS

G_FINAL1, G_NORM2, G_FINAL2 = 3 * LAYERS, 3 * LAYERS + 1, 6 * LAYERS + 1
N_GAINS = 6 * LAYERS + 2


class Seen:

    def __init__(self, **start):
        self.n = dict(start)
        self.turns = []

    def __call__(self, name, more=1):
        self.n[name] = self.n.get(name, 0) + more
        return self.value(name)

    def value(self, name, ahead=0):
        v = self.n.get(name, 0) + ahead
        for turn, per in self.turns:
            if per.get(name, 0):
                v = turn * per[name] + v
        return v

    def skip(self, name, more):
        self.n[name] = self.n.get(name, 0) + more


@contextmanager
def loop(eng, seen, count, **per):
    with eng.Fori(0, count) as turn:
        start = dict(seen.n)
        seen.turns.append((turn, per))
        yield turn
        seen.turns.pop()
        for name in set(seen.n) | set(per):
            took = seen.n.get(name, 0) - start.get(name, 0)
            assert took == per.get(name, 0), (name, took, per.get(name, 0))
    for name, k in per.items():
        seen.n[name] = start.get(name, 0) + count * k


def build_program(nc, a, out):
    ctx = ExitStack()
    with ctx:
        def sb(name, shape, dt=F32):
            return ctx.enter_context(nc.sbuf_tensor(name, shape, dt))

        sems = {}

        def sem(name):
            sems[name] = ctx.enter_context(nc.semaphore(name))
            return sems[name]

        slot = [sb(f"slot{i}", [P, SLOT]) for i in range(RING)]
        wd = [sb(f"wd{i}", [P, FC, P]) for i in range(2)]
        mod_raw = [sb(f"mod_raw{i}", [P, KC, P]) for i in range(2)]
        mod_acc = sb("mod_acc", [P, MOD_GROUP, P])
        x = sb("x", [P, KC, S])
        h = sb("h", [P, KC, S])
        sq = sb("sq", [P, 2, 512])
        sqsum = sb("sqsum", [P, S])
        rstd = sb("rstd", [P, 1024])
        warm = sb("warm", [P, 8])
        ident = sb("ident", [P, P])
        ones = sb("ones", [P, S])
        rope_cos = sb("rope_cos", [P, S])
        rope_sin = sb("rope_sin", [P, S])
        mats = sb("mats", [P, 5, P])
        causal = sb("causal", [P, TB, S])
        na_mask = sb("na_mask", [P, ROWS, GRID_W])
        cmp_bias = sb("cmp_bias", [P, TB, 16])
        cmp_keep = sb("cmp_keep", [P, TB, 16])
        gla_mask = sb("gla_mask", [P, 7, P], U32)
        gains = sb("gains", [P, N_GAINS, KC])
        na_gain = sb("na_gain", [P, LAYERS, 4])
        gla_gain = sb("gla_gain", [P, LAYERS])
        w_code = sb("w_code", [P, LAYERS, KC, 64])
        w_gate = sb("w_gate", [64, LAYERS, 256])
        b_gate = sb("b_gate", [P, LAYERS, 4])
        cond = sb("cond", [P, KC])
        mod_b = sb("mod_b", [P, MOD_CHUNKS])
        mod = sb("mod", [P, MOD_CHUNKS])
        mod_gain = sb("mod_gain", [P, LAYERS, 3, KC])
        mod_gate = sb("mod_gate", [P, LAYERS, 3, KC])
        lru_w = sb("lru_w", [P, 2, 4, P])
        lru_p = sb("lru_p", [P, 32])
        lru_c = sb("lru_c", [P, 48])
        cmp_pos = sb("cmp_pos", [P, 2, CMP_PAIRS])
        cmp_w2 = sb("cmp_w2", [P, 2, P])
        ROOM = 22656
        room = sb("room", [P, ROOM])

        def carve(at, *shape):
            n = int(np.prod(shape))
            assert at[0] + n <= ROOM, (at[0], n)
            v = room[:, at[0]:at[0] + n]
            at[0] += n
            if len(shape) == 2:
                v = v.rearrange("p (a b) -> p a b", a=shape[0])
            elif len(shape) == 3:
                v = v.rearrange("p (a b c) -> p a b c", a=shape[0], b=shape[1])
            return v

        at = [0]
        act_t = carve(at, FC, S)
        sil = carve(at, 2, S)
        at = [0]
        mix = carve(at, KC, S)
        proj = carve(at, 12, 512)
        att_t = carve(at, 2, 800)
        att_e = carve(at, 2, 800)
        att_pt = carve(at, 2, 1024)
        mixer_room = at[0]
        at = [mixer_room]
        na_bias = carve(at, NA_HEADS, 512)
        gb = carve(at, 2, 512)
        ge = carve(at, 2, 1024)
        ga = carve(at, GLA_HEADS, 4, P)
        at = [mixer_room]
        xc = carve(at, 4, S)
        lr = carve(at, 4, S)
        li = carve(at, 4, S)
        la = carve(at, 4, S)
        lb = carve(at, 4, S)
        lg = carve(at, 4, S)
        at = [mixer_room]
        k_rope = carve(at, NSA_GROUPS, 512)
        rope_tmp = carve(at, 512)
        cmp_g = carve(at, 2, CMP_PAIRS, 2 * NCMP)
        cmp_h = carve(at, 2, 32)
        k_cmp = carve(at, 32)
        v_cmp = carve(at, 2, DH)
        gates = carve(at, TB, 48)
        q_rope = carve(at, 4, 512)
        stats = sb("stats", [P, 2, 32])
        code = sb("code", [64, S])

        bank = [ctx.enter_context(nc.psum_tensor(f"bank{i}", [P, 512], F32)) for i in range(8)]

        for name in (
            "const_ready", "x_loaded", "bias_ready", "out_stored",
            "slot0_ready", "slot1_ready", "wd0_ready", "wd1_ready", "mod0_ready", "mod1_ready",
            "slot_done", "y_done", "ss_done", "mod_done", "score_done", "pt_done", "pv_done",
            "code_done", "logit_done", "level_done", "gla_o_done", "rot_done", "lru_gate_done",
            "cmp_dup_done", "cmp_done",
            "act_step", "sil_ready", "proj_ready", "sq_ready", "rstd_ready", "cond_ready", "exp_ready",
            "pt_copied", "o_copied", "decay_ready", "code_ready", "logit_read", "forget_ready", "na_sq_ready",
            "gla_sq_ready", "lru_gate_ready", "lru_exp_ready", "lru_decay_ready", "lru_mult_ready",
            "gelu_ready", "hidden_ready", "cmp_ready", "gates_ready",
            "dve_step", "act_ready", "x_ready", "out_added", "sum_step", "h_ready", "score_read",
            "max_ready", "probs_ready", "pt_half_copied", "diff_ready", "qk_ready", "level_read", "mix_ready",
            "rot_read", "conv_ready", "blocks_ready", "lru_sq_ready", "lru_const_ready",
            "mod_step", "bias_masked",
        ):
            sem(name)
        s = sems
        SLOT_READY = ["slot0_ready", "slot1_ready"]
        WD_READY = ["wd0_ready", "wd1_ready"]
        MOD_READY = ["mod0_ready", "mod1_ready"]
        CONST_LOADS = 21
        na_sq = att_t[:, :, :].rearrange("p a b -> p (a b)")[:, 0:1024]
        block = ctx.enter_context(nc.Block())

        @block.sync
        def _(sp):
            seen = Seen()

            def load_slot(n, b):
                sp.dma_start(slot[b][:, :], a["slots"][bass.ds(n, 1), :, :].rearrange("o p n -> (o p) n")
                             ).then_inc(s[SLOT_READY[b]], 16)

            def load_wd(n, b):
                sp.dma_start(wd[b][:, :, :], a["wd"][bass.ds(n, 1), :, :, :].rearrange("o p f n -> (o p) f n")
                             ).then_inc(s[WD_READY[b]], 16)

            sp.dma_start(x[:, :, :], a["x"]).then_inc(s["x_loaded"], 16)
            load_slot(0, 0)
            for dst, name in ((gains[:, :, :], "gains"), (mod_b[:, :], "mod_b"), (ident[:, :], "ident"),
                              (rope_cos[:, :], "rope_cos"), (rope_sin[:, :], "rope_sin"),
                              (mats[:, :, :], "mats"), (causal[:, :, :], "causal"),
                              (na_mask[:, :, :], "na_mask"), (cmp_bias[:, :, :], "cmp_bias"),
                              (cmp_keep[:, :, :], "cmp_keep"), (gla_mask[:, :, :], "gla_mask"),
                              (na_gain[:, :, :], "na_gain"), (gla_gain[:, :], "gla_gain"),
                              (w_code[:, :, :, :], "w_code"), (w_gate[:, :, :], "w_gate"),
                              (b_gate[:, :, :], "b_gate"), (cond[:, :], "cond"),
                              (lru_w[:, :, :, :], "lru_w"), (lru_p[:, :], "lru_p"),
                              (cmp_pos[:, :, :], "cmp_pos"), (cmp_w2[:, :, :], "cmp_w2")):
                sp.dma_start(dst, a[name]).then_inc(s["const_ready"], 16)
            load_slot(1, 1)
            load_wd(0, 0)
            load_wd(1, 1)

            def refill_slots(first, count, last_missing=0):
                turns = (count - last_missing) // RING
                with loop(sp, seen, turns, slot_done=RING) as t:
                    for b in range(RING):
                        sp.wait_ge(s["slot_done"], seen("slot_done"))
                        load_slot(t * RING + (first + RING + b), b)
                return first + count

            def refill_wd(ffn):
                turns = KC // 2 - (ffn == FFNS - 1)
                with loop(sp, seen, turns, y_done=2) as t:
                    for b in range(2):
                        sp.wait_ge(s["y_done"], seen("y_done"))
                        load_wd(t * 2 + (ffn * KC + 2 + b), b)

            def load_bias(layer):
                for head in range(NA_HEADS):
                    for r in range(ROWS):
                        src = a["rpb"][layer, head, ROWS - 1 - r:2 * ROWS - 1 - r, :, :].rearrange("k q c -> q k c")
                        dst = na_bias[GRID_W * (r % 2):GRID_W * (r % 2) + GRID_W, head,
                                      (r // 2) * S:(r // 2) * S + S].rearrange("p (k c) -> p k c", k=ROWS)
                        sp.dma_start(dst, src).then_inc(s["bias_ready"], 16)

            n = 0
            ffn = 0
            for stack in range(2):
                for layer in range(LAYERS):
                    if stack == 0:
                        load_bias(layer)
                    n = refill_slots(n, FC)
                    refill_wd(ffn)
                    ffn += 1
                    mixer = M1_SLOTS if stack == 0 else M2_SLOTS if layer == 0 else M3_SLOTS
                    n = refill_slots(n, mixer + OUT_SLOTS)
                    n = refill_slots(n, FC, RING if ffn == FFNS - 1 else 0)
                    refill_wd(ffn)
                    ffn += 1
            assert n == TOTAL_SLOTS and ffn == FFNS
            sp.wait_ge(s["h_ready"], KC * N_GAINS)
            sp.dma_start(out, h[:, :, :]).then_inc(s["out_stored"], 16)
            sp.wait_ge(s["out_stored"], 16)

        @block.gpsimd
        def _(pool):
            seen = Seen()

            def link(ins):
                ins.then_inc(s["mod_step"], 1)
                pool.wait_ge(s["mod_step"], seen("mod_step"))

            def load_mod(n, b):
                pool.dma_start(mod_raw[b][:, :, :], a["mod_w"][bass.ds(n, 1), :, :, :].rearrange("o p k n -> (o p) k n")
                               ).then_inc(s[MOD_READY[b]], 16)

            def mod_chunk(c, b):
                w = mod_raw[b]
                pool.wait_ge(s[MOD_READY[b]], seen(MOD_READY[b], 16))
                link(pool.tensor_tensor(w[:, :, :], w[:, :, :], cond[:, :].unsqueeze(2).to_broadcast([P, KC, P]), ALU.mult))
                link(pool.tensor_tensor(w[:, 0:4, :], w[:, 0:4, :], w[:, 4:8, :], ALU.add))
                link(pool.tensor_tensor(w[:, 0:2, :], w[:, 0:2, :], w[:, 2:4, :], ALU.add))
                link(pool.tensor_tensor(mod_acc[:, bass.ds(c, 1), :], w[:, 0:1, :], w[:, 1:2, :], ALU.add))

            load_mod(0, 0)
            load_mod(1, 1)
            pool.wait_ge(s["const_ready"], 16 * CONST_LOADS)
            pool.wait_ge(s["cond_ready"], seen("cond_ready"))
            for g in range(MOD_GROUPS):
                if g:
                    pool.wait_ge(s["mod_done"], seen("mod_done"))
                tail = int(g == MOD_GROUPS - 1)
                with loop(pool, seen, MOD_GROUP // 2 - tail, mod0_ready=16, mod1_ready=16, mod_step=8) as t:
                    for b in range(2):
                        mod_chunk(t * 2 + b, b)
                        load_mod(t * 2 + (g * MOD_GROUP + 2 + b), b)
                if tail:
                    mod_chunk(MOD_GROUP - 2, 0)
                    mod_chunk(MOD_GROUP - 1, 1)
                if g % 2 == 0:
                    pool.wait_ge(s["bias_ready"], seen("bias_ready", 16 * NA_HEADS * ROWS))
                    for head in range(NA_HEADS):
                        for qt in range(TB):
                            v = na_bias[:, head, qt * S:qt * S + S]
                            pool.tensor_tensor(v, v, na_mask[:, :, :].rearrange("p a b -> p (a b)"),
                                               ALU.add).then_inc(s["bias_masked"], 1)

        @block.tensor
        def _(pe):
            seen = Seen(sum_step=2)

            def slot_products(b, rhs, target):
                pe.wait_ge(s[SLOT_READY[b]], seen(SLOT_READY[b], 16))
                for u in range(2):
                    for k in range(KC):
                        w = (u * KC + k) * P
                        last = pe.matmul(target[:, u * S:u * S + S], slot[b][:, w:w + P], rhs[:, k, :],
                                         start=(k == 0), stop=(k == KC - 1))
                last.then_inc(s["slot_done"], 1)

            def slot_products_by_token(b, target, units=2, cols=P):
                pe.wait_ge(s[SLOT_READY[b]], seen(SLOT_READY[b], 16))
                w = slot[b][:, :].rearrange("p (u k n) -> p u k n", u=2, k=KC)
                for tb in range(TB):
                    o = target[:, tb * S:tb * S + units * cols]
                    if units == 2:
                        o = o.rearrange("p (u n) -> p u n", u=2)
                    for k in range(KC):
                        rhs = w[:, :, k, 0:cols] if units == 2 else w[:, 0, k, 0:cols]
                        last = pe.matmul(o, h[:, k, tb * P:tb * P + P], rhs, start=(k == 0), stop=(k == KC - 1))
                last.then_inc(s["slot_done"], 1)

            def norm_sum(batches):
                pe.wait_ge(s["sum_step"], seen("sum_step", batches))
                pe.matmul(bank[4][:, 0:S], ones[:, 0:P], sqsum[:, :], start=True, stop=True).then_inc(s["ss_done"], 1)

            def ffn(group):
                pe.wait_ge(s["h_ready"], seen("h_ready", KC))
                with loop(pe, seen, FC // 2, slot0_ready=16, slot1_ready=16, act_ready=2):
                    for b in range(RING):
                        pe.wait_ge(s["act_ready"], seen("act_ready"))
                        slot_products(b, h, bank[b])
                if group is not None:
                    pe.wait_ge(s["mod_step"], seen("mod_step", 4 * MOD_GROUP))
                    for c in range(MOD_GROUP):
                        last = pe.matmul(bank[5][:, c:c + 1], mod_acc[:, c, :], ones[:, 0:1], start=True, stop=True)
                    last.then_inc(s["mod_done"], 1)
                pe.wait_ge(s["act_ready"], seen.value("act_ready", 2))
                with loop(pe, seen, KC // 2, wd0_ready=16, wd1_ready=16, x_ready=2):
                    for b in range(2):
                        pe.wait_ge(s[WD_READY[b]], seen(WD_READY[b], 16))
                        pe.wait_ge(s["x_ready"], seen("x_ready"))
                        for f in range(FC):
                            last = pe.matmul(bank[2 + b][:, 0:S], wd[b][:, f, :], act_t[:, f, :],
                                             start=(f == 0), stop=(f == FC - 1))
                        last.then_inc(s["y_done"], 1)
                norm_sum(KC)

            def projection(kinds):
                for n, kind in enumerate(kinds):
                    pe.wait_ge(s["proj_ready"], seen("proj_ready"))
                    if kind == "f":
                        slot_products(n % 2, h, bank[n % 2])
                    elif kind == "t":
                        slot_products_by_token(n % 2, bank[n % 2])
                    else:
                        slot_products_by_token(n % 2, bank[n % 2], units=1, cols=48)

            def out_projection():
                for n in range(OUT_SLOTS):
                    pe.wait_ge(s["out_added"], seen("out_added"))
                    slot_products(n % 2, mix, bank[2 + n % 2])
                norm_sum(OUT_SLOTS)

            def attention(q, k, v, heads):
                def scores(i):
                    if i >= 2:
                        pe.wait_ge(s["score_read"], seen("score_read"))
                    p0 = DH * (i % 2)
                    for qt in range(TB):
                        last = pe.matmul(bank[2 + i % 2][:, qt * S:qt * S + S], q(i)[p0:p0 + DH, qt * P:qt * P + P],
                                         k(i)[p0:p0 + DH, :], start=True, stop=True)
                    last.then_inc(s["score_done"], 1)

                def transposes(i):
                    pe.wait_ge(s["probs_ready"], seen("probs_ready"))
                    for kb in range(TB):
                        for qt in range(TB):
                            last = pe.transpose(bank[4 + i % 2][:, kb * S + qt * P:kb * S + qt * P + P],
                                                att_e[:, i % 2, qt * S + kb * P:qt * S + kb * P + P], ident[:, :])
                    last.then_inc(s["pt_done"], 1)

                def values(i):
                    pe.wait_ge(s["pt_copied"], seen("pt_copied"))
                    if i >= 4 and i % 2 == 0:
                        pe.wait_ge(s["o_copied"], seen("o_copied"))
                    p0 = DH * (i % 2)
                    for kb in range(TB):
                        last = pe.matmul(bank[6 + i // 2 % 2][p0:p0 + DH, 0:S], v(i, kb),
                                         att_pt[:, i % 2, kb * S:kb * S + S], start=(kb == 0), stop=(kb == TB - 1))
                    last.then_inc(s["pv_done"], 1)

                for i in range(heads + 2):
                    if i < heads:
                        scores(i)
                    if i >= 2:
                        values(i - 2)
                    if 1 <= i <= heads:
                        transposes(i - 1)
                seen.skip("score_read", 2)
                seen.skip("o_copied", 2)

            def mixer1(layer):
                pe.wait_ge(s["h_ready"], seen("h_ready", KC))
                projection("ffff" "tt" "ffff" "tt")
                for k in range(KC):
                    last = pe.matmul(bank[4][0:64, 0:S], w_code[:, layer, k, :], h[:, k, :],
                                     start=(k == 0), stop=(k == KC - 1))
                last.then_inc(s["code_done"], 1)
                pe.wait_ge(s["code_ready"], seen("code_ready"))
                for way in range(2):
                    for pair in range(2):
                        last = pe.matmul(bank[6 + way][:, pair * S:pair * S + S],
                                         w_gate[32 * way:32 * way + GLA_RANK, layer, pair * P:pair * P + P],
                                         code[32 * way:32 * way + GLA_RANK, :], start=True, stop=True)
                last.then_inc(s["logit_done"], 1)
                pe.wait_ge(s["proj_ready"], seen.value("proj_ready", 2))
                pe.wait_ge(s["logit_read"], seen("logit_read"))
                attention(lambda i: proj[:, i // 4, (i // 2 % 2) * S:(i // 2 % 2) * S + S],
                          lambda i: proj[:, 2 + i // 4, (i // 2 % 2) * S:(i // 2 % 2) * S + S],
                          lambda i, kb: proj[:, 4 + i // 4, kb * S + (i % 4) * DH:kb * S + (i % 4) * DH + DH],
                          NA_HEADS)
                pe.wait_ge(s["na_sq_ready"], seen("na_sq_ready"))
                for c in range(4):
                    last = pe.matmul(bank[4][:, 0:S], ones[:, 0:P], na_sq[:, c * S:c * S + S], start=(c == 0), stop=(c == 3))
                last.then_inc(s["ss_done"], 1)
                for i, n in enumerate(GLA_LEVELS + [1]):
                    if n > 1:
                        pe.wait_ge(s["qk_ready"], seen("qk_ready"))
                    if i >= 2:
                        pe.wait_ge(s["level_read"], seen("level_read"))
                    qk = ge[:, i % 2, :] if n > 1 else proj[:, 6:8, :].rearrange("p a b -> p (a b)")
                    for sblk in range(TB):
                        tblk = 1 - sblk if n == S else sblk
                        for head in range(GLA_HEADS):
                            p0, c = DH * (head % 2), (head // 2) * S
                            o = (head // 2 * TB + sblk) * P
                            last = pe.matmul(bank[(0, 2)[i % 2] + head % 2][:, o:o + P],
                                             qk[p0:p0 + DH, 512 + c + sblk * P:512 + c + sblk * P + P],
                                             qk[p0:p0 + DH, c + tblk * P:c + tblk * P + P], start=True, stop=True)
                    last.then_inc(s["level_done"], 1)
                pe.wait_ge(s["level_read"], seen("level_read", 2))
                for head in range(GLA_HEADS):
                    for sblk in range(TB):
                        v0 = sblk * S + (head % 2) * P
                        last = pe.matmul(bank[6 + head // 2][:, (head % 2) * S:(head % 2) * S + S],
                                         proj[:, 10 + head // 2, v0:v0 + P], ga[:, head, 2 * sblk:2 * sblk + 2, :].rearrange("p a b -> p (a b)"),
                                         start=(sblk == 0), stop=(sblk == TB - 1))
                last.then_inc(s["gla_o_done"], 1)
                for half in range(2):
                    pe.wait_ge(s["gla_sq_ready"], seen("gla_sq_ready"))
                    pe.matmul(bank[half][:, :], ones[:, 0:P], sq[:, half, :], start=True, stop=True).then_inc(s["ss_done"], 1)
                pe.wait_ge(s["mix_ready"], seen("mix_ready", 2))
                out_projection()

            def mixer2():
                pe.wait_ge(s["h_ready"], seen("h_ready", KC))
                projection("ffff" "tt" "ffff")
                pe.wait_ge(s["proj_ready"], seen.value("proj_ready", 2))
                for i in range(4):
                    if i >= 2:
                        pe.wait_ge(s["rot_read"], seen("rot_read"))
                    pe.matmul(bank[4 + i % 2][:, :], mats[:, 0, :], proj[:, i, :], start=True, stop=True
                              ).then_inc(s["rot_done"], 1)
                pe.wait_ge(s["rot_read"], seen("rot_read", 2))
                pe.wait_ge(s["conv_ready"], seen("conv_ready"))
                for c in range(4):
                    if c >= 2:
                        pe.wait_ge(s["lru_gate_ready"], seen("lru_gate_ready"))
                    for gate in range(2):
                        last = pe.matmul(bank[6 + c % 2][:, gate * S:gate * S + S], lru_w[:, gate, c, :],
                                         xc[:, c, :], start=True, stop=True)
                    last.then_inc(s["lru_gate_done"], 1)
                pe.wait_ge(s["lru_gate_ready"], seen("lru_gate_ready", 2))
                attention(lambda i: proj[:, i // 4, (i // 2 % 2) * S:(i // 2 % 2) * S + S],
                          lambda i: proj[:, 2 + i // 4, (i // 2 % 2) * S:(i // 2 % 2) * S + S],
                          lambda i, kb: proj[:, 4 + i // 4, kb * S + (i % 4) * DH:kb * S + (i % 4) * DH + DH],
                          NA_HEADS)
                pe.wait_ge(s["o_copied"], seen.value("o_copied"))
                pe.wait_ge(s["mix_ready"], seen("mix_ready"))
                out_projection()

            def mixer3():
                pe.wait_ge(s["h_ready"], seen("h_ready", KC))
                projection("ffff" "f" "t" "f" "g")
                pe.wait_ge(s["proj_ready"], seen.value("proj_ready", 2))
                for i in range(4):
                    if i >= 2:
                        pe.wait_ge(s["rot_read"], seen("rot_read"))
                    pe.matmul(bank[4 + i % 2][:, :], mats[:, 0, :], proj[:, i, :], start=True, stop=True
                              ).then_inc(s["rot_done"], 1)
                pe.wait_ge(s["rot_read"], seen("rot_read", 2))
                for g in range(NSA_GROUPS):
                    pe.matmul(bank[4 + 2 * g][:, :], mats[:, 1 + g, :], proj[:, 4, :], start=True, stop=True)
                    pe.matmul(bank[5 + 2 * g][:, :], mats[:, 3 + g, :], proj[:, 4, :], start=True, stop=True
                              ).then_inc(s["rot_done"], 1)
                for g in range(NSA_GROUPS):
                    pe.matmul(bank[2 + g][:, :], mats[:, 1 + g, :], proj[:, 6, :], start=True, stop=True
                              ).then_inc(s["cmp_dup_done"], 1)
                for kv in range(2):
                    b = kv
                    pe.wait_ge(s[SLOT_READY[b]], seen(SLOT_READY[b], 16))
                    if kv == 0:
                        pe.wait_ge(s["blocks_ready"], seen("blocks_ready"))
                    for c in range(CMP_PAIRS):
                        last = pe.matmul(bank[kv][:, 0:2 * NCMP], slot[b][:, c * P:c * P + P], cmp_g[:, kv, c, :],
                                         start=(c == 0), stop=(c == CMP_PAIRS - 1))
                    last.then_inc(s["slot_done"], 1)
                pe.wait_ge(s["hidden_ready"], seen("hidden_ready"))
                pe.matmul(bank[4][:, 0:2 * NCMP], cmp_w2[:, 0, :], cmp_h[:, 0, 0:2 * NCMP], start=True, stop=True)
                for g in range(NSA_GROUPS):
                    last = pe.matmul(bank[5][0:NCMP, g * DH:g * DH + DH], cmp_h[:, 1, g * NCMP:g * NCMP + NCMP],
                                     cmp_w2[:, 1, 0:DH], start=True, stop=True)
                last.then_inc(s["cmp_done"], 1)
                pe.wait_ge(s["cmp_ready"], seen("cmp_ready"))
                heads = NSA_HEADS

                def scores(i):
                    if i >= 2:
                        pe.wait_ge(s["score_read"], seen("score_read"))
                    p0, g = DH * (i % 2), i // (NSA_HEADS // NSA_GROUPS)
                    c0 = (i // 2 % 2) * S
                    q = q_rope[p0:p0 + DH, i // 4, c0:c0 + S]
                    qn = proj[p0:p0 + DH, i // 4, c0:c0 + S]
                    kk = k_rope[p0:p0 + DH, g, :].rearrange("p (b t) -> p b t", b=2)
                    big, small = bank[i % 2], bank[2 + i % 2]
                    pe.matmul(big[:, :], q[:, P:S], kk[:, :, :], start=True, stop=True)
                    pe.matmul(small[:, 0:S].rearrange("p (b t) -> p b t", b=2), q[:, 0:P], kk[:, :, 0:P], start=True, stop=True)
                    for qt in range(TB):
                        last = pe.matmul(small[:, S + 16 * qt:S + 16 * qt + NCMP], qn[:, qt * P:qt * P + P],
                                         k_cmp[p0:p0 + DH, g * NCMP:g * NCMP + NCMP], start=True, stop=True)
                    last.then_inc(s["score_done"], 1)

                def transposes(i):
                    pe.wait_ge(s["probs_ready"], seen("probs_ready"))
                    e = att_e[:, i % 2, :]
                    X, Y = bank[4], bank[5]
                    for br in range(2):
                        pe.transpose(X[:, br * S:br * S + P], e[:, 16 + br * P:16 + br * P + P], ident[:, :])
                        q1 = 16 + S + 16 + br * S
                        pe.transpose(X[:, br * S + P:br * S + S], e[:, q1:q1 + P], ident[:, :])
                        pe.transpose(Y[:, br * P:br * P + P], e[:, q1 + P:q1 + S], ident[:, :])
                    for qt in range(TB):
                        c0 = qt * (16 + S)
                        last = pe.transpose(Y[0:NCMP, S + qt * P:S + qt * P + P], e[:, c0:c0 + NCMP], ident[:, :])
                    last.then_inc(s["pt_done"], 1)

                def values(i):
                    pe.wait_ge(s["pt_copied"], seen("pt_copied"))
                    pe.wait_ge(s["pt_half_copied"], seen("pt_half_copied"))
                    if i >= 4 and i % 2 == 0:
                        pe.wait_ge(s["o_copied"], seen("o_copied"))
                    p0, g = DH * (i % 2), i // (NSA_HEADS // NSA_GROUPS)
                    o = bank[6 + i // 2 % 2][p0:p0 + DH, 0:S]
                    pt = att_pt[:, i % 2, :]

                    def v(br, kb):
                        return proj[:, 5, kb * S + br * P + g * DH:kb * S + br * P + g * DH + DH]

                    pe.matmul(o, v(0, 0), pt[:, 0:S], start=True, stop=False)
                    pe.matmul(o[:, P:S], v(0, 1), pt[:, 512:640], start=False, stop=False, skip_group_check=True)
                    pe.matmul(o[:, P:S], v(1, 1), pt[:, 640:768], start=False, stop=False, skip_group_check=True)
                    pe.matmul(o, v_cmp[0:NCMP, g, :], pt[0:NCMP, 768:1024], start=False, stop=False, skip_group_check=True)
                    pe.matmul(o, v(1, 0), pt[:, S:2 * S], start=False, stop=True).then_inc(s["pv_done"], 1)

                for i in range(heads + 2):
                    if i < heads:
                        scores(i)
                    if i >= 2:
                        values(i - 2)
                    if 1 <= i <= heads:
                        transposes(i - 1)
                seen.skip("score_read", 2)
                seen.skip("o_copied", 2)
                pe.wait_ge(s["o_copied"], seen.value("o_copied"))
                out_projection()

            pe.wait_ge(s["const_ready"], 16 * CONST_LOADS)
            norm_sum(OUT_SLOTS)
            for stack in range(2):
                for layer in range(LAYERS):
                    ffn(2 * layer if stack == 0 else None)
                    if stack == 0:
                        mixer1(layer)
                    elif layer == 0:
                        mixer2()
                    else:
                        mixer3()
                    ffn(2 * layer + 1 if stack == 0 else None)
                if stack == 0:
                    seen.skip("h_ready", KC)
                    norm_sum(OUT_SLOTS)

        @block.scalar
        def _(act):
            seen = Seen(x_ready=2, out_added=2)

            def link(ins):
                ins.then_inc(s["act_step"], 1)
                act.wait_ge(s["act_step"], seen("act_step"))

            def rstd_of(target, sums, width):
                act.wait_ge(s["ss_done"], seen("ss_done"))
                link(act.activation(target, sums, ACT.Ln, bias=EPS, scale=1.0 / width))
                act.activation(target, target, ACT.Exp, scale=-0.5).then_inc(s["rstd_ready"], 1)

            def squares_of_slots(ready):
                for n in range(OUT_SLOTS):
                    act.wait_ge(s[ready[0]], seen(ready[0], ready[1]))
                    act.wait_ge(s["sum_step"], seen("sum_step"))
                    act.activation(sq[:, n % 2, :], x[:, 2 * n:2 * n + 2, :].rearrange("p a b -> p (a b)"),
                                   ACT.Square).then_inc(s["sq_ready"], 1)

            def norm():
                rstd_of(rstd[:, 0:S], bank[4][:, 0:S], D)

            def ffn():
                norm()
                with loop(act, seen, FC // 2, slot_done=2, act_ready=2):
                    for b in range(2):
                        act.wait_ge(s["slot_done"], seen("slot_done"))
                        act.wait_ge(s["act_ready"], seen("act_ready"))
                        act.activation(sil[:, b, :], bank[b][:, 0:S], ACT.Silu).then_inc(s["sil_ready"], 1)
                link(act.activation(warm[:, 4:5], ones[:, 0:1], ACT.Ln))
                with loop(act, seen, KC // 2, x_ready=2, sum_step=2) as t:
                    for b in range(2):
                        act.wait_ge(s["x_ready"], seen("x_ready"))
                        act.wait_ge(s["sum_step"], seen("sum_step"))
                        act.activation(sq[:, b, 0:S], x[:, bass.ds(t * 2 + b, 1), :].rearrange("p a b -> p (a b)"),
                                       ACT.Square).then_inc(s["sq_ready"], 1)

            def projection(kinds, scaled=(), swish=()):
                for n, kind in enumerate(kinds):
                    act.wait_ge(s["slot_done"], seen("slot_done"))
                    if kind == "g":
                        last = act.activation(gates[:, :, :], bank[n % 2][:, :].rearrange("p (b n) -> p b n", b=TB)[:, :, 0:48],
                                              ACT.Sigmoid)
                    elif n in swish:
                        last = act.activation(proj[:, n, :], bank[n % 2][:, :], ACT.Silu)
                    else:
                        last = act.activation(proj[:, n, :], bank[n % 2][:, :], ACT.Copy, scale=SCALE if n in scaled else 1.0)
                    last.then_inc(s["proj_ready"], 1)

            def out_projection():
                seen.skip("slot_done", OUT_SLOTS)
                squares_of_slots(("out_added", 1))

            def attention(heads, first_chunk, segments, copies):
                def exps(i):
                    act.wait_ge(s["max_ready"], seen("max_ready"))
                    for j, (c, n) in enumerate(segments):
                        k = len(segments)
                        last = act.activation(att_e[:, i % 2, c:c + n], att_t[:, i % 2, c:c + n], ACT.Exp,
                                              bias=stats[:, i % 2, k + j:k + j + 1],
                                              accum_out=stats[:, i % 2, 2 * k + j:2 * k + j + 1])
                    last.then_inc(s["exp_ready"], 1)

                def copy(i):
                    act.wait_ge(s["pt_done"], seen("pt_done"))
                    if i >= 2:
                        act.wait_ge(s["pv_done"], seen("pv_done"))
                    for dst, src in copies(i):
                        last = act.activation(dst, src, ACT.Copy)
                    last.then_inc(s["pt_copied"], 1)

                def copy_output(i):
                    act.wait_ge(s["pv_done"], seen.value("pv_done", 1 if i < heads - 1 else 2))
                    act.activation(mix[:, first_chunk + i // 2, :], bank[6 + i // 2 % 2][:, 0:S],
                                   ACT.Copy).then_inc(s["o_copied"], 1)

                for i in range(heads + 2):
                    if i < heads:
                        exps(i)
                    if 1 <= i <= heads:
                        copy(i - 1)
                    if i >= 2 and i % 2 == 1:
                        copy_output(i - 2)
                seen.skip("pv_done", 2)

            def plain_attention(first_chunk):
                attention(NA_HEADS, first_chunk, [(0, S), (S, S)],
                          lambda i: [(att_pt[:, i % 2, 0:512], bank[4 + i % 2][:, :])])

            def mixer1(layer):
                norm()
                projection("ffff" "tt" "ffff" "tt", scaled=(6,), swish=(8, 9))
                act.wait_ge(s["code_done"], seen("code_done"))
                act.activation(code[:, :], bank[4][0:64, 0:S], ACT.Copy).then_inc(s["code_ready"], 1)
                act.wait_ge(s["logit_done"], seen("logit_done"))
                z, e = ge[:, 0, :], ge[:, 1, :]
                for way in range(2):
                    for pair in range(2):
                        c = (way * 2 + pair) * S
                        last = act.activation(z[:, c:c + S], bank[6 + way][:, pair * S:pair * S + S], ACT.Identity,
                                              bias=b_gate[:, layer, way * 2 + pair:way * 2 + pair + 1])
                last.then_inc(s["logit_read"], 1)
                act.wait_ge(s["logit_read"], seen("logit_read"))
                link(act.activation(e, z, ACT.Abs))
                link(act.activation(e, e, ACT.Exp, scale=-1.0))
                act.activation(e, e, ACT.Ln, bias=1.0).then_inc(s["forget_ready"], 1)
                plain_attention(0)
                act.wait_ge(s["o_copied"], seen("o_copied", NA_HEADS // 2))
                act.activation(na_sq, mix[:, 0:4, :].rearrange("p a b -> p (a b)"), ACT.Square).then_inc(s["na_sq_ready"], 1)
                rstd_of(rstd[:, 0:S], bank[4][:, 0:S], NA_HEADS * DH)
                for i in range(len(GLA_LEVELS)):
                    act.wait_ge(s["diff_ready"], seen("diff_ready"))
                    act.activation(ge[:, i % 2, :], ge[:, i % 2, :], ACT.Exp, scale=1.0 / GLA_TAU).then_inc(s["decay_ready"], 1)
                act.wait_ge(s["gla_o_done"], seen("gla_o_done"))
                for half in range(2):
                    act.activation(sq[:, half, :], bank[6 + half][:, :], ACT.Square).then_inc(s["gla_sq_ready"], 1)
                for half in range(2):
                    rstd_of(rstd[:, half * 512:half * 512 + 512], bank[half][:, :], P)
                out_projection()

            def mixer2():
                norm()
                projection("ffff" "tt" "ffff")
                for c in range(4):
                    act.wait_ge(s["lru_gate_done"], seen("lru_gate_done"))
                    act.activation(lr[:, c, :], bank[6 + c % 2][:, 0:S], ACT.Sigmoid, bias=lru_p[:, 20 + c:21 + c])
                    act.activation(li[:, c, :], bank[6 + c % 2][:, S:2 * S], ACT.Sigmoid, bias=lru_p[:, 24 + c:25 + c]
                                   ).then_inc(s["lru_gate_ready"], 1)
                act.wait_ge(s["lru_const_ready"], seen("lru_const_ready"))
                act.wait_ge(s["lru_gate_ready"], seen("lru_gate_ready", 4))
                for c in range(4):
                    act.activation(la[:, c, :], lr[:, c, :], ACT.Exp, scale=lru_c[:, 4 + c:5 + c])
                    last = act.activation(lb[:, c, :], lr[:, c, :], ACT.Tanh, scale=lru_c[:, c:c + 1])
                last.then_inc(s["lru_decay_ready"], 1)
                act.wait_ge(s["lru_sq_ready"], seen("lru_sq_ready"))
                lbf = lb[:, :, :].rearrange("p a b -> p (a b)")
                act.activation(lbf, lbf, ACT.Sqrt).then_inc(s["lru_mult_ready"], 1)
                act.wait_ge(s["proj_ready"], 2 + LAYERS * M1_SLOTS + M2_SLOTS)
                act.activation(proj[:, 8:10, :], proj[:, 8:10, :], ACT.Gelu_apprx_tanh).then_inc(s["gelu_ready"], 1)
                plain_attention(4)
                seen.skip("o_copied", 4)
                out_projection()

            def mixer3():
                norm()
                projection("ffff" "f" "t" "f" "g")
                for kv in range(2):
                    act.wait_ge(s["slot_done"], seen("slot_done"))
                    last = act.activation(cmp_h[:, kv, 0:2 * NCMP], bank[kv][:, 0:2 * NCMP], ACT.Gelu_apprx_tanh)
                last.then_inc(s["hidden_ready"], 1)
                act.wait_ge(s["cmp_done"], seen("cmp_done"))
                act.activation(k_cmp[:, 0:2 * NCMP], bank[4][:, 0:2 * NCMP], ACT.Copy)
                act.activation(v_cmp[0:NCMP, :, :].rearrange("p a b -> p (a b)"), bank[5][0:NCMP, 0:P], ACT.Copy
                               ).then_inc(s["cmp_ready"], 1)
                segments = [(0, NCMP), (16, P), (16 + P, P), (S + 16, NCMP), (S + 32, S), (2 * S + 32, S)]
                attention(NSA_HEADS, 0, segments,
                          lambda i: [(att_pt[:, i % 2, 0:512], bank[4][:, :])])
                seen.skip("o_copied", 8)
                out_projection()

            act.wait_ge(s["const_ready"], 16 * CONST_LOADS)
            act.activation(cond[:, :], cond[:, :], ACT.Silu).then_inc(s["cond_ready"], 1)
            act.wait_ge(s["lru_const_ready"], seen("lru_const_ready"))
            act.activation(lru_c[:, 8:12], lru_c[:, 4:8], ACT.Exp, scale=-1.0).then_inc(s["lru_exp_ready"], 1)
            squares_of_slots(("x_loaded", 0))
            for stack in range(2):
                for layer in range(LAYERS):
                    ffn()
                    if stack == 0:
                        mixer1(layer)
                    elif layer == 0:
                        mixer2()
                    else:
                        mixer3()
                    ffn()
                norm()
                if stack == 0:
                    act.wait_ge(s["h_ready"], KC * (3 * LAYERS + 1))
                    squares_of_slots(("h_ready", 0))

        @block.vector
        def _(dve):
            seen = Seen(sum_step=1, proj_ready=2)

            def link(ins):
                ins.then_inc(s["dve_step"], 1)
                dve.wait_ge(s["dve_step"], seen("dve_step"))

            def add_squares(halves, n):
                dve.wait_ge(s["sq_ready"], seen("sq_ready"))
                dve.wait_ge(s["sum_step"], seen("sum_step"))
                for j in range(halves):
                    ins = dve.tensor_tensor(sqsum[:, :], sqsum[:, :], sq[:, n % 2, j * S:j * S + S], ALU.add)
                    if j < halves - 1:
                        link(ins)
                ins.then_inc(s["sum_step"], 1)

            def clear_sum():
                link(dve.memset(sqsum[:, :], 0.0))

            def sum_slots():
                clear_sum()
                for n in range(OUT_SLOTS):
                    add_squares(2, n)

            def norm(dst, gain, shift=None):
                dve.wait_ge(s["rstd_ready"], seen("rstd_ready"))
                for k in range(KC):
                    ins = dve.scalar_tensor_tensor(out=dst[:, k, :], in0=x[:, k, :], scalar=gain(k),
                                                   in1=rstd[:, 0:S], op0=ALU.mult, op1=ALU.mult)
                    if shift is None:
                        ins.then_inc(s["h_ready"], 1)
                if shift is not None:
                    link(ins)
                    for k in range(KC):
                        dve.tensor_scalar(dst[:, k, :], dst[:, k, :], shift(k), None, ALU.add).then_inc(s["h_ready"], 1)

            def norm_of(stack, layer, i):
                if stack == 0:
                    norm(h, lambda k: gains[:, 3 * layer + i, k:k + 1])
                else:
                    c = (layer * 9 + 3 * i) * KC
                    norm(h, lambda k: mod_gain[:, layer, i, k:k + 1], lambda k: mod[:, c + k:c + k + 1])

            def ffn(stack, layer, i, group):
                norm_of(stack, layer, i)
                seen.skip("slot_done", FC)
                with loop(dve, seen, FC // 2, sil_ready=2) as t:
                    for b in range(2):
                        dve.wait_ge(s["sil_ready"], seen("sil_ready"))
                        dve.tensor_tensor(act_t[:, bass.ds(t * 2 + b, 1), :].rearrange("p a b -> p (a b)"),
                                          sil[:, b, :], bank[b][:, S:2 * S], ALU.mult).then_inc(s["act_ready"], 1)
                if group is not None:
                    c = group * MOD_GROUP
                    dve.wait_ge(s["mod_done"], seen("mod_done"))
                    link(dve.tensor_tensor(mod[:, c:c + MOD_GROUP], bank[5][:, 0:MOD_GROUP], mod_b[:, c:c + MOD_GROUP], ALU.add))
                clear_sum()
                with loop(dve, seen, KC // 2, y_done=2, sq_ready=2, sum_step=2, x_ready=2) as t:
                    for b in range(2):
                        j = t * 2 + b
                        xj = x[:, bass.ds(j, 1), :].rearrange("p a b -> p (a b)")
                        half = 0.5 if stack == 0 else mod_gate[:, layer, i, bass.ds(j, 1)]
                        dve.wait_ge(s["y_done"], seen("y_done"))
                        dve.scalar_tensor_tensor(out=xj, in0=bank[2 + b][:, 0:S], scalar=half, in1=xj,
                                                 op0=ALU.mult, op1=ALU.add).then_inc(s["x_ready"], 1)
                        seen("x_ready")
                        add_squares(1, b)

            def take_projection(slots):
                dve.wait_ge(s["proj_ready"], seen("proj_ready", slots))

            def out_projection(stack, layer):
                clear_sum()
                for n in range(OUT_SLOTS):
                    dve.wait_ge(s["slot_done"], seen("slot_done"))
                    for j in range(2):
                        k = 2 * n + j
                        y = bank[2 + n % 2][:, j * S:j * S + S]
                        if stack == 0:
                            ins = dve.tensor_tensor(x[:, k, :], y, x[:, k, :], ALU.add)
                        else:
                            ins = dve.scalar_tensor_tensor(out=x[:, k, :], in0=y, scalar=mod_gate[:, layer, 1, k:k + 1],
                                                           in1=x[:, k, :], op0=ALU.mult, op1=ALU.add)
                    ins.then_inc(s["out_added"], 1)
                    add_squares(2, n)

            def attention(bias):
                def scores(i):
                    b = i % 2
                    dve.wait_ge(s["score_done"], seen("score_done"))
                    dve.scalar_tensor_tensor(out=att_t[:, b, 0:512], in0=bank[2 + b][:, :], scalar=SCALE,
                                             in1=bias(i), op0=ALU.mult, op1=ALU.add).then_inc(s["score_read"], 1)
                    dve.wait_ge(s["score_read"], seen("score_read"))
                    link(dve.tensor_reduce(out=stats[:, b, 0:2], in_=att_t[:, b, 0:512].rearrange("p (a b) -> p a b", a=2),
                                           axis=AXX, op=ALU.max))
                    dve.tensor_scalar(stats[:, b, 2:4], stats[:, b, 0:2], -1.0, None, ALU.mult).then_inc(s["max_ready"], 1)

                def scale(i):
                    b = i % 2
                    dve.wait_ge(s["exp_ready"], seen("exp_ready"))
                    link(dve.reciprocal(stats[:, b, 6:8], stats[:, b, 4:6]))
                    for qt in range(TB):
                        e = att_e[:, b, qt * S:qt * S + S]
                        last = dve.tensor_scalar(e, e, stats[:, b, 6 + qt:7 + qt], None, ALU.mult)
                    last.then_inc(s["probs_ready"], 1)

                for i in range(NA_HEADS + 1):
                    if i < NA_HEADS:
                        scores(i)
                    if i:
                        scale(i - 1)
                seen.skip("pt_done", NA_HEADS)
                seen.skip("pv_done", NA_HEADS)

            def level_halves(way, n, pick):
                return way.rearrange("p (b two t) -> p b two t", two=2, t=n // 2)[:, :, pick, :]

            def mixer1(layer):
                norm_of(0, layer, 1)
                seen.skip("slot_done", M1_SLOTS)
                take_projection(M1_SLOTS)
                dve.wait_ge(s["bias_masked"], seen("bias_masked", NA_HEADS * TB))
                dve.wait_ge(s["forget_ready"], seen("forget_ready"))
                link(dve.scalar_tensor_tensor(out=ge[:, 0, :], in0=ge[:, 0, :], scalar=0.0, in1=ge[:, 1, :],
                                              op0=ALU.min, op1=ALU.subtract))
                for pair in range(2):
                    c, back = pair * S, 512 + pair * S
                    dve.tensor_tensor_scan(gb[:, 0, c:c + S], ones[:, :], ge[:, 0, c:c + S], 0.0, ALU.mult, ALU.add)
                    last = dve.tensor_tensor_scan(gb[:, 1, c:c + S][:, ::-1], ones[:, :], ge[:, 0, back:back + S][:, ::-1],
                                                  0.0, ALU.mult, ALU.add)
                link(last)
                attention(lambda i: na_bias[:, i, :])
                dve.wait_ge(s["rstd_ready"], seen("rstd_ready"))
                for k in range(4):
                    last = dve.scalar_tensor_tensor(out=mix[:, k, :], in0=mix[:, k, :], scalar=na_gain[:, layer, k:k + 1],
                                                    in1=rstd[:, 0:S], op0=ALU.mult, op1=ALU.mult)
                last.then_inc(s["mix_ready"], 1)
                bf, bb = gb[:, 0, :], gb[:, 1, :]
                qk_all = proj[:, 6:8, :].rearrange("p a b -> p (a b)")

                def diffs(i):
                    n = GLA_LEVELS[i]
                    shape = [P, 512 // n, n // 2]
                    f0, f1, b0, b1 = (level_halves(w, n, j) for w in (bf, bb) for j in (0, 1))
                    fm = f0[:, :, n // 2 - 1:n // 2].to_broadcast(shape)
                    bm = b1[:, :, 0:1].to_broadcast(shape)
                    q0, q1, k0, k1 = (level_halves(ge[:, i % 2, w * 512:w * 512 + 512], n, j) for w in (0, 1) for j in (0, 1))
                    dve.tensor_tensor(q1, f1, fm, ALU.subtract)
                    dve.tensor_tensor(q0, b0, bm, ALU.subtract)
                    dve.tensor_tensor(k0, fm, f0, ALU.subtract)
                    dve.tensor_tensor(k1, bm, b1, ALU.subtract).then_inc(s["diff_ready"], 1)

                def products(i):
                    dve.wait_ge(s["decay_ready"], seen("decay_ready"))
                    dve.tensor_tensor(ge[:, i % 2, :], ge[:, i % 2, :], qk_all, ALU.mult).then_inc(s["qk_ready"], 1)

                def read(i):
                    dve.wait_ge(s["level_done"], seen("level_done"))
                    for odd in range(2):
                        src = bank[(0, 2)[i % 2] + odd][:, :].rearrange("p (a b n) -> p a b n", a=2, b=2)
                        dst = ga[:, odd::2, 1:3, :] if i == 0 else ga[:, odd::2, 0::3, :]
                        if i < 2:
                            last = dve.tensor_copy(dst, src)
                        else:
                            m = gla_mask[:, i - 2, :].unsqueeze(1).unsqueeze(1).to_broadcast([P, 2, 2, P])
                            last = dve.copy_predicated(dst, m, src)
                    last.then_inc(s["level_read"], 1)
                    dve.wait_ge(s["level_read"], seen("level_read"))

                diffs(0)
                for i in range(len(GLA_LEVELS)):
                    if i:
                        read(i - 1)
                    if i + 1 < len(GLA_LEVELS):
                        diffs(i + 1)
                    products(i)
                read(len(GLA_LEVELS) - 1)
                read(len(GLA_LEVELS))
                dve.wait_ge(s["rstd_ready"], seen("rstd_ready", 2))
                for half in range(2):
                    last = dve.scalar_tensor_tensor(out=mix[:, 4 + 2 * half:6 + 2 * half, :].rearrange("p a b -> p (a b)"),
                                                    in0=bank[6 + half][:, :], scalar=gla_gain[:, layer:layer + 1],
                                                    in1=rstd[:, half * 512:half * 512 + 512], op0=ALU.mult, op1=ALU.mult)
                link(last)
                m = mix[:, 4:8, :].rearrange("p a b -> p (a b)")
                dve.tensor_tensor(m, m, proj[:, 8:10, :].rearrange("p a b -> p (a b)"), ALU.mult).then_inc(s["mix_ready"], 1)
                out_projection(0, layer)

            def two(v):
                return v.rearrange("p (a b) -> p a b", a=2)

            def both(v):
                return v.unsqueeze(1).to_broadcast([P, 2, v.shape[1]])

            def rotate(dst, plain, turned, tmp):
                dve.wait_ge(s["rot_done"], seen("rot_done"))
                dve.tensor_tensor(two(tmp), two(turned), both(rope_sin[:, :]), ALU.mult).then_inc(s["rot_read"], 1)
                dve.wait_ge(s["rot_read"], seen("rot_read"))
                link(dve.tensor_tensor(two(dst), two(plain), both(rope_cos[:, :]), ALU.mult))
                link(dve.tensor_tensor(dst, dst, tmp, ALU.add))

            def mixer2():
                norm_of(1, 0, 1)
                seen.skip("slot_done", M2_SLOTS)
                take_projection(M2_SLOTS)
                for i in range(4):
                    rotate(proj[:, i, :], proj[:, i, :], bank[4 + i % 2][:, :], att_t[:, 0, 0:512])
                xl = proj[:, 6:8, :].rearrange("p a (b t) -> p (a b) t", b=2)
                for c in range(4):
                    last = dve.tensor_scalar(xc[:, c, :], xl[:, c, :], lru_p[:, 4 * c + 3:4 * c + 4],
                                             lru_p[:, 16 + c:17 + c], ALU.mult, ALU.add)
                link(last)
                for back in range(1, 4):
                    for c in range(4):
                        last = dve.scalar_tensor_tensor(out=xc[:, c, back:S], in0=xl[:, c, 0:S - back],
                                                        scalar=lru_p[:, 4 * c + 3 - back:4 * c + 4 - back],
                                                        in1=xc[:, c, back:S], op0=ALU.mult, op1=ALU.add)
                    if back < 3:
                        link(last)
                last.then_inc(s["conv_ready"], 1)
                dve.wait_ge(s["conv_ready"], seen("conv_ready"))
                flat = lambda v: v[:, :, :].rearrange("p a b -> p (a b)")
                dve.wait_ge(s["lru_decay_ready"], seen("lru_decay_ready"))
                link(dve.tensor_tensor(flat(lg), flat(la), flat(la), ALU.mult))
                dve.scalar_tensor_tensor(out=flat(lb), in0=flat(lg), scalar=1.0, in1=flat(lb),
                                         op0=ALU.add, op1=ALU.mult).then_inc(s["lru_sq_ready"], 1)
                link(dve.tensor_tensor(flat(li), flat(li), flat(xc), ALU.mult))
                dve.wait_ge(s["lru_mult_ready"], seen("lru_mult_ready"))
                link(dve.tensor_tensor(flat(lb), flat(lb), flat(li), ALU.mult))
                for c in range(4):
                    last = dve.tensor_tensor_scan(xc[:, c, :], la[:, c, :], lb[:, c, :], 0.0, ALU.mult, ALU.add)
                link(last)
                dve.wait_ge(s["gelu_ready"], seen("gelu_ready"))
                dve.tensor_tensor(mix[:, 0:4, :].rearrange("p a b -> p (a b)"), flat(xc),
                                  proj[:, 8:10, :].rearrange("p a b -> p (a b)"), ALU.mult).then_inc(s["mix_ready"], 1)
                attention(lambda i: causal[:, :, :].rearrange("p a b -> p (a b)"))
                out_projection(1, 0)

            def mixer3():
                norm_of(1, 1, 1)
                seen.skip("slot_done", M3_SLOTS)
                take_projection(8)
                for i in range(4):
                    rotate(q_rope[:, i, :], proj[:, i, :], bank[4 + i % 2][:, :], rope_tmp[:, :])
                for g in range(NSA_GROUPS):
                    rotate(k_rope[:, g, :], bank[4 + 2 * g][:, :], bank[5 + 2 * g][:, :], rope_tmp[:, :])
                dve.wait_ge(s["cmp_dup_done"], seen("cmp_dup_done", 2))
                for g in range(NSA_GROUPS):
                    for kv in range(2):
                        for half in range(2):
                            p0 = DH * half
                            src = bank[2 + g][p0:p0 + DH, kv * S:kv * S + S].rearrange("p (i c two) -> p c i two", i=16, two=2)
                            for cb in range(2):
                                dst = cmp_g[p0:p0 + DH, kv, 8 * cb:8 * cb + 8, g * NCMP:g * NCMP + NCMP]
                                pos = cmp_pos[p0:p0 + DH, kv, 8 * cb:8 * cb + 8].unsqueeze(2).to_broadcast([DH, 8, NCMP])
                                last = dve.tensor_tensor(dst, src[:, :, cb:cb + NCMP, half], pos, ALU.add)
                last.then_inc(s["blocks_ready"], 1)

                def cmp_cols(v):
                    return v[:, 0:2 * (S + 16)].rearrange("p (a b) -> p a b", a=2)[:, :, 0:NCMP]

                def scores(i):
                    b = i % 2
                    T, big, small = att_t[:, b, :], bank[b], bank[2 + b]
                    dve.wait_ge(s["score_done"], seen("score_done"))
                    early, late = T[:, 16:16 + S], T[:, S + 32:S + 32 + 512]
                    dve.scalar_tensor_tensor(out=two(late), in0=two(big[:, :]), scalar=SCALE, in1=both(causal[:, 1, :]),
                                             op0=ALU.mult, op1=ALU.add)
                    dve.scalar_tensor_tensor(out=two(early), in0=two(small[:, 0:S]), scalar=SCALE, in1=both(causal[:, 0, 0:P]),
                                             op0=ALU.mult, op1=ALU.add)
                    dve.scalar_tensor_tensor(out=cmp_cols(T), in0=two(small[:, S:S + 32])[:, :, 0:NCMP], scalar=SCALE,
                                             in1=cmp_bias[:, :, 0:NCMP], op0=ALU.mult, op1=ALU.add).then_inc(s["score_read"], 1)
                    dve.wait_ge(s["score_read"], seen("score_read"))
                    dve.tensor_reduce(out=stats[:, b, 4:6], in_=two(late), axis=AXX, op=ALU.max)
                    dve.tensor_reduce(out=stats[:, b, 1:3], in_=two(early), axis=AXX, op=ALU.max)
                    link(dve.tensor_reduce(out=two(stats[:, b, 0:6])[:, :, 0], in_=cmp_cols(T), axis=AXX, op=ALU.max))
                    dve.tensor_scalar(stats[:, b, 6:12], stats[:, b, 0:6], -1.0, None, ALU.mult).then_inc(s["max_ready"], 1)

                def scale(i):
                    b = i % 2
                    dve.wait_ge(s["exp_ready"], seen("exp_ready"))
                    link(dve.reciprocal(stats[:, b, 18:24], stats[:, b, 12:18]))
                    link(dve.tensor_tensor(two(stats[:, b, 18:24]), two(stats[:, b, 18:24]), gates[:, :, 3 * i:3 * i + 3], ALU.mult))
                    for qt in range(TB):
                        f = stats[:, b, 18 + 3 * qt:21 + 3 * qt]
                        c0 = qt * (S + 16)
                        e = att_e[:, b, c0:c0 + NCMP]
                        dve.scalar_tensor_tensor(out=e, in0=e, scalar=f[:, 0:1], in1=cmp_keep[:, qt, 0:NCMP],
                                                 op0=ALU.mult, op1=ALU.mult)
                        n = (P, S)[qt]
                        for br in range(2):
                            e = att_e[:, b, c0 + 16 + br * n:c0 + 16 + br * n + n]
                            last = dve.tensor_scalar(e, e, f[:, 1 + br:2 + br], None, ALU.mult)
                    last.then_inc(s["probs_ready"], 1)

                def copy(i):
                    dve.wait_ge(s["pt_done"], seen("pt_done"))
                    if i >= 2:
                        dve.wait_ge(s["pv_done"], seen("pv_done"))
                    dve.tensor_copy(att_pt[:, i % 2, 512:768], bank[5][:, 0:S])
                    dve.tensor_copy(att_pt[0:NCMP, i % 2, 768:1024], bank[5][0:NCMP, S:2 * S]).then_inc(s["pt_half_copied"], 1)

                for i in range(NSA_HEADS + 2):
                    if i < NSA_HEADS:
                        scores(i)
                    if i >= 2:
                        copy(i - 2)
                    if 1 <= i <= NSA_HEADS:
                        scale(i - 1)
                seen.skip("pv_done", 2)
                out_projection(1, 1)

            dve.memset(ones[:, :], 1.0).then_inc(s["sum_step"], 2)
            dve.memset(warm[:, 0:1], 1.0).then_inc(s["act_ready"], 2)
            dve.memset(warm[:, 1:2], 1.0).then_inc(s["x_ready"], 2)
            dve.memset(warm[:, 2:3], 1.0).then_inc(s["out_added"], 2)
            dve.memset(warm[:, 3:4], 1.0).then_inc(s["proj_ready"], 2)
            dve.wait_ge(s["const_ready"], 16 * CONST_LOADS)
            lam, sp8, ns8 = lru_p[:, 28:32], lru_c[:, 0:4], lru_c[:, 4:8]
            u, z, z2, p, d = (lru_c[:, 8 + 4 * i:12 + 4 * i] for i in range(5))
            link(dve.tensor_scalar(ns8, lam, -1.0, None, ALU.mult))
            dve.tensor_tensor(ns8, ns8, lam, ALU.max).then_inc(s["lru_const_ready"], 1)
            dve.wait_ge(s["lru_exp_ready"], seen("lru_exp_ready"))
            link(dve.tensor_scalar(d, u, 2.0, None, ALU.add))
            link(dve.reciprocal(d, d))
            link(dve.tensor_tensor(z, u, d, ALU.mult))
            link(dve.tensor_tensor(z2, z, z, ALU.mult))
            link(dve.tensor_scalar(p, z2, 1.0 / 17, 1.0 / 15, ALU.mult, ALU.add))
            for k in (13, 11, 9, 7, 5, 3, 1):
                link(dve.tensor_tensor(p, p, z2, ALU.mult))
                link(dve.tensor_scalar(p, p, 1.0 / k, None, ALU.add))
            link(dve.tensor_tensor(p, p, z, ALU.mult))
            link(dve.tensor_scalar(p, p, 2.0, None, ALU.mult))
            link(dve.tensor_scalar(d, lam, -1.0, 0.0, ALU.mult, ALU.max))
            link(dve.tensor_tensor(p, p, d, ALU.add))
            dve.tensor_scalar(sp8, p, 8.0, None, ALU.mult)
            dve.tensor_scalar(ns8, p, -8.0, None, ALU.mult).then_inc(s["lru_const_ready"], 1)
            sum_slots()
            for stack in range(2):
                for layer in range(LAYERS):
                    ffn(stack, layer, 0, 2 * layer if stack == 0 else None)
                    if stack == 0:
                        mixer1(layer)
                    elif layer == 0:
                        mixer2()
                    else:
                        mixer3()
                    ffn(stack, layer, 2, 2 * layer + 1 if stack == 0 else None)
                if stack == 0:
                    for l in range(LAYERS):
                        for i in range(3):
                            c = (l * 9 + 3 * i) * KC
                            dve.scalar_tensor_tensor(out=mod_gain[:, l, i, :], in0=mod[:, c + KC:c + 2 * KC], scalar=1.0,
                                                     in1=gains[:, G_NORM2 + 3 * l + i, :], op0=ALU.add, op1=ALU.mult)
                            last = dve.tensor_scalar(mod_gate[:, l, i, :], mod[:, c + 2 * KC:c + 3 * KC],
                                                     1.0 if i == 1 else 0.5, None, ALU.mult)
                    link(last)
                    norm(x, lambda k: gains[:, G_FINAL1, k:k + 1])
                    sum_slots()
                else:
                    norm(h, lambda k: gains[:, G_FINAL2, k:k + 1])


def constants():
    f = np.float32
    d = np.arange(P) % DH
    half = DH // 8
    freqs = f(500000.0) ** (-np.arange(half, dtype=f) * f(2.0) / f(DH // 4))
    ang = np.arange(S, dtype=f)[None, :] * freqs.astype(f)[d % half][:, None]
    turned = (d < 2 * half)[:, None]
    cos, sin = np.where(turned, np.cos(ang), f(1)).astype(f), np.where(turned, np.sin(ang), f(0)).astype(f)
    rot = np.zeros((P, P), f)
    for o in range(P):
        if o % DH < half:
            rot[o + half, o] = -1
        elif o % DH < 2 * half:
            rot[o - half, o] = 1
    pick = [np.zeros((P, P), f) for _ in range(2)]
    for g in range(2):
        for o in range(P):
            pick[g][g * DH + o % DH, o] = 1
    mats = np.stack([rot, pick[0], pick[1], pick[0] @ rot, pick[1] @ rot], axis=1)
    q = np.arange(TB)[None, :, None] * P + np.arange(P)[:, None, None]
    causal = np.where(np.arange(S)[None, None, :] <= q, f(0), f(NEG))
    seen = np.arange(16)[None, None, :] * CMP_STRIDE + CMP_LEN - 1 <= q
    col = np.arange(P) % GRID_W
    start = np.clip(col - WIN_W // 2, 0, GRID_W - WIN_W)[:, None]
    kc = np.arange(GRID_W)[None, :]
    inside = (kc >= start) & (kc < start + WIN_W)
    na = np.repeat(np.where(inside, f(0), f(NEG))[:, None, :], ROWS, axis=1)
    i, j = np.arange(P)[:, None], np.arange(P)[None, :]
    masks = [(i // n == j // n) for n in GLA_LEVELS[2:] + [1]]
    return {
        "ident": np.eye(P, dtype=f), "rope_cos": cos, "rope_sin": sin, "mats": mats.astype(f),
        "causal": causal.astype(f), "cmp_bias": np.where(seen, f(0), f(NEG)).astype(f),
        "cmp_keep": seen.astype(f), "na_mask": na.astype(f),
        "gla_mask": np.stack(masks, axis=1).astype(np.uint32),
    }


def units(w):
    n = w.shape[1] // P
    return w.reshape(KC, P, n // 2, 2, P).transpose(2, 1, 3, 0, 4)


def gate_up(wg, wu):
    pair = [w.reshape(KC, P, FC, P) for w in (wg, wu)]
    return np.stack(pair, axis=0).transpose(3, 2, 0, 1, 4)


def per_partition(v):
    v = v.reshape(v.shape[:-1] + (v.shape[-1] // P, P))
    return np.moveaxis(v, -1, 0)


def lay_out(i):
    a = dict(constants())
    f = np.float32
    a["x"] = i["x"][0].T.reshape(KC, P, S).transpose(1, 0, 2)
    slots = np.zeros((TOTAL_SLOTS, P, 2, KC, P), f)
    wd = np.empty((FFNS * KC, P, FC, P), f)
    n = m = 0

    def put(block):
        nonlocal n
        slots[n:n + len(block)] = block
        n += len(block)

    def put_down(w):
        nonlocal m
        wd[m:m + KC] = w.reshape(FC, P, KC, P).transpose(2, 1, 0, 3)
        m += KC

    for l in range(LAYERS):
        put(gate_up(i["ffn1_wg"][l], i["ffn1_wu"][l]))
        put_down(i["ffn1_wd"][l])
        w = i["w_in"][l]
        q, k, v, gq, gk, gv, gr = (w[:, c:c + m_] for c, m_ in ((0, 512), (512, 512), (1024, 512), (1536, 256),
                                                              (1792, 256), (2048, 512), (2560, 512)))
        for part in (q, k, v, gq, gk, gr, gv, i["w_out"][l]):
            put(units(part))
        put(gate_up(i["ffn2_wg"][l], i["ffn2_wu"][l]))
        put_down(i["ffn2_wd"][l])
    for l in range(LAYERS):
        for j in range(2):
            w1 = i["ffn_w1_2"][l, j]
            put(gate_up(w1[:, :FF], w1[:, FF:]))
            put_down(i["ffn_w2_2"][l, j])
            if j:
                continue
            if l == 0:
                w = i["mix0_in_w_2"][0]
                xl, gl, q, k, v = (w[:, 512 * c:512 * c + 512] for c in range(5))
                for part in (q, k, v, xl, gl, i["mix0_out_w_2"][0]):
                    put(units(part))
            else:
                w = i["mix1_in_w_2"][0]
                kc, vc, ks, vs, kw, vw = (w[:, D + P * c:D + P * c + P] for c in range(6))
                put(units(w[:, :D]))
                for pair in ((ks, kw), (vs, vw), (kc, vc)):
                    put(units(np.concatenate(pair, axis=1)))
                gate = np.zeros((D, 2 * P), f)
                gate[:, :48] = w[:, D + 6 * P:]
                put(units(gate))
                for kv in range(2):
                    w1 = i["cmp_w1_2"][0, kv].reshape(CMP_PAIRS, P, P).transpose(1, 0, 2)
                    slots[n].reshape(P, CMP_PAIRS, P)[:] = w1
                    n += 1
                put(units(i["mix1_out_w_2"][0]))
    assert n == TOTAL_SLOTS and m == FFNS * KC
    a["slots"], a["wd"] = slots.reshape(TOTAL_SLOTS, P, SLOT), wd
    rpb = i["na_rpb"][:, :, WIN_H - ROWS:WIN_H + ROWS - 1]
    padded = np.zeros(rpb.shape[:3] + (2 * GRID_W - 1,), f)
    padded[..., GRID_W - WIN_W:GRID_W + WIN_W - 1] = rpb
    a["rpb"] = np.stack([padded[..., GRID_W - 1 - c:2 * GRID_W - 1 - c] for c in range(GRID_W)], axis=3)
    a["mod_w"] = i["mod_w_2"].reshape(LAYERS, KC, P, 9 * KC, P).transpose(0, 3, 2, 1, 4).reshape(MOD_CHUNKS, P, KC, P)
    a["mod_b"] = per_partition(i["mod_b_2"]).reshape(P, MOD_CHUNKS)
    a["cond"] = per_partition(i["c_2"][0])
    norms = [i[k][l] for l in range(LAYERS) for k in ("ffn1_norm", "mix_norm", "ffn2_norm")]
    norms += [i["final_norm"]] + [i["norm_g_2"][l, j] for l in range(LAYERS) for j in range(3)] + [i["final_norm_g_2"]]
    a["gains"] = per_partition(np.stack(norms))
    a["na_gain"] = per_partition(i["na_gain"])
    a["gla_gain"] = i["gla_gain"].T
    code = np.zeros((LAYERS, KC, P, 64), f)
    wg = np.zeros((64, LAYERS, 256), f)
    for way, key in enumerate(("w_gate_f", "w_gate_b")):
        c = 3072 + GLA_RANK * way
        code[..., 32 * way:32 * way + GLA_RANK] = i["w_in"][:, :, c:c + GLA_RANK].reshape(LAYERS, KC, P, GLA_RANK)
        wg[32 * way:32 * way + GLA_RANK] = i[key].transpose(1, 0, 2)
    a["w_code"] = code.transpose(2, 0, 1, 3)
    a["w_gate"] = wg
    a["b_gate"] = np.concatenate([per_partition(i["b_gate_f"]), per_partition(i["b_gate_b"])], axis=2)

    def block_diagonal(w):
        full = np.zeros((2, DH, 4, 2, DH), f)
        for j in range(2):
            full[j, :, :, j] = w.reshape(4, 2, DH, DH)[:, j].transpose(1, 0, 2)
        return full.reshape(P, 4, P)

    a["lru_w"] = np.stack([block_diagonal(i["lru_wa_2"][0]), block_diagonal(i["lru_wx_2"][0])], axis=1)
    taps = i["lru_conv_w_2"][0].reshape(4, 4, P).transpose(2, 1, 0).reshape(P, 16)
    a["lru_p"] = np.concatenate([taps] + [per_partition(v.reshape(-1)) for v in (
        i["lru_conv_b_2"][0], i["lru_ba_2"][0], i["lru_bx_2"][0], i["lru_lambda_2"][0])], axis=1)
    a["cmp_pos"] = i["cmp_pos_2"][0].reshape(2, CMP_PAIRS, 2, DH).transpose(2, 3, 0, 1).reshape(P, 2, CMP_PAIRS)
    w2 = i["cmp_w2_2"][0]
    v2 = np.zeros((P, P), f)
    v2[:, :DH] = w2[1]
    a["cmp_w2"] = np.stack([np.concatenate([w2[0], w2[0]], axis=1), v2], axis=1)
    return {k: np.ascontiguousarray(v) for k, v in a.items()}


def kernel(**inputs):
    import concourse.bacc as _bacc
    from concourse.bass_utils import run_bass_kernel_spmd as _run

    arrays = lay_out({k: np.asarray(v) for k, v in inputs.items()})
    nc = _bacc.Bacc("TRN2", target_bir_lowering=False, num_devices=1)
    args = {k: nc.dram_tensor(f"in_{k}_dram", v.shape, mybir.dt.from_np(v.dtype), kind="ExternalInput").ap()
            for k, v in arrays.items()}
    out = nc.dram_tensor("out_0_dram", (P, KC, S), F32, kind="ExternalOutput").ap()
    build_program(nc, args, out)
    r = _run(nc, [{f"in_{k}_dram": v for k, v in arrays.items()}], core_ids=[0])
    got = r.results[0]["out_0_dram"]
    return got.transpose(1, 0, 2).reshape(1, D, S).transpose(0, 2, 1)
```

```python
from contextlib import ExitStack, contextmanager

import numpy as np

import concourse.bass as bass
from concourse import mybir

F32 = mybir.dt.float32
F32R = mybir.dt.float32r
U32 = mybir.dt.uint32
U8 = mybir.dt.uint8
ALU = mybir.AluOpType
ACT = mybir.ActivationFunctionType
AXX = mybir.AxisListType.X

P = 128
S = 256
TB = S // P
D = 1024
KC = D // P
FF = 2816
FC = FF // P
LAYERS = 2
FFNS = 2 * 2 * LAYERS
EPS = 1e-6
NEG = -1e30
RING = 2
SLOT = 2 * KC * P
HF = FC // 2
HALF_SLOT = HF * P

GRID_W, ROWS, WIN_H, WIN_W = 64, S // 64, 8, 16
NA_HEADS, DH = 8, 64
GLA_HEADS, GLA_TAU, GLA_RANK = 4, 16.0, 16
CODE = 32 + GLA_RANK
SCALE = DH ** -0.5
NSA_HEADS, NSA_GROUPS = 16, 2
CMP_LEN, CMP_STRIDE = 32, 16
NCMP = S // CMP_STRIDE - 1
CMP_PAIRS = CMP_LEN // 2

M1_SLOTS = 12
M2_SLOTS = 10
M3_SLOTS = 10
OUT_SLOTS = D // (2 * P)
TOTAL_SLOTS = FFNS * FC + LAYERS * (M1_SLOTS + OUT_SLOTS) + M2_SLOTS + M3_SLOTS + 2 * OUT_SLOTS
GLA_LEVELS = [256, 128, 64, 32, 16, 8, 4, 2]
MOD_CHUNKS = LAYERS * 9 * KC
MOD_GROUPS = 12
MOD_GROUP = MOD_CHUNKS // MOD_GROUPS

G_FINAL1, G_NORM2, G_FINAL2 = 3 * LAYERS, 3 * LAYERS + 1, 6 * LAYERS + 1
N_GAINS = 6 * LAYERS + 2


class Seen:

    def __init__(self, **start):
        self.n = dict(start)
        self.turns = []

    def __call__(self, name, more=1):
        self.n[name] = self.n.get(name, 0) + more
        return self.value(name)

    def value(self, name, ahead=0):
        v = self.n.get(name, 0) + ahead
        for turn, per in self.turns:
            if per.get(name, 0):
                v = turn * per[name] + v
        return v

    def skip(self, name, more):
        self.n[name] = self.n.get(name, 0) + more


@contextmanager
def loop(eng, seen, count, **per):
    with eng.Fori(0, count) as turn:
        start = dict(seen.n)
        seen.turns.append((turn, per))
        yield turn
        seen.turns.pop()
        for name in set(seen.n) | set(per):
            took = seen.n.get(name, 0) - start.get(name, 0)
            assert took == per.get(name, 0), (name, took, per.get(name, 0))
    for name, k in per.items():
        seen.n[name] = start.get(name, 0) + count * k


def build_program(nc, a, out):
    ctx = ExitStack()
    with ctx:
        def sb(name, shape, dt=F32):
            return ctx.enter_context(nc.sbuf_tensor(name, shape, dt))

        sems = {}

        def sem(name):
            sems[name] = ctx.enter_context(nc.semaphore(name))
            return sems[name]

        slot = [sb(f"slot{i}", [P, SLOT]) for i in range(RING)]
        slot_hi = [sb(f"slot_hi{i}", [P, SLOT], F32R) for i in range(RING)]
        slot_lo = [sb(f"slot_lo{i}", [P, SLOT], F32R) for i in range(RING)]
        mod_raw = [sb(f"mod_raw{i}", [P, KC, P]) for i in range(2)]
        mod_acc = [sb(f"mod_acc{i}", [P, MOD_GROUP, P]) for i in range(2)]
        x = sb("x", [P, KC, S])
        h = sb("h", [P, KC, S])
        h_hi = sb("h_hi", [P, KC, S], F32R)
        h_lo = sb("h_lo", [P, KC, S], F32R)
        sq = sb("sq", [P, 2, 512])
        sqsum = sb("sqsum", [P, S])
        rstd = sb("rstd", [P, S])
        warm = sb("warm", [P, 8])
        ident = sb("ident", [P, P])
        ones = sb("ones", [P, S])
        rope_cos = sb("rope_cos", [P, S])
        rope_sin = sb("rope_sin", [P, S])
        mats = sb("mats", [P, 5, P])
        causal = sb("causal", [P, TB, S])
        na_mask = sb("na_mask", [P, ROWS, GRID_W])
        cmp_bias = sb("cmp_bias", [P, TB, 16])
        cmp_keep = sb("cmp_keep", [P, TB, 16])
        gla_mask = sb("gla_mask", [P, 7, P], U8)
        gains = sb("gains", [P, N_GAINS, KC])
        na_gain = sb("na_gain", [P, LAYERS, 4])
        gla_gain = sb("gla_gain", [P, LAYERS])
        w_code = sb("w_code", [P, LAYERS, KC, CODE])
        w_gate = sb("w_gate", [CODE, LAYERS, 256])
        b_gate = sb("b_gate", [P, LAYERS, 4])
        cond = sb("cond", [P, KC])
        mod_b = sb("mod_b", [P, MOD_CHUNKS])
        mod = sb("mod", [P, MOD_CHUNKS])
        mod_gain = sb("mod_gain", [P, LAYERS, 3, KC])
        mod_gate = sb("mod_gate", [P, LAYERS, 3, KC])
        lru_w = sb("lru_w", [P, 2, 4, P])
        lru_p = sb("lru_p", [P, 32])
        lru_c = sb("lru_c", [P, 48])
        cmp_pos = sb("cmp_pos", [P, 2, CMP_PAIRS])
        cmp_w2 = sb("cmp_w2", [P, 2, P])
        with nc.sbuf_tensor("act_hi", [P, FC, S], F32R) as act_hi, nc.sbuf_tensor("act_lo", [P, FC, S], F32R) as act_lo:
            pass
        ROOM = 19008
        room = sb("room", [P, ROOM])

        def carve(at, *shape):
            n = int(np.prod(shape))
            assert at[0] + n <= ROOM, (at[0], n)
            v = room[:, at[0]:at[0] + n]
            at[0] += n
            if len(shape) == 2:
                v = v.rearrange("p (a b) -> p a b", a=shape[0])
            elif len(shape) == 3:
                v = v.rearrange("p (a b c) -> p a b c", a=shape[0], b=shape[1])
            return v

        at = [2 * FC * S]
        sil = carve(at, 2, S)
        act_f = carve(at, 2, S)
        at = [0]
        proj = carve(at, 12, 512)
        att_t = carve(at, 2, 800)
        att_pt = carve(at, 2, 1024)
        mixer_room = at[0]
        wide_mask = proj[:, 0:2, :].rearrange("p a b -> p (a b)")[:, 0:7 * P].bitcast(U32)
        mix = h
        at = [mixer_room]
        gb = carve(at, 2, 512)
        ge = carve(at, 2, 1024)
        ga = carve(at, GLA_HEADS, 4, P)
        na_bias = carve(at, NA_HEADS, 512)
        gla_rstd = ge[:, 0, :]
        at = [mixer_room]
        xc = carve(at, 4, S)
        lr = carve(at, 4, S)
        li = carve(at, 4, S)
        la = carve(at, 4, S)
        lb = carve(at, 4, S)
        lg = carve(at, 4, S)
        at = [mixer_room]
        k_rope = carve(at, NSA_GROUPS, 512)
        rope_tmp = carve(at, 512)
        cmp_g = carve(at, 2, CMP_PAIRS, 2 * NCMP)
        cmp_h = carve(at, 2, 32)
        k_cmp = carve(at, 32)
        v_cmp = carve(at, 2, DH)
        gates = carve(at, TB, 48)
        q_rope = carve(at, 4, 512)
        stats = sb("stats", [P, 2, 32])
        code = sb("code", [CODE, S])

        bank = [ctx.enter_context(nc.psum_tensor(f"bank{i}", [P, 512], F32)) for i in range(8)]

        for name in (
            "const_ready", "x_loaded", "cond_loaded", "gains_loaded", "mask_loaded", "bias_ready", "out_stored",
            "slot0_ready", "slot1_ready", "mod0_ready", "mod1_ready",
            "slot_done", "ss_done", "mod_done", "score_done", "pt_done", "pv_done",
            "code_done", "logit_done", "level_done", "gla_o_done", "rot_done", "lru_gate_done",
            "cmp_dup_done", "cmp_done",
            "act_step", "hi_ready", "h_hi_ready", "mix_hi_ready", "sil_ready", "proj_ready", "sq_ready", "rstd_ready", "cond_ready", "exp_ready",
            "pt_copied", "o_copied", "decay_ready", "code_ready", "logit_read", "forget_ready", "na_sq_ready",
            "gla_sq_ready", "gla_rstd_ready", "lru_gate_ready", "lru_exp_ready", "lru_decay_ready", "lru_mult_ready",
            "gelu_ready", "hidden_ready", "cmp_ready", "gates_ready",
            "dve_step", "lo_ready", "h_raw", "mix_raw", "mix_split", "o_split", "act_ready", "x_ready", "out_added", "sum_step", "h_ready", "score_read",
            "max_ready", "probs_ready", "pt_half_copied", "diff_ready", "qk_ready", "level_read", "mix_ready",
            "final_ready", "rot_read", "conv_ready", "blocks_ready", "lru_sq_ready", "lru_const_ready",
            "mod_step", "bias_masked",
        ):
            sem(name)
        s = sems
        SLOT_READY = ["slot0_ready", "slot1_ready"]
        MOD_READY = ["mod0_ready", "mod1_ready"]
        CONST_LOADS = 18
        BIAS_PARTS = 4
        na_sq = att_t[:, :, :].rearrange("p a b -> p (a b)")[:, 0:1024]
        block = ctx.enter_context(nc.Block())

        @block.sync
        def _(sp):
            seen = Seen()

            def load_slots(first, count):
                with loop(sp, seen, count // RING, lo_ready=RING) as t:
                    for b in range(RING):
                        sp.wait_ge(s["lo_ready"], seen("lo_ready"))
                        sp.dma_start(slot[b][:, :], a["slots"][bass.ds(t * RING + (first + b), 1), :, :]
                                     .rearrange("o p n -> (o p) n")).then_inc(s[SLOT_READY[b]], 16)
                return first + count

            def load_down_slots(ffn, first, count):
                with loop(sp, seen, count, lo_ready=RING) as t:
                    for b in range(RING):
                        sp.wait_ge(s["lo_ready"], seen("lo_ready"))
                        sp.dma_start(slot[b][:, 0:HALF_SLOT], a["wd"][bass.ds(t * RING + ((ffn * KC + first) * RING + b), 1), :, :]
                                     .rearrange("o p n -> (o p) n")).then_inc(s[SLOT_READY[b]], 16)

            def load_constants(*which):
                for dst, name in which:
                    sp.dma_start(dst, a[name]).then_inc(s["const_ready"], 16)

            def load_bias(layer, part):
                heads = NA_HEADS // BIAS_PARTS
                sp.dma_start(na_bias[:, part * heads:part * heads + heads, :],
                             a["na_bias"][layer, :, part * heads:part * heads + heads, :]).then_inc(s["bias_ready"], 16)

            sp.dma_start(x[:, :, :], a["x"]).then_inc(s["x_loaded"], 16)
            sp.dma_start(cond[:, :], a["cond"]).then_inc(s["cond_loaded"], 16)
            sp.dma_start(gains[:, :, :], a["gains"]).then_inc(s["gains_loaded"], 16)
            n = load_slots(0, RING)
            sp.dma_start(wide_mask, a["gla_mask"]).then_inc(s["mask_loaded"], 16)
            n = load_slots(n, 4)
            load_constants((mod_b[:, :], "mod_b"), (ident[:, :], "ident"), (na_mask[:, :, :], "na_mask"),
                           (na_gain[:, :, :], "na_gain"), (gla_gain[:, :], "gla_gain"), (w_gate[:, :, :], "w_gate"),
                           (b_gate[:, :, :], "b_gate"))
            n = load_slots(n, 4)
            load_constants((w_code[:, :, :, :], "w_code"), (rope_cos[:, :], "rope_cos"), (rope_sin[:, :], "rope_sin"),
                           (lru_p[:, :], "lru_p"))
            n = load_slots(n, 4)
            load_constants((mats[:, :, :], "mats"), (causal[:, :, :], "causal"), (cmp_bias[:, :, :], "cmp_bias"),
                           (cmp_keep[:, :, :], "cmp_keep"))
            n = load_slots(n, 4)
            load_constants((lru_w[:, :, :, :], "lru_w"), (cmp_pos[:, :, :], "cmp_pos"), (cmp_w2[:, :, :], "cmp_w2"))
            first = n
            ffn = 0
            for stack in range(2):
                for layer in range(LAYERS):
                    n = load_slots(n, FC - first)
                    first = 0
                    for part in range(BIAS_PARTS):
                        load_down_slots(ffn, part * KC // BIAS_PARTS, KC // BIAS_PARTS)
                        if stack == 0:
                            load_bias(layer, part)
                    ffn += 1
                    mixer = M1_SLOTS if stack == 0 else M2_SLOTS if layer == 0 else M3_SLOTS
                    n = load_slots(n, mixer + OUT_SLOTS)
                    n = load_slots(n, FC)
                    load_down_slots(ffn, 0, KC)
                    ffn += 1
            assert n == TOTAL_SLOTS and ffn == FFNS
            sp.wait_ge(s["final_ready"], 2 * KC)
            sp.dma_start(out, h[:, :, :]).then_inc(s["out_stored"], 16)
            sp.wait_ge(s["out_stored"], 16)

        @block.gpsimd
        def _(pool):
            seen = Seen()

            def link(ins):
                ins.then_inc(s["mod_step"], 1)
                pool.wait_ge(s["mod_step"], seen("mod_step"))

            def load_mod(n, b):
                pool.dma_start(mod_raw[b][:, :, :], a["mod_w"][bass.ds(n, 1), :, :, :].rearrange("o p k n -> (o p) k n")
                               ).then_inc(s[MOD_READY[b]], 16)

            def mod_chunk(acc, c, b):
                w = mod_raw[b]
                pool.wait_ge(s[MOD_READY[b]], seen(MOD_READY[b], 16))
                link(pool.tensor_tensor(w[:, :, :], w[:, :, :], cond[:, :].unsqueeze(2).to_broadcast([P, KC, P]), ALU.mult))
                link(pool.tensor_tensor(w[:, 0:4, :], w[:, 0:4, :], w[:, 4:8, :], ALU.add))
                link(pool.tensor_tensor(w[:, 0:2, :], w[:, 0:2, :], w[:, 2:4, :], ALU.add))
                link(pool.tensor_tensor(acc[:, bass.ds(c, 1), :], w[:, 0:1, :], w[:, 1:2, :], ALU.add))

            load_mod(0, 0)
            load_mod(1, 1)
            pool.wait_ge(s["cond_ready"], seen("cond_ready"))
            for g in range(MOD_GROUPS):
                if g >= 2:
                    pool.wait_ge(s["mod_done"], seen("mod_done"))
                acc = mod_acc[g % 2]
                tail = int(g == MOD_GROUPS - 1)
                with loop(pool, seen, MOD_GROUP // 2 - tail, mod0_ready=16, mod1_ready=16, mod_step=8) as t:
                    for b in range(2):
                        mod_chunk(acc, t * 2 + b, b)
                        load_mod(t * 2 + (g * MOD_GROUP + 2 + b), b)
                if tail:
                    mod_chunk(acc, MOD_GROUP - 2, 0)
                    mod_chunk(acc, MOD_GROUP - 1, 1)
                if g in (1, 1 + MOD_GROUPS // 2):
                    pool.wait_ge(s["const_ready"], 16 * CONST_LOADS)
                    pool.wait_ge(s["bias_ready"], seen("bias_ready", 16 * BIAS_PARTS))
                    for head in range(NA_HEADS):
                        for qt in range(TB):
                            v = na_bias[:, head, qt * S:qt * S + S]
                            pool.tensor_tensor(v, v, na_mask[:, :, :].rearrange("p a b -> p (a b)"),
                                               ALU.add).then_inc(s["bias_masked"], 1)

        @block.tensor
        def _(pe):
            seen = Seen(sum_step=2, lo_ready=2)

            def three(o, w, x_hi, x_lo, b, first, last, skip=False):
                pe.matmul(o, slot_hi[b][:, w:w + P], x_hi, start=first, stop=False, skip_group_check=skip)
                pe.matmul(o, slot_hi[b][:, w:w + P], x_lo, start=False, stop=False, skip_group_check=skip)
                return pe.matmul(o, slot_lo[b][:, w:w + P], x_hi, start=False, stop=last, skip_group_check=skip)

            def slot_products(b, target, fresh=None):
                pe.wait_ge(s["lo_ready"], seen("lo_ready"))
                order = [(u, k) for k in range(KC) for u in range(2)] if fresh else [(u, k) for u in range(2) for k in range(KC)]
                for u, k in order:
                    if fresh and u == 0:
                        pe.wait_ge(s[fresh], seen(fresh))
                    last = three(target[:, u * S:u * S + S], (u * KC + k) * P, h_hi[:, k, :], h_lo[:, k, :], b,
                                 k == 0 and not (fresh and u), k == KC - 1, bool(fresh))
                last.then_inc(s["slot_done"], 1)

            def slot_products_by_token(b, target, units=2, cols=P):
                pe.wait_ge(s["lo_ready"], seen("lo_ready"))
                hi, lo = (w[b][:, :].rearrange("p (u k n) -> p u k n", u=2, k=KC) for w in (slot_hi, slot_lo))
                for tb in range(TB):
                    o = target[:, tb * S:tb * S + units * cols]
                    if units == 2:
                        o = o.rearrange("p (u n) -> p u n", u=2)
                    for k in range(KC):
                        w_hi, w_lo = (w[:, :, k, 0:cols] if units == 2 else w[:, 0, k, 0:cols] for w in (hi, lo))
                        t_hi, t_lo = (v[:, k, tb * P:tb * P + P] for v in (h_hi, h_lo))
                        pe.matmul(o, t_hi, w_hi, start=(k == 0), stop=False)
                        pe.matmul(o, t_hi, w_lo, start=False, stop=False)
                        last = pe.matmul(o, t_lo, w_hi, start=False, stop=(k == KC - 1))
                last.then_inc(s["slot_done"], 1)

            def norm_sum(batches):
                pe.wait_ge(s["sum_step"], seen("sum_step", batches - 1))
                pe.matmul(bank[4][:, 0:S], ones[:, 0:P], sqsum[:, :], start=True, stop=False)
                pe.wait_ge(s["sq_ready"], seen("sq_ready", batches))
                halves = KC // batches
                for j in range(halves):
                    last = pe.matmul(bank[4][:, 0:S], ones[:, 0:P], sq[:, 1, j * S:j * S + S], start=False, stop=(j == halves - 1))
                last.then_inc(s["ss_done"], 1)

            def mod_sums(group):
                pe.wait_ge(s["mod_step"], seen("mod_step", 4 * MOD_GROUP))
                for c in range(MOD_GROUP):
                    last = pe.matmul(bank[5][:, c:c + 1], mod_acc[group % 2][:, c, :], ones[:, 0:1], start=True, stop=True)
                last.then_inc(s["mod_done"], 1)

            def ffn(group):
                for b in range(RING):
                    pe.wait_ge(s["act_ready"], seen("act_ready"))
                    slot_products(b, bank[b], None if b else "h_ready")
                with loop(pe, seen, FC // 2 - 1, lo_ready=2, act_ready=2):
                    for b in range(RING):
                        pe.wait_ge(s["act_ready"], seen("act_ready"))
                        slot_products(b, bank[b])
                if group is not None:
                    mod_sums(group)
                all_hidden = seen.value("act_ready", 2)
                with loop(pe, seen, KC // 2, lo_ready=4, x_ready=2):
                    for j in range(2):
                        pe.wait_ge(s["x_ready"], seen("x_ready"))
                        for b in range(RING):
                            pe.wait_ge(s["lo_ready"], seen("lo_ready"))
                            if j == 0 and b == 1:
                                pe.wait_ge(s["act_ready"], all_hidden)
                            for f in range(HF):
                                c = b * HF + f
                                last = three(bank[2 + j][:, 0:S], f * P, act_hi[:, c, :], act_lo[:, c, :], b,
                                             c == 0, c == FC - 1)
                            last.then_inc(s["slot_done"], 1)
                norm_sum(KC)
                if group is not None:
                    mod_sums(group + 1)

            def projection(kinds):
                for n, kind in enumerate(kinds):
                    pe.wait_ge(s["proj_ready"], seen("proj_ready"))
                    if kind == "f":
                        slot_products(n % 2, bank[n % 2], None if n else "h_ready")
                    elif kind == "t":
                        slot_products_by_token(n % 2, bank[n % 2])
                    else:
                        slot_products_by_token(n % 2, bank[n % 2], units=1, cols=48)

            def out_projection(fresh="mix_split"):
                for n in range(OUT_SLOTS):
                    pe.wait_ge(s["out_added"], seen("out_added"))
                    slot_products(n % 2, bank[2 + n % 2], None if n else fresh)
                norm_sum(OUT_SLOTS)

            def attention(q, k, v, heads, freed):
                def scores(i):
                    if i >= 2:
                        pe.wait_ge(s["score_read"], seen("score_read"))
                    p0 = DH * (i % 2)
                    for qt in range(TB):
                        last = pe.matmul(bank[2 + i % 2][:, qt * S:qt * S + S], q(i)[p0:p0 + DH, qt * P:qt * P + P],
                                         k(i)[p0:p0 + DH, :], start=True, stop=True)
                    last.then_inc(s["score_done"], 1)

                def transposes(i):
                    pe.wait_ge(s["probs_ready"], seen("probs_ready"))
                    for kb in range(TB):
                        for qt in range(TB):
                            last = pe.transpose(bank[4 + i % 2][:, kb * S + qt * P:kb * S + qt * P + P],
                                                att_t[:, i % 2, qt * S + kb * P:qt * S + kb * P + P], ident[:, :])
                    last.then_inc(s["pt_done"], 1)

                def values(i):
                    pe.wait_ge(s["pt_copied"], seen("pt_copied"))
                    if i >= 4 and i % 2 == 0:
                        pe.wait_ge(s[freed], seen(freed))
                    p0 = DH * (i % 2)
                    for kb in range(TB):
                        last = pe.matmul(bank[6 + i // 2 % 2][p0:p0 + DH, 0:S], v(i, kb),
                                         att_pt[:, i % 2, kb * S:kb * S + S], start=(kb == 0), stop=(kb == TB - 1))
                    last.then_inc(s["pv_done"], 1)

                for i in range(heads + 2):
                    if i < heads:
                        scores(i)
                    if i >= 2:
                        values(i - 2)
                    if 1 <= i <= heads:
                        transposes(i - 1)
                seen.skip("score_read", 2)
                seen.skip(freed, 2)

            def mixer1(layer):
                projection("ffff" "tt" "ffff" "tt")
                pe.wait_ge(s["const_ready"], 16 * CONST_LOADS)
                for k in range(KC):
                    last = pe.matmul(bank[4][0:CODE, 0:S], w_code[:, layer, k, :], h[:, k, :],
                                     start=(k == 0), stop=(k == KC - 1))
                last.then_inc(s["code_done"], 1)
                pe.wait_ge(s["code_ready"], seen("code_ready"))
                for way in range(2):
                    for pair in range(2):
                        last = pe.matmul(bank[6 + way][:, pair * S:pair * S + S],
                                         w_gate[32 * way:32 * way + GLA_RANK, layer, pair * P:pair * P + P],
                                         code[32 * way:32 * way + GLA_RANK, :], start=True, stop=True)
                last.then_inc(s["logit_done"], 1)
                pe.wait_ge(s["proj_ready"], seen.value("proj_ready", 2))
                pe.wait_ge(s["logit_read"], seen("logit_read"))
                attention(lambda i: proj[:, i // 4, (i // 2 % 2) * S:(i // 2 % 2) * S + S],
                          lambda i: proj[:, 2 + i // 4, (i // 2 % 2) * S:(i // 2 % 2) * S + S],
                          lambda i, kb: proj[:, 4 + i // 4, kb * S + (i % 4) * DH:kb * S + (i % 4) * DH + DH],
                          NA_HEADS, "o_copied")
                mod_sums(6 * layer + 2)
                pe.wait_ge(s["na_sq_ready"], seen("na_sq_ready"))
                for c in range(4):
                    last = pe.matmul(bank[4][:, 0:S], ones[:, 0:P], na_sq[:, c * S:c * S + S], start=(c == 0), stop=(c == 3))
                last.then_inc(s["ss_done"], 1)
                for i, n in enumerate(GLA_LEVELS + [1]):
                    if n > 1:
                        pe.wait_ge(s["qk_ready"], seen("qk_ready"))
                    if i >= 2:
                        pe.wait_ge(s["level_read"], seen("level_read"))
                    qk = ge[:, i % 2, :] if n > 1 else proj[:, 6:8, :].rearrange("p a b -> p (a b)")
                    for sblk in range(TB):
                        tblk = 1 - sblk if n == S else sblk
                        for head in range(GLA_HEADS):
                            p0, c = DH * (head % 2), (head // 2) * S
                            o = (head // 2 * TB + sblk) * P
                            last = pe.matmul(bank[(0, 2)[i % 2] + head % 2][:, o:o + P],
                                             qk[p0:p0 + DH, 512 + c + sblk * P:512 + c + sblk * P + P],
                                             qk[p0:p0 + DH, c + tblk * P:c + tblk * P + P], start=True, stop=True)
                    last.then_inc(s["level_done"], 1)
                pe.wait_ge(s["level_read"], seen("level_read", 2))
                for head in range(GLA_HEADS):
                    for sblk in range(TB):
                        v0 = sblk * S + (head % 2) * P
                        last = pe.matmul(bank[6 + head // 2][:, (head % 2) * S:(head % 2) * S + S],
                                         proj[:, 10 + head // 2, v0:v0 + P], ga[:, head, 2 * sblk:2 * sblk + 2, :].rearrange("p a b -> p (a b)"),
                                         start=(sblk == 0), stop=(sblk == TB - 1))
                last.then_inc(s["gla_o_done"], 1)
                for half in range(2):
                    pe.wait_ge(s["gla_sq_ready"], seen("gla_sq_ready"))
                    pe.matmul(bank[half][:, :], ones[:, 0:P], sq[:, half, :], start=True, stop=True).then_inc(s["ss_done"], 1)
                mod_sums(6 * layer + 3)
                out_projection()

            def mixer2():
                projection("ffff" "tt" "ffff")
                pe.wait_ge(s["proj_ready"], seen.value("proj_ready", 2))
                for i in range(4):
                    if i >= 2:
                        pe.wait_ge(s["rot_read"], seen("rot_read"))
                    pe.matmul(bank[4 + i % 2][:, :], mats[:, 0, :], proj[:, i, :], start=True, stop=True
                              ).then_inc(s["rot_done"], 1)
                pe.wait_ge(s["rot_read"], seen("rot_read", 2))
                pe.wait_ge(s["conv_ready"], seen("conv_ready"))
                for c in range(4):
                    if c >= 2:
                        pe.wait_ge(s["lru_gate_ready"], seen("lru_gate_ready"))
                    for gate in range(2):
                        last = pe.matmul(bank[6 + c % 2][:, gate * S:gate * S + S], lru_w[:, gate, c, :],
                                         xc[:, c, :], start=True, stop=True)
                    last.then_inc(s["lru_gate_done"], 1)
                pe.wait_ge(s["lru_gate_ready"], seen("lru_gate_ready", 2))
                attention(lambda i: proj[:, i // 4, (i // 2 % 2) * S:(i // 2 % 2) * S + S],
                          lambda i: proj[:, 2 + i // 4, (i // 2 % 2) * S:(i // 2 % 2) * S + S],
                          lambda i, kb: proj[:, 4 + i // 4, kb * S + (i % 4) * DH:kb * S + (i % 4) * DH + DH],
                          NA_HEADS, "o_split")
                pe.wait_ge(s["mix_split"], seen("mix_split", 4))
                pe.wait_ge(s["o_split"], seen.value("o_split"))
                out_projection(None)

            def mixer3():
                projection("ffff" "f" "t" "f" "g")
                pe.wait_ge(s["proj_ready"], seen.value("proj_ready", 2))
                for i in range(4):
                    if i >= 2:
                        pe.wait_ge(s["rot_read"], seen("rot_read"))
                    pe.matmul(bank[4 + i % 2][:, :], mats[:, 0, :], proj[:, i, :], start=True, stop=True
                              ).then_inc(s["rot_done"], 1)
                pe.wait_ge(s["rot_read"], seen("rot_read", 2))
                for g in range(NSA_GROUPS):
                    pe.matmul(bank[4 + 2 * g][:, :], mats[:, 1 + g, :], proj[:, 4, :], start=True, stop=True)
                    pe.matmul(bank[5 + 2 * g][:, :], mats[:, 3 + g, :], proj[:, 4, :], start=True, stop=True
                              ).then_inc(s["rot_done"], 1)
                for g in range(NSA_GROUPS):
                    pe.matmul(bank[2 + g][:, :], mats[:, 1 + g, :], proj[:, 6, :], start=True, stop=True
                              ).then_inc(s["cmp_dup_done"], 1)
                for kv in range(2):
                    pe.wait_ge(s["lo_ready"], seen("lo_ready"))
                    if kv == 0:
                        pe.wait_ge(s["blocks_ready"], seen("blocks_ready"))
                    for c in range(CMP_PAIRS):
                        for part in (slot_hi, slot_lo):
                            last = pe.matmul(bank[kv][:, 0:2 * NCMP], part[kv][:, c * P:c * P + P].bitcast(F32), cmp_g[:, kv, c, :],
                                             start=(c == 0 and part is slot_hi),
                                             stop=(c == CMP_PAIRS - 1 and part is slot_lo))
                    last.then_inc(s["slot_done"], 1)
                pe.wait_ge(s["hidden_ready"], seen("hidden_ready", 2))
                pe.matmul(bank[4][:, 0:2 * NCMP], cmp_w2[:, 0, :], cmp_h[:, 0, 0:2 * NCMP], start=True, stop=True)
                for g in range(NSA_GROUPS):
                    last = pe.matmul(bank[5][0:NCMP, g * DH:g * DH + DH], cmp_h[:, 1, g * NCMP:g * NCMP + NCMP],
                                     cmp_w2[:, 1, 0:DH], start=True, stop=True)
                last.then_inc(s["cmp_done"], 1)
                pe.wait_ge(s["cmp_ready"], seen("cmp_ready"))
                heads = NSA_HEADS

                def scores(i):
                    if i >= 2:
                        pe.wait_ge(s["score_read"], seen("score_read"))
                    p0, g = DH * (i % 2), i // (NSA_HEADS // NSA_GROUPS)
                    c0 = (i // 2 % 2) * S
                    q = q_rope[p0:p0 + DH, i // 4, c0:c0 + S]
                    qn = proj[p0:p0 + DH, i // 4, c0:c0 + S]
                    kk = k_rope[p0:p0 + DH, g, :].rearrange("p (b t) -> p b t", b=2)
                    big, small = bank[i % 2], bank[2 + i % 2]
                    pe.matmul(big[:, :], q[:, P:S], kk[:, :, :], start=True, stop=True)
                    pe.matmul(small[:, 0:S].rearrange("p (b t) -> p b t", b=2), q[:, 0:P], kk[:, :, 0:P], start=True, stop=True)
                    for qt in range(TB):
                        last = pe.matmul(small[:, S + 16 * qt:S + 16 * qt + NCMP], qn[:, qt * P:qt * P + P],
                                         k_cmp[p0:p0 + DH, g * NCMP:g * NCMP + NCMP], start=True, stop=True)
                    last.then_inc(s["score_done"], 1)

                def transposes(i):
                    pe.wait_ge(s["probs_ready"], seen("probs_ready"))
                    e = att_t[:, i % 2, :]
                    X, Y = bank[4], bank[5]
                    for br in range(2):
                        pe.transpose(X[:, br * S:br * S + P], e[:, 16 + br * P:16 + br * P + P], ident[:, :])
                        q1 = 16 + S + 16 + br * S
                        pe.transpose(X[:, br * S + P:br * S + S], e[:, q1:q1 + P], ident[:, :])
                        pe.transpose(Y[:, br * P:br * P + P], e[:, q1 + P:q1 + S], ident[:, :])
                    for qt in range(TB):
                        c0 = qt * (16 + S)
                        last = pe.transpose(Y[0:NCMP, S + qt * P:S + qt * P + P], e[:, c0:c0 + NCMP], ident[:, :])
                    last.then_inc(s["pt_done"], 1)

                def values(i):
                    pe.wait_ge(s["pt_copied"], seen("pt_copied"))
                    pe.wait_ge(s["pt_half_copied"], seen("pt_half_copied"))
                    if i >= 4 and i % 2 == 0:
                        pe.wait_ge(s["o_split"], seen("o_split"))
                    p0, g = DH * (i % 2), i // (NSA_HEADS // NSA_GROUPS)
                    o = bank[6 + i // 2 % 2][p0:p0 + DH, 0:S]
                    pt = att_pt[:, i % 2, :]

                    def v(br, kb):
                        return proj[:, 5, kb * S + br * P + g * DH:kb * S + br * P + g * DH + DH]

                    pe.matmul(o, v(0, 0), pt[:, 0:S], start=True, stop=False)
                    pe.matmul(o[:, P:S], v(0, 1), pt[:, 512:640], start=False, stop=False, skip_group_check=True)
                    pe.matmul(o[:, P:S], v(1, 1), pt[:, 640:768], start=False, stop=False, skip_group_check=True)
                    pe.matmul(o, v_cmp[0:NCMP, g, :], pt[0:NCMP, 768:1024], start=False, stop=False, skip_group_check=True)
                    pe.matmul(o, v(1, 0), pt[:, S:2 * S], start=False, stop=True).then_inc(s["pv_done"], 1)

                for i in range(heads + 2):
                    if i < heads:
                        scores(i)
                    if i >= 2:
                        values(i - 2)
                    if 1 <= i <= heads:
                        transposes(i - 1)
                seen.skip("score_read", 2)
                seen.skip("o_split", 2)
                pe.wait_ge(s["o_split"], seen.value("o_split"))
                out_projection(None)

            norm_sum(OUT_SLOTS)
            for stack in range(2):
                for layer in range(LAYERS):
                    ffn(6 * layer if stack == 0 else None)
                    if stack == 0:
                        mixer1(layer)
                    elif layer == 0:
                        mixer2()
                    else:
                        mixer3()
                    ffn(6 * layer + 4 if stack == 0 else None)
                if stack == 0:
                    norm_sum(OUT_SLOTS)

        @block.scalar
        def _(act):
            seen = Seen(x_ready=2, out_added=2)

            def link(ins):
                ins.then_inc(s["act_step"], 1)
                act.wait_ge(s["act_step"], seen("act_step"))

            def split_hi(b, cols=SLOT):
                act.wait_ge(s[SLOT_READY[b]], seen(SLOT_READY[b], 16))
                for c0, c1 in ((0, cols // 2), (cols // 2, cols)):
                    act.activation(slot_hi[b][:, c0:c1], slot[b][:, c0:c1], ACT.Copy).then_inc(s["hi_ready"], 1)

            def rstd_of(target, sums, width, ready="rstd_ready"):
                act.wait_ge(s["ss_done"], seen("ss_done"))
                link(act.activation(target, sums, ACT.Ln, bias=EPS, scale=1.0 / width))
                act.activation(target, target, ACT.Exp, scale=-0.5).then_inc(s[ready], 1)

            def squares_of_slots():
                for n in range(OUT_SLOTS):
                    act.wait_ge(s["sum_step"], seen("sum_step"))
                    act.activation(sq[:, n % 2, :], x[:, 2 * n:2 * n + 2, :].rearrange("p a b -> p (a b)"),
                                   ACT.Square).then_inc(s["sq_ready"], 1)
                seen.skip("sum_step", -1)

            def norm(shift=None):
                rstd_of(rstd[:, :], bank[4][:, 0:S], D)
                for k in range(KC):
                    act.wait_ge(s["h_raw"], seen("h_raw"))
                    if shift is None:
                        ins = act.activation(h_hi[:, k, :], h[:, k, :], ACT.Copy)
                    else:
                        ins = act.activation(h_hi[:, k, :], h[:, k, :], ACT.Identity, bias=mod[:, shift + k:shift + k + 1])
                    ins.then_inc(s["h_hi_ready"], 1)
                split_hi(1)

            def shift_of(stack, layer, i):
                return (layer * 9 + 3 * i) * KC if stack else None

            def ffn(stack, layer, i, last_one=False):
                norm(shift_of(stack, layer, i))

                def gate(b, cols):
                    act.wait_ge(s["slot_done"], seen("slot_done"))
                    act.wait_ge(s["act_ready"], seen("act_ready"))
                    act.activation(sil[:, b, :], bank[b][:, 0:S], ACT.Silu).then_inc(s["sil_ready"], 1)
                    split_hi(b, cols)

                with loop(act, seen, FC // 2 - 1, slot_done=2, act_ready=2, slot0_ready=16, slot1_ready=16, act_step=1):
                    link(act.activation(warm[:, 4:5], ones[:, 0:1], ACT.Silu))
                    for b in range(2):
                        gate(b, SLOT)
                for b in range(2):
                    gate(b, HALF_SLOT)
                link(act.activation(warm[:, 4:5], ones[:, 0:1], ACT.Ln))

                def square(j, b):
                    act.wait_ge(s["x_ready"], seen("x_ready"))
                    act.wait_ge(s["sum_step"], seen("sum_step"))
                    act.activation(sq[:, b, 0:S], x[:, bass.ds(j, 1), :].rearrange("p a b -> p (a b)"),
                                   ACT.Square).then_inc(s["sq_ready"], 1)

                with loop(act, seen, KC // 2 - 1, x_ready=2, sum_step=2, slot_done=4, slot0_ready=32, slot1_ready=32) as t:
                    for j in range(2):
                        for b in range(RING):
                            act.wait_ge(s["slot_done"], seen("slot_done"))
                            split_hi(b, HALF_SLOT)
                        square(t * 2 + j, j)
                for b in range(RING):
                    act.wait_ge(s["slot_done"], seen("slot_done"))
                    split_hi(b, HALF_SLOT)
                square(KC - 2, 0)
                act.wait_ge(s["slot_done"], seen("slot_done"))
                if not last_one:
                    split_hi(0)
                square(KC - 1, 1)
                seen.skip("sum_step", -1)
                act.wait_ge(s["slot_done"], seen("slot_done"))

            def projection(kinds, scaled=(), swish=()):
                for n, kind in enumerate(kinds):
                    act.wait_ge(s["slot_done"], seen("slot_done"))
                    if kind == "g":
                        last = act.activation(gates[:, :, :], bank[n % 2][:, :].rearrange("p (b n) -> p b n", b=TB)[:, :, 0:48],
                                              ACT.Sigmoid)
                    elif n in swish:
                        last = act.activation(proj[:, n, :], bank[n % 2][:, :], ACT.Silu)
                    else:
                        last = act.activation(proj[:, n, :], bank[n % 2][:, :], ACT.Copy, scale=SCALE if n in scaled else 1.0)
                    last.then_inc(s["proj_ready"], 1)
                    split_hi(n % 2)

            def out_projection():
                for n in range(OUT_SLOTS):
                    act.wait_ge(s["slot_done"], seen("slot_done"))
                    if n < OUT_SLOTS - 1:
                        split_hi(n % 2)
                    act.wait_ge(s["out_added"], seen("out_added"))
                    act.wait_ge(s["sum_step"], seen("sum_step"))
                    act.activation(sq[:, n % 2, :], x[:, 2 * n:2 * n + 2, :].rearrange("p a b -> p (a b)"),
                                   ACT.Square).then_inc(s["sq_ready"], 1)
                seen.skip("sum_step", -1)

            def attention(heads, first_chunk, segments, copies, split):
                def exps(i):
                    act.wait_ge(s["max_ready"], seen("max_ready"))
                    for j, (c, n) in enumerate(segments):
                        k = len(segments)
                        last = act.activation(att_t[:, i % 2, c:c + n], att_t[:, i % 2, c:c + n], ACT.Exp,
                                              bias=stats[:, i % 2, k + j:k + j + 1],
                                              accum_out=stats[:, i % 2, 2 * k + j:2 * k + j + 1])
                    last.then_inc(s["exp_ready"], 1)

                def copy(i):
                    act.wait_ge(s["pt_done"], seen("pt_done"))
                    if i >= 2:
                        act.wait_ge(s["pv_done"], seen("pv_done"))
                    for dst, src in copies(i):
                        last = act.activation(dst, src, ACT.Copy)
                    last.then_inc(s["pt_copied"], 1)

                def copy_output(i):
                    act.wait_ge(s["pv_done"], seen.value("pv_done", 1 if i < heads - 1 else 2))
                    target = h_hi if split else mix
                    act.activation(target[:, first_chunk + i // 2, :], bank[6 + i // 2 % 2][:, 0:S],
                                   ACT.Copy).then_inc(s["o_copied"], 1)

                for i in range(heads + 2):
                    if i < heads:
                        exps(i)
                    if 1 <= i <= heads:
                        copy(i - 1)
                    if i >= 2 and i % 2 == 1:
                        copy_output(i - 2)
                seen.skip("pv_done", 2)

            def plain_attention(first_chunk, split):
                attention(NA_HEADS, first_chunk, [(0, S), (S, S)],
                          lambda i: [(att_pt[:, i % 2, 0:512], bank[4 + i % 2][:, :])], split)

            def split_mix(first):
                act.wait_ge(s["mix_raw"], seen("mix_raw"))
                act.activation(h_hi[:, first:first + 4, :], mix[:, first:first + 4, :], ACT.Copy).then_inc(s["mix_hi_ready"], 1)

            def mixer1(layer):
                norm()
                projection("ffff" "tt" "ffff" "tt", scaled=(6,), swish=(8, 9))
                act.wait_ge(s["const_ready"], 16 * CONST_LOADS)
                act.wait_ge(s["code_done"], seen("code_done"))
                act.activation(code[:, :], bank[4][0:CODE, 0:S], ACT.Copy).then_inc(s["code_ready"], 1)
                act.wait_ge(s["logit_done"], seen("logit_done"))
                z, e = ge[:, 0, :], ge[:, 1, :]
                for way in range(2):
                    for pair in range(2):
                        c = (way * 2 + pair) * S
                        last = act.activation(z[:, c:c + S], bank[6 + way][:, pair * S:pair * S + S], ACT.Identity,
                                              bias=b_gate[:, layer, way * 2 + pair:way * 2 + pair + 1])
                last.then_inc(s["logit_read"], 1)
                act.wait_ge(s["logit_read"], seen("logit_read"))
                link(act.activation(e, z, ACT.Abs))
                link(act.activation(e, e, ACT.Exp, scale=-1.0))
                if layer == 0:
                    act.wait_ge(s["lru_const_ready"], seen("lru_const_ready"))
                    act.activation(lru_c[:, 8:12], lru_c[:, 4:8], ACT.Exp, scale=-1.0).then_inc(s["lru_exp_ready"], 1)
                act.activation(e, e, ACT.Ln, bias=1.0).then_inc(s["forget_ready"], 1)
                plain_attention(0, False)
                act.wait_ge(s["o_copied"], seen("o_copied", NA_HEADS // 2))
                act.activation(na_sq, mix[:, 0:4, :].rearrange("p a b -> p (a b)"), ACT.Square).then_inc(s["na_sq_ready"], 1)
                rstd_of(rstd[:, :], bank[4][:, 0:S], NA_HEADS * DH)
                split_mix(0)
                for i in range(len(GLA_LEVELS)):
                    act.wait_ge(s["diff_ready"], seen("diff_ready"))
                    act.activation(ge[:, i % 2, :], ge[:, i % 2, :], ACT.Exp, scale=1.0 / GLA_TAU).then_inc(s["decay_ready"], 1)
                act.wait_ge(s["gla_o_done"], seen("gla_o_done"))
                for half in range(2):
                    act.activation(sq[:, half, :], bank[6 + half][:, :], ACT.Square).then_inc(s["gla_sq_ready"], 1)
                for half in range(2):
                    rstd_of(gla_rstd[:, half * 512:half * 512 + 512], bank[half][:, :], P, "gla_rstd_ready")
                split_mix(4)
                out_projection()

            def mixer2():
                norm(shift_of(1, 0, 1))
                projection("ffff" "tt" "ffff")
                for c in range(4):
                    act.wait_ge(s["lru_gate_done"], seen("lru_gate_done"))
                    act.activation(lr[:, c, :], bank[6 + c % 2][:, 0:S], ACT.Sigmoid, bias=lru_p[:, 20 + c:21 + c])
                    act.activation(li[:, c, :], bank[6 + c % 2][:, S:2 * S], ACT.Sigmoid, bias=lru_p[:, 24 + c:25 + c]
                                   ).then_inc(s["lru_gate_ready"], 1)
                act.wait_ge(s["lru_const_ready"], seen("lru_const_ready"))
                act.wait_ge(s["lru_gate_ready"], seen("lru_gate_ready", 4))
                for c in range(4):
                    act.activation(la[:, c, :], lr[:, c, :], ACT.Exp, scale=lru_c[:, 4 + c:5 + c])
                    last = act.activation(lb[:, c, :], lr[:, c, :], ACT.Tanh, scale=lru_c[:, c:c + 1])
                last.then_inc(s["lru_decay_ready"], 1)
                act.wait_ge(s["lru_sq_ready"], seen("lru_sq_ready"))
                lbf = lb[:, :, :].rearrange("p a b -> p (a b)")
                act.activation(lbf, lbf, ACT.Sqrt).then_inc(s["lru_mult_ready"], 1)
                act.wait_ge(s["proj_ready"], 2 + LAYERS * M1_SLOTS + M2_SLOTS)
                act.activation(proj[:, 8:10, :], proj[:, 8:10, :], ACT.Gelu_apprx_tanh).then_inc(s["gelu_ready"], 1)
                split_mix(0)
                plain_attention(4, True)
                seen.skip("o_copied", 4)
                out_projection()

            def mixer3():
                norm(shift_of(1, 1, 1))
                projection("ffff" "f" "t" "f" "g")
                for kv in range(2):
                    act.wait_ge(s["slot_done"], seen("slot_done"))
                    act.activation(cmp_h[:, kv, 0:2 * NCMP], bank[kv][:, 0:2 * NCMP], ACT.Gelu_apprx_tanh
                                   ).then_inc(s["hidden_ready"], 1)
                    split_hi(kv)
                act.wait_ge(s["cmp_done"], seen("cmp_done"))
                act.activation(k_cmp[:, 0:2 * NCMP], bank[4][:, 0:2 * NCMP], ACT.Copy)
                act.activation(v_cmp[0:NCMP, :, :].rearrange("p a b -> p (a b)"), bank[5][0:NCMP, 0:P], ACT.Copy
                               ).then_inc(s["cmp_ready"], 1)
                segments = [(0, NCMP), (16, P), (16 + P, P), (S + 16, NCMP), (S + 32, S), (2 * S + 32, S)]
                attention(NSA_HEADS, 0, segments,
                          lambda i: [(att_pt[:, i % 2, 0:512], bank[4][:, :])], True)
                seen.skip("o_copied", 8)
                out_projection()

            act.wait_ge(s["x_loaded"], 16)
            squares_of_slots()
            act.wait_ge(s["cond_loaded"], 16)
            act.activation(cond[:, :], cond[:, :], ACT.Silu).then_inc(s["cond_ready"], 1)
            split_hi(0)
            for stack in range(2):
                for layer in range(LAYERS):
                    ffn(stack, layer, 0)
                    if stack == 0:
                        mixer1(layer)
                    elif layer == 0:
                        mixer2()
                    else:
                        mixer3()
                    ffn(stack, layer, 2, stack == 1 and layer == LAYERS - 1)
                rstd_of(rstd[:, :], bank[4][:, 0:S], D)
                if stack == 0:
                    act.wait_ge(s["final_ready"], KC)
                    squares_of_slots()

        @block.vector
        def _(dve):
            seen = Seen(sum_step=1, proj_ready=2, out_added=2)

            def link(ins):
                ins.then_inc(s["dve_step"], 1)
                dve.wait_ge(s["dve_step"], seen("dve_step"))

            def split_lo(b, part, cols=SLOT):
                dve.wait_ge(s["hi_ready"], seen("hi_ready"))
                c0, c1 = ((0, cols // 2), (cols // 2, cols))[part]
                ins = dve.tensor_tensor(slot_lo[b][:, c0:c1], slot[b][:, c0:c1], slot_hi[b][:, c0:c1].bitcast(F32), ALU.subtract)
                if part:
                    ins.then_inc(s["lo_ready"], 1)

            def split_both(b, cols=SLOT):
                split_lo(b, 0, cols)
                split_lo(b, 1, cols)

            def add_squares(halves, n):
                dve.wait_ge(s["sq_ready"], seen("sq_ready"))
                dve.wait_ge(s["sum_step"], seen("sum_step"))
                for j in range(halves):
                    ins = dve.tensor_tensor(sqsum[:, :], sqsum[:, :], sq[:, n % 2, j * S:j * S + S], ALU.add)
                    if j < halves - 1:
                        link(ins)
                ins.then_inc(s["sum_step"], 1)

            def clear_sum():
                link(dve.memset(sqsum[:, :], 0.0))

            def sum_slots():
                clear_sum()
                for n in range(OUT_SLOTS - 1):
                    add_squares(2, n)
                seen.skip("sq_ready", 1)

            def final_norm(dst, i):
                dve.wait_ge(s["rstd_ready"], seen("rstd_ready"))
                for k in range(KC):
                    dve.scalar_tensor_tensor(out=dst[:, k, :], in0=x[:, k, :], scalar=gains[:, i, k:k + 1],
                                             in1=rstd[:, :], op0=ALU.mult, op1=ALU.mult).then_inc(s["final_ready"], 1)

            def norm_of(stack, layer, i, group=None):
                dve.wait_ge(s["rstd_ready"], seen("rstd_ready"))
                lag = 2
                for n in range(KC + lag):
                    if n < KC:
                        gain = mod_gain[:, layer, i, n:n + 1] if stack else gains[:, 3 * layer + i, n:n + 1]
                        dve.scalar_tensor_tensor(out=h[:, n, :], in0=x[:, n, :], scalar=gain,
                                                 in1=rstd[:, :], op0=ALU.mult, op1=ALU.mult).then_inc(s["h_raw"], 1)
                    if n >= lag:
                        k = n - lag
                        dve.wait_ge(s["h_hi_ready"], seen("h_hi_ready"))
                        hi = h_hi[:, k, :].bitcast(F32)
                        if stack:
                            c = (layer * 9 + 3 * i) * KC + k
                            ins = dve.scalar_tensor_tensor(out=h_lo[:, k, :], in0=h[:, k, :], scalar=mod[:, c:c + 1],
                                                           in1=hi, op0=ALU.add, op1=ALU.subtract)
                        else:
                            ins = dve.tensor_tensor(h_lo[:, k, :], h[:, k, :], hi, ALU.subtract)
                        ins.then_inc(s["h_ready"], 1)
                split_both(1)
                if group is not None:
                    mod_group(group)

            def mod_group(group):
                c = group * MOD_GROUP
                dve.wait_ge(s["mod_done"], seen("mod_done"))
                link(dve.tensor_tensor(mod[:, c:c + MOD_GROUP], bank[5][:, 0:MOD_GROUP], mod_b[:, c:c + MOD_GROUP], ALU.add))

            def ffn(stack, layer, i, group, last_one=False):
                norm_of(stack, layer, i, 6 * (layer - 1) + 5 if stack == 0 and i == 0 and layer else None)
                if group == 0:
                    dve.wait_ge(s["mask_loaded"], 16)
                    link(dve.tensor_copy(gla_mask[:, :, :].rearrange("p a b -> p (a b)"), wide_mask))
                seen.skip("slot_done", FC)

                def hidden(c, b, cols):
                    dve.wait_ge(s["sil_ready"], seen("sil_ready"))
                    dve.tensor_tensor(act_f[:, b, :], sil[:, b, :], bank[b][:, S:2 * S], ALU.mult).then_inc(s["dve_step"], 1)
                    value = seen("dve_step")
                    split_lo(b, 0, cols)
                    dve.wait_ge(s["dve_step"], value)
                    hi, lo = (v[:, bass.ds(c, 1), :].rearrange("p a b -> p (a b)") for v in (act_hi, act_lo))
                    dve.tensor_copy(hi, act_f[:, b, :]).then_inc(s["dve_step"], 1)
                    value = seen("dve_step")
                    split_lo(b, 1, cols)
                    dve.wait_ge(s["dve_step"], value)
                    dve.tensor_tensor(lo, act_f[:, b, :], hi.bitcast(F32), ALU.subtract).then_inc(s["act_ready"], 1)

                with loop(dve, seen, FC // 2 - 1, sil_ready=2, dve_step=4, hi_ready=4) as t:
                    for b in range(2):
                        hidden(t * 2 + b, b, SLOT)
                for b in range(2):
                    hidden(FC - 2 + b, b, HALF_SLOT)
                if group == 0:
                    dve.wait_ge(s["const_ready"], 16 * CONST_LOADS)
                if group is not None:
                    mod_group(group)
                clear_sum()

                def residual(j, bk):
                    dve.wait_ge(s["slot_done"], seen("slot_done", 2))
                    xj = x[:, bass.ds(j, 1), :].rearrange("p a b -> p (a b)")
                    half = 0.5 if stack == 0 else mod_gate[:, layer, i, bass.ds(j, 1)]
                    dve.scalar_tensor_tensor(out=xj, in0=bank[2 + bk][:, 0:S], scalar=half, in1=xj,
                                             op0=ALU.mult, op1=ALU.add).then_inc(s["x_ready"], 1)

                with loop(dve, seen, KC // 2 - 1, slot_done=4, sq_ready=2, sum_step=2, hi_ready=8) as t:
                    for j in range(2):
                        split_both(0, HALF_SLOT)
                        residual(t * 2 + j, j)
                        split_both(1, HALF_SLOT)
                        add_squares(1, j)
                split_both(0, HALF_SLOT)
                residual(KC - 2, 0)
                split_both(1, HALF_SLOT)
                add_squares(1, 0)
                if not last_one:
                    split_both(0)
                residual(KC - 1, 1)
                seen.skip("sq_ready", 1)

            def take_projection(slots):
                for n in range(slots):
                    split_both(n % 2)
                seen.skip("slot_done", slots)
                dve.wait_ge(s["proj_ready"], seen("proj_ready", slots))

            def split_mix(first):
                dve.wait_ge(s["mix_hi_ready"], seen("mix_hi_ready"))
                for k in range(first, first + 4):
                    dve.tensor_tensor(h_lo[:, k, :], mix[:, k, :], h_hi[:, k, :].bitcast(F32), ALU.subtract
                                      ).then_inc(s["mix_split"], 1)

            def split_output(chunk, i):
                dve.wait_ge(s["o_copied"], seen("o_copied"))
                dve.tensor_tensor(h_lo[:, chunk, :], bank[6 + i // 2 % 2][:, 0:S], h_hi[:, chunk, :].bitcast(F32),
                                  ALU.subtract).then_inc(s["o_split"], 1)

            def out_projection(stack, layer):
                clear_sum()
                for n in range(OUT_SLOTS):
                    dve.wait_ge(s["slot_done"], seen("slot_done"))
                    for j in range(2):
                        k = 2 * n + j
                        y = bank[2 + n % 2][:, j * S:j * S + S]
                        if stack == 0:
                            ins = dve.tensor_tensor(x[:, k, :], y, x[:, k, :], ALU.add)
                        else:
                            ins = dve.scalar_tensor_tensor(out=x[:, k, :], in0=y, scalar=mod_gate[:, layer, 1, k:k + 1],
                                                           in1=x[:, k, :], op0=ALU.mult, op1=ALU.add)
                    ins.then_inc(s["out_added"], 1)
                    if n < OUT_SLOTS - 1:
                        split_both(n % 2)
                        add_squares(2, n)
                seen.skip("sq_ready", 1)

            def attention(bias, first_chunk=None):
                def scores(i):
                    b = i % 2
                    dve.wait_ge(s["score_done"], seen("score_done"))
                    if i >= 2:
                        dve.wait_ge(s["pt_done"], seen("pt_done"))
                    dve.scalar_tensor_tensor(out=att_t[:, b, 0:512], in0=bank[2 + b][:, :], scalar=SCALE,
                                             in1=bias(i), op0=ALU.mult, op1=ALU.add).then_inc(s["score_read"], 1)
                    dve.wait_ge(s["score_read"], seen("score_read"))
                    link(dve.tensor_reduce(out=stats[:, b, 0:2], in_=att_t[:, b, 0:512].rearrange("p (a b) -> p a b", a=2),
                                           axis=AXX, op=ALU.max))
                    dve.tensor_scalar(stats[:, b, 2:4], stats[:, b, 0:2], -1.0, None, ALU.mult).then_inc(s["max_ready"], 1)

                def scale(i):
                    b = i % 2
                    dve.wait_ge(s["exp_ready"], seen("exp_ready"))
                    link(dve.reciprocal(stats[:, b, 6:8], stats[:, b, 4:6]))
                    for qt in range(TB):
                        e = att_t[:, b, qt * S:qt * S + S]
                        last = dve.tensor_scalar(e, e, stats[:, b, 6 + qt:7 + qt], None, ALU.mult)
                    last.then_inc(s["probs_ready"], 1)

                for i in range(NA_HEADS + 3):
                    if i < NA_HEADS:
                        scores(i)
                    if first_chunk is not None and i >= 4 and i % 2 == 0:
                        split_output(first_chunk + (i - 4) // 2, i - 4)
                    if 1 <= i <= NA_HEADS:
                        scale(i - 1)
                if first_chunk is None:
                    seen.skip("o_copied", NA_HEADS // 2)
                seen.skip("pt_done", 2)
                seen.skip("pv_done", NA_HEADS)

            def level_halves(way, n, pick):
                return way.rearrange("p (b two t) -> p b two t", two=2, t=n // 2)[:, :, pick, :]

            lam, sp8, ns8 = lru_p[:, 28:32], lru_c[:, 0:4], lru_c[:, 4:8]
            u, z, z2, p, d = (lru_c[:, 8 + 4 * i:12 + 4 * i] for i in range(5))

            def lru_magnitude():
                link(dve.tensor_scalar(ns8, lam, -1.0, None, ALU.mult))
                dve.tensor_tensor(ns8, ns8, lam, ALU.max).then_inc(s["lru_const_ready"], 1)

            def lru_softplus():
                dve.wait_ge(s["lru_exp_ready"], seen("lru_exp_ready"))
                link(dve.tensor_scalar(d, u, 2.0, None, ALU.add))
                link(dve.reciprocal(d, d))
                link(dve.tensor_tensor(z, u, d, ALU.mult))
                link(dve.tensor_tensor(z2, z, z, ALU.mult))
                link(dve.tensor_scalar(p, z2, 1.0 / 17, 1.0 / 15, ALU.mult, ALU.add))
                for k in (13, 11, 9, 7, 5, 3, 1):
                    link(dve.tensor_tensor(p, p, z2, ALU.mult))
                    link(dve.tensor_scalar(p, p, 1.0 / k, None, ALU.add))
                link(dve.tensor_tensor(p, p, z, ALU.mult))
                link(dve.tensor_scalar(p, p, 2.0, None, ALU.mult))
                link(dve.tensor_scalar(d, lam, -1.0, 0.0, ALU.mult, ALU.max))
                link(dve.tensor_tensor(p, p, d, ALU.add))
                dve.tensor_scalar(sp8, p, 8.0, None, ALU.mult)
                dve.tensor_scalar(ns8, p, -8.0, None, ALU.mult).then_inc(s["lru_const_ready"], 1)

            def mixer1(layer):
                norm_of(0, layer, 1, 6 * layer + 1)
                if layer == 0:
                    lru_magnitude()
                take_projection(M1_SLOTS)
                dve.wait_ge(s["bias_masked"], seen("bias_masked", NA_HEADS * TB))
                dve.wait_ge(s["forget_ready"], seen("forget_ready"))
                link(dve.scalar_tensor_tensor(out=ge[:, 0, :], in0=ge[:, 0, :], scalar=0.0, in1=ge[:, 1, :],
                                              op0=ALU.min, op1=ALU.subtract))
                for pair in range(2):
                    c, back = pair * S, 512 + pair * S
                    dve.tensor_tensor_scan(gb[:, 0, c:c + S], ones[:, :], ge[:, 0, c:c + S], 0.0, ALU.mult, ALU.add)
                    last = dve.tensor_tensor_scan(gb[:, 1, c:c + S][:, ::-1], ones[:, :], ge[:, 0, back:back + S][:, ::-1],
                                                  0.0, ALU.mult, ALU.add)
                link(last)
                attention(lambda i: na_bias[:, i, :])
                mod_group(6 * layer + 2)
                dve.wait_ge(s["rstd_ready"], seen("rstd_ready"))
                for k in range(4):
                    last = dve.scalar_tensor_tensor(out=mix[:, k, :], in0=mix[:, k, :], scalar=na_gain[:, layer, k:k + 1],
                                                    in1=rstd[:, :], op0=ALU.mult, op1=ALU.mult)
                last.then_inc(s["mix_raw"], 1)
                bf, bb = gb[:, 0, :], gb[:, 1, :]
                qk_all = proj[:, 6:8, :].rearrange("p a b -> p (a b)")

                def diffs(i):
                    n = GLA_LEVELS[i]
                    shape = [P, 512 // n, n // 2]
                    f0, f1, b0, b1 = (level_halves(w, n, j) for w in (bf, bb) for j in (0, 1))
                    fm = f0[:, :, n // 2 - 1:n // 2].to_broadcast(shape)
                    bm = b1[:, :, 0:1].to_broadcast(shape)
                    q0, q1, k0, k1 = (level_halves(ge[:, i % 2, w * 512:w * 512 + 512], n, j) for w in (0, 1) for j in (0, 1))
                    dve.tensor_tensor(q1, f1, fm, ALU.subtract)
                    dve.tensor_tensor(q0, b0, bm, ALU.subtract)
                    dve.tensor_tensor(k0, fm, f0, ALU.subtract)
                    dve.tensor_tensor(k1, bm, b1, ALU.subtract).then_inc(s["diff_ready"], 1)

                def products(i):
                    dve.wait_ge(s["decay_ready"], seen("decay_ready"))
                    dve.tensor_tensor(ge[:, i % 2, :], ge[:, i % 2, :], qk_all, ALU.mult).then_inc(s["qk_ready"], 1)

                def read(i):
                    dve.wait_ge(s["level_done"], seen("level_done"))
                    for odd in range(2):
                        src = bank[(0, 2)[i % 2] + odd][:, :].rearrange("p (a b n) -> p a b n", a=2, b=2)
                        dst = ga[:, odd::2, 1:3, :] if i == 0 else ga[:, odd::2, 0::3, :]
                        if i < 2:
                            last = dve.tensor_copy(dst, src)
                        else:
                            m = gla_mask[:, i - 2, :].unsqueeze(1).unsqueeze(1).to_broadcast([P, 2, 2, P])
                            last = dve.copy_predicated(dst, m, src)
                    last.then_inc(s["level_read"], 1)
                    dve.wait_ge(s["level_read"], seen("level_read"))

                diffs(0)
                split_mix(0)
                for i in range(len(GLA_LEVELS)):
                    if i:
                        read(i - 1)
                    if i + 1 < len(GLA_LEVELS):
                        diffs(i + 1)
                    products(i)
                read(len(GLA_LEVELS) - 1)
                read(len(GLA_LEVELS))
                if layer == 0:
                    lru_softplus()
                dve.wait_ge(s["gla_rstd_ready"], seen("gla_rstd_ready", 2))
                for half in range(2):
                    last = dve.scalar_tensor_tensor(out=mix[:, 4 + 2 * half:6 + 2 * half, :].rearrange("p a b -> p (a b)"),
                                                    in0=bank[6 + half][:, :], scalar=gla_gain[:, layer:layer + 1],
                                                    in1=gla_rstd[:, half * 512:half * 512 + 512], op0=ALU.mult, op1=ALU.mult)
                link(last)
                m = mix[:, 4:8, :].rearrange("p a b -> p (a b)")
                dve.tensor_tensor(m, m, proj[:, 8:10, :].rearrange("p a b -> p (a b)"), ALU.mult).then_inc(s["mix_raw"], 1)
                split_mix(4)
                mod_group(6 * layer + 3)
                out_projection(0, layer)

            def two(v):
                return v.rearrange("p (a b) -> p a b", a=2)

            def both(v):
                return v.unsqueeze(1).to_broadcast([P, 2, v.shape[1]])

            def rotate(dst, plain, turned, tmp):
                dve.wait_ge(s["rot_done"], seen("rot_done"))
                dve.tensor_tensor(two(tmp), two(turned), both(rope_sin[:, :]), ALU.mult).then_inc(s["rot_read"], 1)
                dve.wait_ge(s["rot_read"], seen("rot_read"))
                link(dve.tensor_tensor(two(dst), two(plain), both(rope_cos[:, :]), ALU.mult))
                link(dve.tensor_tensor(dst, dst, tmp, ALU.add))

            def mixer2():
                norm_of(1, 0, 1)
                take_projection(M2_SLOTS)
                for i in range(4):
                    rotate(proj[:, i, :], proj[:, i, :], bank[4 + i % 2][:, :], att_t[:, 0, 0:512])
                xl = proj[:, 6:8, :].rearrange("p a (b t) -> p (a b) t", b=2)
                for c in range(4):
                    last = dve.tensor_scalar(xc[:, c, :], xl[:, c, :], lru_p[:, 4 * c + 3:4 * c + 4],
                                             lru_p[:, 16 + c:17 + c], ALU.mult, ALU.add)
                link(last)
                for back in range(1, 4):
                    for c in range(4):
                        last = dve.scalar_tensor_tensor(out=xc[:, c, back:S], in0=xl[:, c, 0:S - back],
                                                        scalar=lru_p[:, 4 * c + 3 - back:4 * c + 4 - back],
                                                        in1=xc[:, c, back:S], op0=ALU.mult, op1=ALU.add)
                    if back < 3:
                        link(last)
                last.then_inc(s["conv_ready"], 1)
                dve.wait_ge(s["conv_ready"], seen("conv_ready"))
                flat = lambda v: v[:, :, :].rearrange("p a b -> p (a b)")
                dve.wait_ge(s["lru_decay_ready"], seen("lru_decay_ready"))
                link(dve.tensor_tensor(flat(lg), flat(la), flat(la), ALU.mult))
                dve.scalar_tensor_tensor(out=flat(lb), in0=flat(lg), scalar=1.0, in1=flat(lb),
                                         op0=ALU.add, op1=ALU.mult).then_inc(s["lru_sq_ready"], 1)
                link(dve.tensor_tensor(flat(li), flat(li), flat(xc), ALU.mult))
                dve.wait_ge(s["lru_mult_ready"], seen("lru_mult_ready"))
                link(dve.tensor_tensor(flat(lb), flat(lb), flat(li), ALU.mult))
                for c in range(4):
                    last = dve.tensor_tensor_scan(xc[:, c, :], la[:, c, :], lb[:, c, :], 0.0, ALU.mult, ALU.add)
                link(last)
                dve.wait_ge(s["gelu_ready"], seen("gelu_ready"))
                dve.tensor_tensor(mix[:, 0:4, :].rearrange("p a b -> p (a b)"), flat(xc),
                                  proj[:, 8:10, :].rearrange("p a b -> p (a b)"), ALU.mult).then_inc(s["mix_raw"], 1)
                split_mix(0)
                attention(lambda i: causal[:, :, :].rearrange("p a b -> p (a b)"), 4)
                out_projection(1, 0)

            def mixer3():
                norm_of(1, 1, 1)
                take_projection(8)
                for i in range(4):
                    rotate(q_rope[:, i, :], proj[:, i, :], bank[4 + i % 2][:, :], rope_tmp[:, :])
                for g in range(NSA_GROUPS):
                    rotate(k_rope[:, g, :], bank[4 + 2 * g][:, :], bank[5 + 2 * g][:, :], rope_tmp[:, :])
                dve.wait_ge(s["cmp_dup_done"], seen("cmp_dup_done", 2))
                for g in range(NSA_GROUPS):
                    for kv in range(2):
                        for half in range(2):
                            p0 = DH * half
                            src = bank[2 + g][p0:p0 + DH, kv * S:kv * S + S].rearrange("p (i c two) -> p c i two", i=16, two=2)
                            for cb in range(2):
                                dst = cmp_g[p0:p0 + DH, kv, 8 * cb:8 * cb + 8, g * NCMP:g * NCMP + NCMP]
                                pos = cmp_pos[p0:p0 + DH, kv, 8 * cb:8 * cb + 8].unsqueeze(2).to_broadcast([DH, 8, NCMP])
                                last = dve.tensor_tensor(dst, src[:, :, cb:cb + NCMP, half], pos, ALU.add)
                last.then_inc(s["blocks_ready"], 1)
                for kv in range(2):
                    split_both(kv)
                seen.skip("slot_done", 2)

                def cmp_cols(v):
                    return v[:, 0:2 * (S + 16)].rearrange("p (a b) -> p a b", a=2)[:, :, 0:NCMP]

                def scores(i):
                    b = i % 2
                    T, big, small = att_t[:, b, :], bank[b], bank[2 + b]
                    dve.wait_ge(s["score_done"], seen("score_done"))
                    early, late = T[:, 16:16 + S], T[:, S + 32:S + 32 + 512]
                    dve.scalar_tensor_tensor(out=two(late), in0=two(big[:, :]), scalar=SCALE, in1=both(causal[:, 1, :]),
                                             op0=ALU.mult, op1=ALU.add)
                    dve.scalar_tensor_tensor(out=two(early), in0=two(small[:, 0:S]), scalar=SCALE, in1=both(causal[:, 0, 0:P]),
                                             op0=ALU.mult, op1=ALU.add)
                    dve.scalar_tensor_tensor(out=cmp_cols(T), in0=two(small[:, S:S + 32])[:, :, 0:NCMP], scalar=SCALE,
                                             in1=cmp_bias[:, :, 0:NCMP], op0=ALU.mult, op1=ALU.add).then_inc(s["score_read"], 1)
                    dve.wait_ge(s["score_read"], seen("score_read"))
                    dve.tensor_reduce(out=stats[:, b, 4:6], in_=two(late), axis=AXX, op=ALU.max)
                    dve.tensor_reduce(out=stats[:, b, 1:3], in_=two(early), axis=AXX, op=ALU.max)
                    link(dve.tensor_reduce(out=two(stats[:, b, 0:6])[:, :, 0], in_=cmp_cols(T), axis=AXX, op=ALU.max))
                    dve.tensor_scalar(stats[:, b, 6:12], stats[:, b, 0:6], -1.0, None, ALU.mult).then_inc(s["max_ready"], 1)

                def scale(i):
                    b = i % 2
                    dve.wait_ge(s["exp_ready"], seen("exp_ready"))
                    link(dve.reciprocal(stats[:, b, 18:24], stats[:, b, 12:18]))
                    link(dve.tensor_tensor(two(stats[:, b, 18:24]), two(stats[:, b, 18:24]), gates[:, :, 3 * i:3 * i + 3], ALU.mult))
                    for qt in range(TB):
                        f = stats[:, b, 18 + 3 * qt:21 + 3 * qt]
                        c0 = qt * (S + 16)
                        e = att_t[:, b, c0:c0 + NCMP]
                        dve.scalar_tensor_tensor(out=e, in0=e, scalar=f[:, 0:1], in1=cmp_keep[:, qt, 0:NCMP],
                                                 op0=ALU.mult, op1=ALU.mult)
                        n = (P, S)[qt]
                        for br in range(2):
                            e = att_t[:, b, c0 + 16 + br * n:c0 + 16 + br * n + n]
                            last = dve.tensor_scalar(e, e, f[:, 1 + br:2 + br], None, ALU.mult)
                    last.then_inc(s["probs_ready"], 1)

                def copy(i):
                    dve.wait_ge(s["pt_done"], seen("pt_done"))
                    if i >= 2:
                        dve.wait_ge(s["pv_done"], seen("pv_done"))
                    dve.tensor_copy(att_pt[:, i % 2, 512:768], bank[5][:, 0:S])
                    dve.tensor_copy(att_pt[0:NCMP, i % 2, 768:1024], bank[5][0:NCMP, S:2 * S]).then_inc(s["pt_half_copied"], 1)

                for i in range(NSA_HEADS + 3):
                    if 2 <= i < NSA_HEADS + 2:
                        copy(i - 2)
                    if i < NSA_HEADS:
                        scores(i)
                    if i >= 4 and i % 2 == 0:
                        split_output((i - 4) // 2, i - 4)
                    if 1 <= i <= NSA_HEADS:
                        scale(i - 1)
                seen.skip("pv_done", 2)
                out_projection(1, 1)

            dve.memset(ones[:, :], 1.0).then_inc(s["sum_step"], 2)
            dve.memset(warm[:, 0:1], 1.0).then_inc(s["act_ready"], 2)
            dve.memset(warm[:, 1:2], 1.0).then_inc(s["x_ready"], 2)
            dve.memset(warm[:, 2:3], 1.0).then_inc(s["out_added"], 2)
            dve.memset(warm[:, 3:4], 1.0).then_inc(s["proj_ready"], 2)
            dve.memset(warm[:, 5:6], 1.0).then_inc(s["lo_ready"], 2)
            sum_slots()
            split_both(0)
            dve.wait_ge(s["gains_loaded"], 16)
            for stack in range(2):
                for layer in range(LAYERS):
                    ffn(stack, layer, 0, 6 * layer if stack == 0 else None)
                    if stack == 0:
                        mixer1(layer)
                    elif layer == 0:
                        mixer2()
                    else:
                        mixer3()
                    ffn(stack, layer, 2, 6 * layer + 4 if stack == 0 else None, stack == 1 and layer == LAYERS - 1)
                if stack == 0:
                    mod_group(MOD_GROUPS - 1)
                    for l in range(LAYERS):
                        for i in range(3):
                            c = (l * 9 + 3 * i) * KC
                            dve.scalar_tensor_tensor(out=mod_gain[:, l, i, :], in0=mod[:, c + KC:c + 2 * KC], scalar=1.0,
                                                     in1=gains[:, G_NORM2 + 3 * l + i, :], op0=ALU.add, op1=ALU.mult)
                            last = dve.tensor_scalar(mod_gate[:, l, i, :], mod[:, c + 2 * KC:c + 3 * KC],
                                                     1.0 if i == 1 else 0.5, None, ALU.mult)
                    link(last)
                    final_norm(x, G_FINAL1)
                    sum_slots()
                else:
                    final_norm(h, G_FINAL2)


def constants():
    f = np.float32
    d = np.arange(P) % DH
    half = DH // 8
    freqs = f(500000.0) ** (-np.arange(half, dtype=f) * f(2.0) / f(DH // 4))
    ang = np.arange(S, dtype=f)[None, :] * freqs.astype(f)[d % half][:, None]
    turned = (d < 2 * half)[:, None]
    cos, sin = np.where(turned, np.cos(ang), f(1)).astype(f), np.where(turned, np.sin(ang), f(0)).astype(f)
    rot = np.zeros((P, P), f)
    for o in range(P):
        if o % DH < half:
            rot[o + half, o] = -1
        elif o % DH < 2 * half:
            rot[o - half, o] = 1
    pick = [np.zeros((P, P), f) for _ in range(2)]
    for g in range(2):
        for o in range(P):
            pick[g][g * DH + o % DH, o] = 1
    mats = np.stack([rot, pick[0], pick[1], pick[0] @ rot, pick[1] @ rot], axis=1)
    q = np.arange(TB)[None, :, None] * P + np.arange(P)[:, None, None]
    causal = np.where(np.arange(S)[None, None, :] <= q, f(0), f(NEG))
    seen = np.arange(16)[None, None, :] * CMP_STRIDE + CMP_LEN - 1 <= q
    col = np.arange(P) % GRID_W
    start = np.clip(col - WIN_W // 2, 0, GRID_W - WIN_W)[:, None]
    kc = np.arange(GRID_W)[None, :]
    inside = (kc >= start) & (kc < start + WIN_W)
    na = np.repeat(np.where(inside, f(0), f(NEG))[:, None, :], ROWS, axis=1)
    i, j = np.arange(P)[:, None], np.arange(P)[None, :]
    masks = [(i // n == j // n) for n in GLA_LEVELS[2:] + [1]]
    return {
        "ident": np.eye(P, dtype=f), "rope_cos": cos, "rope_sin": sin, "mats": mats.astype(f),
        "causal": causal.astype(f), "cmp_bias": np.where(seen, f(0), f(NEG)).astype(f),
        "cmp_keep": seen.astype(f), "na_mask": na.astype(f),
        "gla_mask": np.stack(masks, axis=1).astype(np.uint32).reshape(P, 7 * P),
    }


def units(w):
    n = w.shape[1] // P
    return w.reshape(KC, P, n // 2, 2, P).transpose(2, 1, 3, 0, 4)


def gate_up(wg, wu):
    pair = [w.reshape(KC, P, FC, P) for w in (wg, wu)]
    return np.stack(pair, axis=0).transpose(3, 2, 0, 1, 4)


def per_partition(v):
    v = v.reshape(v.shape[:-1] + (v.shape[-1] // P, P))
    return np.moveaxis(v, -1, 0)


def lay_out(i):
    a = dict(constants())
    f = np.float32
    a["x"] = i["x"][0].T.reshape(KC, P, S).transpose(1, 0, 2)
    slots = np.zeros((TOTAL_SLOTS, P, 2, KC, P), f)
    wd = np.empty((FFNS * KC * 2, P, HF, P), f)
    n = m = 0

    def put(block):
        nonlocal n
        slots[n:n + len(block)] = block
        n += len(block)

    def put_down(w):
        nonlocal m
        wd[m:m + 2 * KC] = w.reshape(2, HF, P, KC, P).transpose(3, 0, 2, 1, 4).reshape(2 * KC, P, HF, P)
        m += 2 * KC

    for l in range(LAYERS):
        put(gate_up(i["ffn1_wg"][l], i["ffn1_wu"][l]))
        put_down(i["ffn1_wd"][l])
        w = i["w_in"][l]
        q, k, v, gq, gk, gv, gr = (w[:, c:c + m_] for c, m_ in ((0, 512), (512, 512), (1024, 512), (1536, 256),
                                                              (1792, 256), (2048, 512), (2560, 512)))
        for part in (q, k, v, gq, gk, gr, gv, i["w_out"][l]):
            put(units(part))
        put(gate_up(i["ffn2_wg"][l], i["ffn2_wu"][l]))
        put_down(i["ffn2_wd"][l])
    for l in range(LAYERS):
        for j in range(2):
            w1 = i["ffn_w1_2"][l, j]
            put(gate_up(w1[:, :FF], w1[:, FF:]))
            put_down(i["ffn_w2_2"][l, j])
            if j:
                continue
            if l == 0:
                w = i["mix0_in_w_2"][0]
                xl, gl, q, k, v = (w[:, 512 * c:512 * c + 512] for c in range(5))
                for part in (q, k, v, xl, gl, i["mix0_out_w_2"][0]):
                    put(units(part))
            else:
                w = i["mix1_in_w_2"][0]
                kc, vc, ks, vs, kw, vw = (w[:, D + P * c:D + P * c + P] for c in range(6))
                put(units(w[:, :D]))
                for pair in ((ks, kw), (vs, vw), (kc, vc)):
                    put(units(np.concatenate(pair, axis=1)))
                gate = np.zeros((D, 2 * P), f)
                gate[:, :48] = w[:, D + 6 * P:]
                put(units(gate))
                for kv in range(2):
                    w1 = i["cmp_w1_2"][0, kv].reshape(CMP_PAIRS, P, P).transpose(1, 0, 2)
                    slots[n].reshape(P, CMP_PAIRS, P)[:] = w1
                    n += 1
                put(units(i["mix1_out_w_2"][0]))
    assert n == TOTAL_SLOTS and m == FFNS * KC * 2
    a["slots"], a["wd"] = slots.reshape(TOTAL_SLOTS, P, SLOT), wd.reshape(-1, P, HALF_SLOT)
    rpb = i["na_rpb"][:, :, WIN_H - ROWS:WIN_H + ROWS - 1]
    padded = np.zeros(rpb.shape[:3] + (2 * GRID_W - 1,), f)
    padded[..., GRID_W - WIN_W:GRID_W + WIN_W - 1] = rpb
    rows = np.stack([padded[..., GRID_W - 1 - c:2 * GRID_W - 1 - c] for c in range(GRID_W)], axis=3)
    bias = np.stack([rows[:, :, ROWS - 1 - r:2 * ROWS - 1 - r] for r in range(ROWS)], axis=1)
    bias = bias.reshape(LAYERS, TB, ROWS // TB, NA_HEADS, ROWS, GRID_W, GRID_W).transpose(0, 2, 5, 3, 1, 4, 6)
    a["na_bias"] = bias.reshape(LAYERS, P, NA_HEADS, TB * S)
    a["mod_w"] = i["mod_w_2"].reshape(LAYERS, KC, P, 9 * KC, P).transpose(0, 3, 2, 1, 4).reshape(MOD_CHUNKS, P, KC, P)
    a["mod_b"] = per_partition(i["mod_b_2"]).reshape(P, MOD_CHUNKS)
    a["cond"] = per_partition(i["c_2"][0])
    norms = [i[k][l] for l in range(LAYERS) for k in ("ffn1_norm", "mix_norm", "ffn2_norm")]
    norms += [i["final_norm"]] + [i["norm_g_2"][l, j] for l in range(LAYERS) for j in range(3)] + [i["final_norm_g_2"]]
    a["gains"] = per_partition(np.stack(norms))
    a["na_gain"] = per_partition(i["na_gain"])
    a["gla_gain"] = i["gla_gain"].T
    code = np.zeros((LAYERS, KC, P, CODE), f)
    wg = np.zeros((CODE, LAYERS, 256), f)
    for way, key in enumerate(("w_gate_f", "w_gate_b")):
        c = 3072 + GLA_RANK * way
        code[..., 32 * way:32 * way + GLA_RANK] = i["w_in"][:, :, c:c + GLA_RANK].reshape(LAYERS, KC, P, GLA_RANK)
        wg[32 * way:32 * way + GLA_RANK] = i[key].transpose(1, 0, 2)
    a["w_code"] = code.transpose(2, 0, 1, 3)
    a["w_gate"] = wg
    a["b_gate"] = np.concatenate([per_partition(i["b_gate_f"]), per_partition(i["b_gate_b"])], axis=2)

    def block_diagonal(w):
        full = np.zeros((2, DH, 4, 2, DH), f)
        for j in range(2):
            full[j, :, :, j] = w.reshape(4, 2, DH, DH)[:, j].transpose(1, 0, 2)
        return full.reshape(P, 4, P)

    a["lru_w"] = np.stack([block_diagonal(i["lru_wa_2"][0]), block_diagonal(i["lru_wx_2"][0])], axis=1)
    taps = i["lru_conv_w_2"][0].reshape(4, 4, P).transpose(2, 1, 0).reshape(P, 16)
    a["lru_p"] = np.concatenate([taps] + [per_partition(v.reshape(-1)) for v in (
        i["lru_conv_b_2"][0], i["lru_ba_2"][0], i["lru_bx_2"][0], i["lru_lambda_2"][0])], axis=1)
    a["cmp_pos"] = i["cmp_pos_2"][0].reshape(2, CMP_PAIRS, 2, DH).transpose(2, 3, 0, 1).reshape(P, 2, CMP_PAIRS)
    w2 = i["cmp_w2_2"][0]
    v2 = np.zeros((P, P), f)
    v2[:, :DH] = w2[1]
    a["cmp_w2"] = np.stack([np.concatenate([w2[0], w2[0]], axis=1), v2], axis=1)
    return {k: np.ascontiguousarray(v) for k, v in a.items()}


def kernel(**inputs):
    import concourse.bacc as _bacc
    from concourse.bass_utils import run_bass_kernel_spmd as _run

    arrays = lay_out({k: np.asarray(v) for k, v in inputs.items()})
    nc = _bacc.Bacc("TRN2", target_bir_lowering=False, num_devices=1)
    args = {k: nc.dram_tensor(f"in_{k}_dram", v.shape, mybir.dt.from_np(v.dtype), kind="ExternalInput").ap()
            for k, v in arrays.items()}
    out = nc.dram_tensor("out_0_dram", (P, KC, S), F32, kind="ExternalOutput").ap()
    build_program(nc, args, out)
    r = _run(nc, [{f"in_{k}_dram": v for k, v in arrays.items()}], core_ids=[0])
    got = r.results[0]["out_0_dram"]
    return got.transpose(1, 0, 2).reshape(1, D, S).transpose(0, 2, 1)
```

```python
from contextlib import ExitStack, contextmanager

import numpy as np

import concourse.bass as bass
from concourse import mybir

F32 = mybir.dt.float32
F32R = mybir.dt.float32r
U32 = mybir.dt.uint32
U8 = mybir.dt.uint8
ALU = mybir.AluOpType
ACT = mybir.ActivationFunctionType
AXX = mybir.AxisListType.X

P = 128
S = 256
TB = S // P
D = 1024
KC = D // P
FF = 2816
FC = FF // P
LAYERS = 2
FFNS = 2 * 2 * LAYERS
EPS = 1e-6
NEG = -1e30
RING = 2
SLOT = 2 * KC * P
HF = FC // 2
HALF_SLOT = HF * P

GRID_W, ROWS, WIN_H, WIN_W = 64, S // 64, 8, 16
NA_HEADS, DH = 8, 64
GLA_HEADS, GLA_TAU, GLA_RANK = 4, 16.0, 16
CODE = 32 + GLA_RANK
SCALE = DH ** -0.5
NSA_HEADS, NSA_GROUPS = 16, 2
CMP_LEN, CMP_STRIDE = 32, 16
NCMP = S // CMP_STRIDE - 1
CMP_PAIRS = CMP_LEN // 2

M1_SLOTS = 12
M2_SLOTS = 10
M3_SLOTS = 10
M2_PLACES = [6, 7, 0, 1, 2, 3, 8, 9, 4, 5]
M3_PLACES = [6, 4, 0, 1, 2, 3, None, None, 5, None]
OUT_SLOTS = D // (2 * P)
TOTAL_SLOTS = FFNS * FC + LAYERS * (M1_SLOTS + OUT_SLOTS) + M2_SLOTS + M3_SLOTS + 2 * OUT_SLOTS
GLA_LEVELS = [256, 128, 64, 32, 16, 8, 4, 2]
MOD_CHUNKS = LAYERS * 9 * KC
MOD_GROUPS = 3 * LAYERS
MOD_GROUP = MOD_CHUNKS // MOD_GROUPS

G_FINAL1, G_NORM2, G_FINAL2 = 3 * LAYERS, 3 * LAYERS + 1, 6 * LAYERS + 1
N_GAINS = 6 * LAYERS + 2


class Seen:

    def __init__(self, **start):
        self.n = dict(start)
        self.turns = []

    def __call__(self, name, more=1):
        self.n[name] = self.n.get(name, 0) + more
        return self.value(name)

    def value(self, name, ahead=0):
        v = self.n.get(name, 0) + ahead
        for turn, per in self.turns:
            if per.get(name, 0):
                v = turn * per[name] + v
        return v

    def skip(self, name, more):
        self.n[name] = self.n.get(name, 0) + more


@contextmanager
def loop(eng, seen, count, **per):
    with eng.Fori(0, count) as turn:
        start = dict(seen.n)
        seen.turns.append((turn, per))
        yield turn
        seen.turns.pop()
        for name in set(seen.n) | set(per):
            took = seen.n.get(name, 0) - start.get(name, 0)
            assert took == per.get(name, 0), (name, took, per.get(name, 0))
    for name, k in per.items():
        seen.n[name] = start.get(name, 0) + count * k


def build_program(nc, a, out):
    ctx = ExitStack()
    with ctx:
        def sb(name, shape, dt=F32):
            return ctx.enter_context(nc.sbuf_tensor(name, shape, dt))

        sems = {}

        def sem(name):
            sems[name] = ctx.enter_context(nc.semaphore(name))
            return sems[name]

        slot = [sb(f"slot{i}", [P, SLOT]) for i in range(RING)]
        slot_hi = [sb(f"slot_hi{i}", [P, SLOT], F32R) for i in range(RING)]
        slot_lo = [sb(f"slot_lo{i}", [P, SLOT], F32R) for i in range(RING)]
        mod_raw = [sb(f"mod_raw{i}", [P, KC, P]) for i in range(2)]
        mod_acc = sb("mod_acc", [P, MOD_GROUP, P])
        x = sb("x", [P, KC, S])
        h = sb("h", [P, KC, S])
        h_hi = sb("h_hi", [P, KC, S], F32R)
        h_lo = sb("h_lo", [P, KC, S], F32R)
        sq = sb("sq", [P, 2, 512])
        sqsum = sb("sqsum", [P, S])
        rstd = sb("rstd", [P, S])
        warm = sb("warm", [P, 8])
        ident = sb("ident", [P, P])
        ones = sb("ones", [P, S])
        rope_cos = sb("rope_cos", [P, S])
        rope_sin = sb("rope_sin", [P, S])
        mats = sb("mats", [P, 5, P])
        causal = sb("causal", [P, TB, S])
        na_mask = sb("na_mask", [P, ROWS, GRID_W])
        cmp_bias = sb("cmp_bias", [P, TB, 16])
        cmp_keep = sb("cmp_keep", [P, TB, 16])
        gla_mask = sb("gla_mask", [P, 7, P], U8)
        gains = sb("gains", [P, N_GAINS, KC])
        na_gain = sb("na_gain", [P, LAYERS, 4])
        gla_gain = sb("gla_gain", [P, LAYERS])
        w_code = sb("w_code", [P, LAYERS, KC, CODE])
        w_gate = sb("w_gate", [CODE, LAYERS, 256])
        b_gate = sb("b_gate", [P, LAYERS, 4])
        cond = sb("cond", [P, KC])
        mod_b = sb("mod_b", [P, MOD_CHUNKS])
        mod = sb("mod", [P, MOD_CHUNKS])
        mod_gain = sb("mod_gain", [P, LAYERS, 3, KC])
        mod_gate = sb("mod_gate", [P, LAYERS, 3, KC])
        lru_w = sb("lru_w", [P, 2, 4, P])
        lru_p = sb("lru_p", [P, 32])
        lru_c = sb("lru_c", [P, 48])
        cmp_pos = sb("cmp_pos", [P, 2, CMP_PAIRS])
        cmp_w2 = sb("cmp_w2", [P, 2, P])
        with nc.sbuf_tensor("act_hi", [P, FC, S], F32R) as act_hi, nc.sbuf_tensor("act_lo", [P, FC, S], F32R) as act_lo:
            pass
        ROOM = 19008
        room = sb("room", [P, ROOM])

        def carve(at, *shape):
            n = int(np.prod(shape))
            assert at[0] + n <= ROOM, (at[0], n)
            v = room[:, at[0]:at[0] + n]
            at[0] += n
            if len(shape) == 2:
                v = v.rearrange("p (a b) -> p a b", a=shape[0])
            elif len(shape) == 3:
                v = v.rearrange("p (a b c) -> p a b c", a=shape[0], b=shape[1])
            return v

        at = [2 * FC * S]
        sil = carve(at, 2, S)
        act_f = carve(at, 2, S)
        at = [0]
        proj = carve(at, 12, 512)
        att_t = carve(at, 2, 800)
        att_pt = carve(at, 2, 1024)
        mixer_room = at[0]
        wide_mask = proj[:, 0:2, :].rearrange("p a b -> p (a b)")[:, 0:7 * P].bitcast(U32)
        mix = h
        at = [mixer_room]
        gb = carve(at, 2, 512)
        ge = carve(at, 2, 1024)
        ga = carve(at, GLA_HEADS, 4, P)
        na_bias = carve(at, NA_HEADS, 512)
        gla_rstd = ge[:, 0, :]
        at = [mixer_room]
        xc = carve(at, 4, S)
        lr = carve(at, 4, S)
        li = carve(at, 4, S)
        la = carve(at, 4, S)
        lb = carve(at, 4, S)
        lg = carve(at, 4, S)
        at = [mixer_room]
        nsa_t = carve(at, 3, 800)
        k_rope = carve(at, NSA_GROUPS, 512)
        rope_tmp = carve(at, 512)
        cmp_g = carve(at, 2, CMP_PAIRS, 2 * NCMP)
        cmp_h = carve(at, 2, 32)
        k_cmp = carve(at, 32)
        v_cmp = carve(at, 2, DH)
        gates = carve(at, TB, 48)
        q_rope = carve(at, 4, 512)
        assert FC * S + 2 * S == 12 * 512 and FC * S + 10 * S <= mixer_room
        cmp_parts = act_lo[:, 2:10, :].rearrange("p a b -> p (a b)")[:, 0:4 * CMP_PAIRS * 2 * NCMP].rearrange(
            "p (v c s n) -> p v c s n", v=2, c=CMP_PAIRS, s=2)
        cmp_hi, cmp_lo = cmp_parts[:, :, :, 0, :], cmp_parts[:, :, :, 1, :]
        stats = sb("stats", [P, 2, 32])
        code = sb("code", [CODE, S])

        bank = [ctx.enter_context(nc.psum_tensor(f"bank{i}", [P, 512], F32)) for i in range(8)]

        for name in (
            "const_ready", "x_loaded", "cond_loaded", "gains_loaded", "mask_loaded", "bias_ready", "out_stored",
            "slot0_ready", "slot1_ready", "mod0_ready", "mod1_ready",
            "slot_done", "ss_done", "mod_done", "score_done", "pt_done", "pv_done",
            "code_done", "logit_done", "level_done", "gla_o_done", "rot_done", "lru_gate_done",
            "cmp_dup_done", "cmp_done",
            "act_step", "hi_ready", "h_hi_ready", "mix_hi_ready", "sil_ready", "proj_ready", "sq_ready", "rstd_ready", "cond_ready", "exp_ready",
            "pt_copied", "o_copied", "decay_ready", "code_ready", "logit_read", "forget_ready", "na_sq_ready",
            "gla_sq_ready", "gla_rstd_ready", "lru_gate_ready", "lru_exp_ready", "lru_decay_ready", "lru_mult_ready",
            "gelu_ready", "cmp_hi_ready", "cmp_ready", "gates_ready",
            "dve_step", "lo_ready", "h_raw", "mix_raw", "mix_split", "o_split", "act_ready", "x_ready", "out_added", "sum_step", "h_ready", "score_read",
            "max_ready", "recip_ready", "probs_ready", "pt_half_copied", "diff_ready", "qk_ready", "level_read", "mix_ready",
            "final_ready", "rot_read", "conv_step", "blocks_raw", "cmp_summed", "blocks_ready", "rope_ready", "lru_sq_ready", "lru_const_ready", "lru_scanned",
            "mod_step", "bias_masked", "lru_in_ready",
        ):
            sem(name)
        s = sems
        SLOT_READY = ["slot0_ready", "slot1_ready"]
        MOD_READY = ["mod0_ready", "mod1_ready"]
        CONST_LOADS = 18
        WARM = 16
        WARM_MOD = 7
        WARM_START = 9
        BIAS_PARTS = 4
        att3 = att_t[:, :, :].rearrange("p a b -> p (a b)")[:, 0:3 * 512].rearrange("p (a b) -> p a b", a=3)
        na_sq = att_t[:, :, :].rearrange("p a b -> p (a b)")[:, 0:1024]
        lru_bank = [bank[6], bank[7], bank[2], bank[3]]
        block = ctx.enter_context(nc.Block())

        @block.sync
        def _(sp):
            seen = Seen()

            def load_slots(first, count):
                with loop(sp, seen, count // RING, lo_ready=RING) as t:
                    for b in range(RING):
                        sp.wait_ge(s["lo_ready"], seen("lo_ready"))
                        sp.dma_start(slot[b][:, :], a["slots"][bass.ds(t * RING + (first + b), 1), :, :]
                                     .rearrange("o p n -> (o p) n")).then_inc(s[SLOT_READY[b]], 16)
                return first + count

            def load_down_slots(ffn, first, count):
                with loop(sp, seen, count, lo_ready=RING) as t:
                    for b in range(RING):
                        sp.wait_ge(s["lo_ready"], seen("lo_ready"))
                        sp.dma_start(slot[b][:, 0:HALF_SLOT], a["wd"][bass.ds(t * RING + ((ffn * KC + first) * RING + b), 1), :, :]
                                     .rearrange("o p n -> (o p) n")).then_inc(s[SLOT_READY[b]], 16)

            def load_constants(*which):
                for dst, name in which:
                    sp.dma_start(dst, a[name]).then_inc(s["const_ready"], 16)

            def load_bias(layer, part):
                heads = NA_HEADS // BIAS_PARTS
                sp.dma_start(na_bias[:, part * heads:part * heads + heads, :],
                             a["na_bias"][layer, :, part * heads:part * heads + heads, :]).then_inc(s["bias_ready"], 16)

            sp.dma_start(x[:, :, :], a["x"]).then_inc(s["x_loaded"], 16)
            sp.dma_start(cond[:, :], a["cond"]).then_inc(s["cond_loaded"], 16)
            sp.dma_start(gains[:, :, :], a["gains"]).then_inc(s["gains_loaded"], 16)
            n = load_slots(0, RING)
            sp.dma_start(wide_mask, a["gla_mask"]).then_inc(s["mask_loaded"], 16)
            n = load_slots(n, 4)
            load_constants((mod_b[:, :], "mod_b"), (ident[:, :], "ident"), (na_mask[:, :, :], "na_mask"),
                           (na_gain[:, :, :], "na_gain"), (gla_gain[:, :], "gla_gain"), (w_gate[:, :, :], "w_gate"),
                           (b_gate[:, :, :], "b_gate"))
            n = load_slots(n, 4)
            load_constants((w_code[:, :, :, :], "w_code"), (rope_cos[:, :], "rope_cos"), (rope_sin[:, :], "rope_sin"),
                           (lru_p[:, :], "lru_p"))
            n = load_slots(n, 4)
            load_constants((mats[:, :, :], "mats"), (causal[:, :, :], "causal"), (cmp_bias[:, :, :], "cmp_bias"),
                           (cmp_keep[:, :, :], "cmp_keep"))
            n = load_slots(n, 4)
            load_constants((lru_w[:, :, :, :], "lru_w"), (cmp_pos[:, :, :], "cmp_pos"), (cmp_w2[:, :, :], "cmp_w2"))
            first = n
            ffn = 0
            for stack in range(2):
                for layer in range(LAYERS):
                    n = load_slots(n, FC - first)
                    first = 0
                    for part in range(BIAS_PARTS):
                        load_down_slots(ffn, part * KC // BIAS_PARTS, KC // BIAS_PARTS)
                        if stack == 0:
                            load_bias(layer, part)
                    ffn += 1
                    mixer = M1_SLOTS if stack == 0 else M2_SLOTS if layer == 0 else M3_SLOTS
                    n = load_slots(n, mixer + OUT_SLOTS)
                    n = load_slots(n, FC)
                    load_down_slots(ffn, 0, KC)
                    ffn += 1
            assert n == TOTAL_SLOTS and ffn == FFNS
            for k in range(0, KC, 2):
                sp.wait_ge(s["final_ready"], KC + k + 2)
                sp.dma_start(out[:, k:k + 2, :], h[:, k:k + 2, :]).then_inc(s["out_stored"], 16)
            sp.wait_ge(s["out_stored"], 16 * KC // 2)

        @block.gpsimd
        def _(pool):
            seen = Seen()

            def link(ins):
                ins.then_inc(s["mod_step"], 1)
                pool.wait_ge(s["mod_step"], seen("mod_step"))

            def load_mod(n, b):
                pool.dma_start(mod_raw[b][:, :, :], a["mod_w"][bass.ds(n, 1), :, :, :].rearrange("o p k n -> (o p) k n")
                               ).then_inc(s[MOD_READY[b]], 16)

            def mod_chunk(c, b):
                w = mod_raw[b]
                pool.wait_ge(s[MOD_READY[b]], seen(MOD_READY[b], 16))
                link(pool.tensor_tensor(w[:, :, :], w[:, :, :], cond[:, :].unsqueeze(2).to_broadcast([P, KC, P]), ALU.mult))
                link(pool.tensor_tensor(w[:, 0:4, :], w[:, 0:4, :], w[:, 4:8, :], ALU.add))
                link(pool.tensor_tensor(w[:, 0:2, :], w[:, 0:2, :], w[:, 2:4, :], ALU.add))
                link(pool.tensor_tensor(mod_acc[:, bass.ds(c, 1), :], w[:, 0:1, :], w[:, 1:2, :], ALU.add))

            load_mod(0, 0)
            load_mod(1, 1)
            pool.wait_ge(s["cond_ready"], seen("cond_ready"))
            for g in range(MOD_GROUPS):
                if g:
                    pool.wait_ge(s["mod_done"], seen("mod_done"))
                tail = int(g == MOD_GROUPS - 1)
                with loop(pool, seen, MOD_GROUP // 2 - tail, mod0_ready=16, mod1_ready=16, mod_step=8) as t:
                    for b in range(2):
                        mod_chunk(t * 2 + b, b)
                        load_mod(t * 2 + (g * MOD_GROUP + 2 + b), b)
                if tail:
                    mod_chunk(MOD_GROUP - 2, 0)
                    mod_chunk(MOD_GROUP - 1, 1)
                if g % 3 == 0:
                    pool.wait_ge(s["const_ready"], 16 * CONST_LOADS)
                    pool.wait_ge(s["bias_ready"], seen("bias_ready", 16 * BIAS_PARTS))
                    for head in range(NA_HEADS):
                        for qt in range(TB):
                            v = na_bias[:, head, qt * S:qt * S + S]
                            pool.tensor_tensor(v, v, na_mask[:, :, :].rearrange("p a b -> p (a b)"),
                                               ALU.add).then_inc(s["bias_masked"], 1)
            flat = lambda v: v[:, :, :].rearrange("p a b -> p (a b)")
            pool.wait_ge(s["lru_gate_ready"], seen("lru_gate_ready", 4))
            pool.tensor_tensor(flat(li), flat(li), flat(xc), ALU.mult).then_inc(s["lru_in_ready"], 1)
            pool.wait_ge(s["lru_scanned"], seen("lru_scanned"))
            pool.wait_ge(s["gelu_ready"], seen("gelu_ready"))
            pool.tensor_tensor(mix[:, 0:4, :].rearrange("p a b -> p (a b)"), flat(xc),
                               proj[:, 8:10, :].rearrange("p a b -> p (a b)"), ALU.mult).then_inc(s["mix_raw"], 1)

        @block.tensor
        def _(pe):
            seen = Seen(sum_step=2, lo_ready=2)

            def three(o, w, x_hi, x_lo, b, first, last, skip=False):
                pe.matmul(o, slot_hi[b][:, w:w + P], x_hi, start=first, stop=False, skip_group_check=skip)
                pe.matmul(o, slot_hi[b][:, w:w + P], x_lo, start=False, stop=False, skip_group_check=skip)
                return pe.matmul(o, slot_lo[b][:, w:w + P], x_hi, start=False, stop=last, skip_group_check=skip)

            def slot_products(b, target, fresh=None):
                pe.wait_ge(s["lo_ready"], seen("lo_ready"))
                order = [(u, k) for k in range(KC) for u in range(2)] if fresh else [(u, k) for u in range(2) for k in range(KC)]
                for u, k in order:
                    if fresh and u == 0:
                        pe.wait_ge(s[fresh], seen(fresh))
                    last = three(target[:, u * S:u * S + S], (u * KC + k) * P, h_hi[:, k, :], h_lo[:, k, :], b,
                                 k == 0 and not (fresh and u), k == KC - 1, bool(fresh))
                last.then_inc(s["slot_done"], 1)

            def slot_products_by_token(b, target, units=2, cols=P):
                pe.wait_ge(s["lo_ready"], seen("lo_ready"))
                hi, lo = (w[b][:, :].rearrange("p (u k n) -> p u k n", u=2, k=KC) for w in (slot_hi, slot_lo))
                for tb in range(TB):
                    o = target[:, tb * S:tb * S + units * cols]
                    if units == 2:
                        o = o.rearrange("p (u n) -> p u n", u=2)
                    for k in range(KC):
                        w_hi, w_lo = (w[:, :, k, 0:cols] if units == 2 else w[:, 0, k, 0:cols] for w in (hi, lo))
                        t_hi, t_lo = (v[:, k, tb * P:tb * P + P] for v in (h_hi, h_lo))
                        pe.matmul(o, t_hi, w_hi, start=(k == 0), stop=False)
                        pe.matmul(o, t_hi, w_lo, start=False, stop=False)
                        last = pe.matmul(o, t_lo, w_hi, start=False, stop=(k == KC - 1))
                last.then_inc(s["slot_done"], 1)

            def norm_sum(batches):
                pe.wait_ge(s["sum_step"], seen("sum_step", batches - 1))
                pe.matmul(bank[4][:, 0:S], ones[:, 0:P], sqsum[:, :], start=True, stop=False)
                pe.wait_ge(s["sq_ready"], seen("sq_ready", batches))
                halves = KC // batches
                for j in range(halves):
                    last = pe.matmul(bank[4][:, 0:S], ones[:, 0:P], sq[:, 1, j * S:j * S + S], start=False, stop=(j == halves - 1))
                last.then_inc(s["ss_done"], 1)

            def keep_warm(count):
                for _ in range(count):
                    pe.matmul(bank[7][:, :], slot_hi[0][:, 0:P], slot_hi[0][:, 0:512], start=True, stop=True)

            def mod_sums(half):
                n = MOD_GROUP // 2
                pe.wait_ge(s["mod_step"], seen("mod_step", 4 * n))
                for c in range(half * n, half * n + n):
                    last = pe.matmul(bank[5][:, c:c + 1], mod_acc[:, c, :], ones[:, 0:1], start=True, stop=True)
                if half:
                    last.then_inc(s["mod_done"], 1)
                    keep_warm(WARM_MOD)

            def ffn(modulation, warm_after=True):
                for b in range(RING):
                    pe.wait_ge(s["act_ready"], seen("act_ready"))
                    slot_products(b, bank[b], None if b else "h_ready")
                with loop(pe, seen, FC // 2 - 1, lo_ready=2, act_ready=2):
                    for b in range(RING):
                        pe.wait_ge(s["act_ready"], seen("act_ready"))
                        slot_products(b, bank[b])
                if modulation:
                    mod_sums(0)
                all_hidden = seen.value("act_ready", 2)
                with loop(pe, seen, KC // 2, lo_ready=4, x_ready=2):
                    for j in range(2):
                        pe.wait_ge(s["x_ready"], seen("x_ready"))
                        for b in range(RING):
                            pe.wait_ge(s["lo_ready"], seen("lo_ready"))
                            if j == 0 and b == 1:
                                pe.wait_ge(s["act_ready"], all_hidden)
                            for f in range(HF):
                                c = b * HF + f
                                last = three(bank[2 + j][:, 0:S], f * P, act_hi[:, c, :], act_lo[:, c, :], b,
                                             c == 0, c == FC - 1)
                            last.then_inc(s["slot_done"], 1)
                norm_sum(KC)
                if modulation:
                    mod_sums(1)
                elif warm_after:
                    keep_warm(WARM)

            def project(n, kind):
                pe.wait_ge(s["proj_ready"], seen("proj_ready"))
                if kind == "f":
                    slot_products(n % 2, bank[n % 2], None if n else "h_ready")
                elif kind == "t":
                    slot_products_by_token(n % 2, bank[n % 2])
                else:
                    slot_products_by_token(n % 2, bank[n % 2], units=1, cols=48)

            def turn_chunks(places):
                for b, i in enumerate(places):
                    pe.matmul(bank[4 + b][:, :], mats[:, 0, :], proj[:, i, :], start=True, stop=True
                              ).then_inc(s["rot_done"], 1)

            def out_projection(fresh="mix_split"):
                for n in range(OUT_SLOTS):
                    pe.wait_ge(s["out_added"], seen("out_added"))
                    slot_products(n % 2, bank[2 + n % 2], None if n else fresh)
                norm_sum(OUT_SLOTS)

            def attention(q, k, v, heads, freed, last_slot, beside=None):
                def scores(i):
                    if i >= 2:
                        pe.wait_ge(s["score_read"], seen("score_read"))
                    p0 = DH * (i % 2)
                    for qt in range(TB):
                        last = pe.matmul(bank[2 + i % 2][:, qt * S:qt * S + S], q(i)[p0:p0 + DH, qt * P:qt * P + P],
                                         k(i)[p0:p0 + DH, :], start=True, stop=True)
                    last.then_inc(s["score_done"], 1)

                def transposes(i):
                    pe.wait_ge(s["probs_ready"], seen("probs_ready"))
                    for kb in range(TB):
                        for qt in range(TB):
                            last = pe.transpose(bank[4 + i % 2][:, kb * S + qt * P:kb * S + qt * P + P],
                                                att3[:, i % 3, qt * S + kb * P:qt * S + kb * P + P], ident[:, :])
                    last.then_inc(s["pt_done"], 1)

                def values(i):
                    pe.wait_ge(s["pt_copied"], seen("pt_copied"))
                    if i >= 4 and i % 2 == 0:
                        pe.wait_ge(s[freed], seen(freed))
                    p0 = DH * (i % 2)
                    for kb in range(TB):
                        last = pe.matmul(bank[6 + i // 2 % 2][p0:p0 + DH, 0:S], v(i, kb),
                                         att_pt[:, i % 2, kb * S:kb * S + S], start=(kb == 0), stop=(kb == TB - 1))
                    last.then_inc(s["pv_done"], 1)

                last_slot()
                scores(0)
                for i in range(heads + 2):
                    if i + 1 < heads:
                        scores(i + 1)
                    if i >= 2:
                        values(i - 2)
                    if 1 <= i <= heads:
                        transposes(i - 1)
                    if beside:
                        beside(i)
                seen.skip("score_read", 2)
                seen.skip(freed, 2)

            def mixer1(layer):
                for n, kind in enumerate("ffff" "tt" "ffff" "t"):
                    project(n, kind)
                    if n == 1:
                        pe.wait_ge(s["const_ready"], 16 * CONST_LOADS)
                        for k in range(KC):
                            last = pe.matmul(bank[4][0:CODE, 0:S], w_code[:, layer, k, :], h[:, k, :],
                                             start=(k == 0), stop=(k == KC - 1))
                        last.then_inc(s["code_done"], 1)
                    elif n == 3:
                        pe.wait_ge(s["code_ready"], seen("code_ready"))
                        for way in range(2):
                            for pair in range(2):
                                last = pe.matmul(bank[6 + way][:, pair * S:pair * S + S],
                                                 w_gate[32 * way:32 * way + GLA_RANK, layer, pair * P:pair * P + P],
                                                 code[32 * way:32 * way + GLA_RANK, :], start=True, stop=True)
                        last.then_inc(s["logit_done"], 1)
                def last_slot():
                    project(11, "t")
                    pe.wait_ge(s["proj_ready"], seen.value("proj_ready", 2))
                    pe.wait_ge(s["logit_read"], seen("logit_read"))

                def level(i):
                    if i > len(GLA_LEVELS):
                        return
                    n = (GLA_LEVELS + [1])[i]
                    if n > 1:
                        pe.wait_ge(s["qk_ready"], seen("qk_ready"))
                    if i >= 1:
                        pe.wait_ge(s["level_read"], seen("level_read"))
                    qk = ge[:, i % 2, :] if n > 1 else proj[:, 6:8, :].rearrange("p a b -> p (a b)")
                    for sblk in range(TB):
                        tblk = 1 - sblk if n == S else sblk
                        for head in range(GLA_HEADS):
                            p0, c = DH * (head % 2), (head // 2) * S
                            o = (head // 2 * TB + sblk) * P
                            last = pe.matmul(bank[head % 2][:, o:o + P],
                                             qk[p0:p0 + DH, 512 + c + sblk * P:512 + c + sblk * P + P],
                                             qk[p0:p0 + DH, c + tblk * P:c + tblk * P + P], start=True, stop=True)
                    last.then_inc(s["level_done"], 1)

                attention(lambda i: proj[:, i // 4, (i // 2 % 2) * S:(i // 2 % 2) * S + S],
                          lambda i: proj[:, 2 + i // 4, (i // 2 % 2) * S:(i // 2 % 2) * S + S],
                          lambda i, kb: proj[:, 4 + i // 4, kb * S + (i % 4) * DH:kb * S + (i % 4) * DH + DH],
                          NA_HEADS, "o_copied", last_slot, level)
                mod_sums(0)
                pe.wait_ge(s["na_sq_ready"], seen("na_sq_ready"))
                for c in range(4):
                    last = pe.matmul(bank[4][:, 0:S], ones[:, 0:P], na_sq[:, c * S:c * S + S], start=(c == 0), stop=(c == 3))
                last.then_inc(s["ss_done"], 1)
                pe.wait_ge(s["level_read"], seen("level_read"))
                for head in range(GLA_HEADS):
                    for sblk in range(TB):
                        v0 = sblk * S + (head % 2) * P
                        last = pe.matmul(bank[6 + head // 2][:, (head % 2) * S:(head % 2) * S + S],
                                         proj[:, 10 + head // 2, v0:v0 + P], ga[:, head, 2 * sblk:2 * sblk + 2, :].rearrange("p a b -> p (a b)"),
                                         start=(sblk == 0), stop=(sblk == TB - 1))
                last.then_inc(s["gla_o_done"], 1)
                for half in range(2):
                    pe.wait_ge(s["gla_sq_ready"], seen("gla_sq_ready"))
                    pe.matmul(bank[half][:, :], ones[:, 0:P], sq[:, half, :], start=True, stop=True).then_inc(s["ss_done"], 1)
                out_projection()
                mod_sums(1)

            def mixer2():
                for n in range(5):
                    project(n, "f")
                pe.wait_ge(s["conv_step"], seen("conv_step", 4))
                for c in range(4):
                    for gate in range(2):
                        last = pe.matmul(lru_bank[c][:, gate * S:gate * S + S], lru_w[:, gate, c, :],
                                         xc[:, c, :], start=True, stop=True)
                    last.then_inc(s["lru_gate_done"], 1)
                project(5, "f")
                turn_chunks((0, 1))
                project(6, "f")
                project(7, "f")
                pe.wait_ge(s["rot_read"], seen("rot_read", 2))
                turn_chunks((2, 3))
                project(8, "t")
                seen.skip("rot_read", 2)

                def last_slot():
                    project(9, "t")
                    pe.wait_ge(s["lru_gate_ready"], seen("lru_gate_ready", 4))
                    pe.wait_ge(s["proj_ready"], seen.value("proj_ready", 2))
                    pe.wait_ge(s["rope_ready"], seen("rope_ready", 4))

                attention(lambda i: proj[:, i // 4, (i // 2 % 2) * S:(i // 2 % 2) * S + S],
                          lambda i: proj[:, 2 + i // 4, (i // 2 % 2) * S:(i // 2 % 2) * S + S],
                          lambda i, kb: proj[:, 4 + i // 4, kb * S + (i % 4) * DH:kb * S + (i % 4) * DH + DH],
                          NA_HEADS, "o_split", last_slot)
                pe.wait_ge(s["mix_split"], seen("mix_split", 4))
                pe.wait_ge(s["o_split"], seen.value("o_split"))
                out_projection(None)
                keep_warm(WARM)

            def compress(kv):
                pe.wait_ge(s["proj_ready"], seen("proj_ready"))
                pe.wait_ge(s["lo_ready"], seen("lo_ready"))
                if kv == 0:
                    pe.wait_ge(s["blocks_ready"], seen("blocks_ready"))
                n = 2 * NCMP
                for c in range(CMP_PAIRS):
                    def wide(stop):
                        return pe.matmul(bank[kv][:, 0:2 * n], slot_hi[kv][:, c * P:c * P + P],
                                         cmp_parts[:, kv, c, :, :].rearrange("p s n -> p (s n)"), start=(c == 0), stop=stop)
                    if c < CMP_PAIRS - 1:
                        wide(False)
                    pe.matmul(bank[kv][:, 0:n], slot_lo[kv][:, c * P:c * P + P], cmp_hi[:, kv, c, :], start=False, stop=False)
                    if c == CMP_PAIRS - 1:
                        wide(True).then_inc(s["slot_done"], 1)

            def mixer3():
                project(0, "f")
                project(1, "f")
                project(2, "f")
                for g in range(NSA_GROUPS):
                    pe.matmul(bank[2 + g][:, :], mats[:, 1 + g, :], proj[:, 6, :], start=True, stop=True
                              ).then_inc(s["cmp_dup_done"], 1)
                project(3, "f")
                for g in range(NSA_GROUPS):
                    pe.matmul(bank[4 + 2 * g][:, :], mats[:, 1 + g, :], proj[:, 4, :], start=True, stop=True)
                    pe.matmul(bank[5 + 2 * g][:, :], mats[:, 3 + g, :], proj[:, 4, :], start=True, stop=True
                              ).then_inc(s["rot_done"], 1)
                project(4, "f")
                project(5, "f")
                pe.wait_ge(s["rot_read"], seen("rot_read", 2))
                turn_chunks((0, 1))
                compress(0)
                compress(1)
                pe.wait_ge(s["rot_read"], seen("rot_read", 2))
                turn_chunks((2, 3))
                seen.skip("rot_read", 2)
                project(8, "t")
                pe.wait_ge(s["proj_ready"], seen.value("proj_ready", 1))
                pe.matmul(bank[2][:, 0:2 * NCMP], cmp_w2[:, 0, :], cmp_h[:, 0, 0:2 * NCMP], start=True, stop=True)
                for g in range(NSA_GROUPS):
                    last = pe.matmul(bank[3][0:NCMP, g * DH:g * DH + DH], cmp_h[:, 1, g * NCMP:g * NCMP + NCMP],
                                     cmp_w2[:, 1, 0:DH], start=True, stop=True)
                last.then_inc(s["cmp_done"], 1)
                pe.wait_ge(s["cmp_summed"], seen("cmp_summed", 2))

                def last_slot():
                    project(9, "g")
                    pe.wait_ge(s["proj_ready"], seen.value("proj_ready", 2))
                    pe.wait_ge(s["cmp_ready"], seen("cmp_ready"))
                    pe.wait_ge(s["rope_ready"], seen("rope_ready", NSA_GROUPS))

                heads = NSA_HEADS

                def scores(i):
                    if i >= 2:
                        pe.wait_ge(s["score_read"], seen("score_read"))
                    if i % 4 == 0:
                        pe.wait_ge(s["rope_ready"], seen("rope_ready"))
                    p0, g = DH * (i % 2), i // (NSA_HEADS // NSA_GROUPS)
                    c0 = (i // 2 % 2) * S
                    q = q_rope[p0:p0 + DH, i // 4, c0:c0 + S]
                    qn = proj[p0:p0 + DH, i // 4, c0:c0 + S]
                    kk = k_rope[p0:p0 + DH, g, :].rearrange("p (b t) -> p b t", b=2)
                    big, small = bank[i % 2], bank[2 + i % 2]
                    pe.matmul(big[:, :], q[:, P:S], kk[:, :, :], start=True, stop=True)
                    pe.matmul(small[:, 0:S].rearrange("p (b t) -> p b t", b=2), q[:, 0:P], kk[:, :, 0:P], start=True, stop=True)
                    for qt in range(TB):
                        last = pe.matmul(small[:, S + 16 * qt:S + 16 * qt + NCMP], qn[:, qt * P:qt * P + P],
                                         k_cmp[p0:p0 + DH, g * NCMP:g * NCMP + NCMP], start=True, stop=True)
                    last.then_inc(s["score_done"], 1)

                def transposes(i):
                    pe.wait_ge(s["probs_ready"], seen("probs_ready"))
                    e = nsa_t[:, i % 3, :]
                    X, Y = bank[4], bank[5]
                    for br in range(2):
                        pe.transpose(X[:, br * S:br * S + P], e[:, 16 + br * P:16 + br * P + P], ident[:, :])
                        q1 = 16 + S + 16 + br * S
                        pe.transpose(X[:, br * S + P:br * S + S], e[:, q1:q1 + P], ident[:, :])
                        pe.transpose(Y[:, br * P:br * P + P], e[:, q1 + P:q1 + S], ident[:, :])
                    for qt in range(TB):
                        c0 = qt * (16 + S)
                        last = pe.transpose(Y[0:NCMP, S + qt * P:S + qt * P + P], e[:, c0:c0 + NCMP], ident[:, :])
                    last.then_inc(s["pt_done"], 1)

                def values(i):
                    pe.wait_ge(s["pt_copied"], seen("pt_copied"))
                    pe.wait_ge(s["pt_half_copied"], seen("pt_half_copied"))
                    if i >= 4 and i % 2 == 0:
                        pe.wait_ge(s["o_split"], seen("o_split"))
                    p0, g = DH * (i % 2), i // (NSA_HEADS // NSA_GROUPS)
                    o = bank[6 + i // 2 % 2][p0:p0 + DH, 0:S]
                    pt = att_pt[:, i % 2, :]

                    def v(br, kb):
                        return proj[:, 5, kb * S + br * P + g * DH:kb * S + br * P + g * DH + DH]

                    pe.matmul(o, v(0, 0), pt[:, 0:S], start=True, stop=False)
                    pe.matmul(o[:, P:S], v(0, 1), pt[:, 512:640], start=False, stop=False, skip_group_check=True)
                    pe.matmul(o[:, P:S], v(1, 1), pt[:, 640:768], start=False, stop=False, skip_group_check=True)
                    pe.matmul(o, v_cmp[0:NCMP, g, :], pt[0:NCMP, 768:1024], start=False, stop=False, skip_group_check=True)
                    pe.matmul(o, v(1, 0), pt[:, S:2 * S], start=False, stop=True).then_inc(s["pv_done"], 1)

                last_slot()
                scores(0)
                for i in range(heads + 2):
                    if i + 1 < heads:
                        scores(i + 1)
                    if i >= 2:
                        values(i - 2)
                    if 1 <= i <= heads:
                        transposes(i - 1)
                seen.skip("score_read", 2)
                seen.skip("o_split", 2)
                pe.wait_ge(s["o_split"], seen.value("o_split"))
                out_projection(None)
                keep_warm(WARM)

            pe.wait_ge(s["sum_step"], 2)
            for _ in range(WARM_START):
                pe.matmul(bank[5][:, 0:S], ones[:, 0:P], ones[:, :], start=True, stop=True)
            norm_sum(OUT_SLOTS)
            for _ in range(WARM // 2):
                pe.matmul(bank[5][:, 0:S], ones[:, 0:P], ones[:, :], start=True, stop=True)
            for stack in range(2):
                for layer in range(LAYERS):
                    ffn(stack == 0)
                    if stack == 0:
                        mixer1(layer)
                    elif layer == 0:
                        mixer2()
                    else:
                        mixer3()
                    ffn(stack == 0, layer < LAYERS - 1)
                if stack == 0:
                    norm_sum(OUT_SLOTS)

        @block.scalar
        def _(act):
            seen = Seen(x_ready=2, out_added=2)

            def link(ins):
                ins.then_inc(s["act_step"], 1)
                act.wait_ge(s["act_step"], seen("act_step"))

            def split_hi(b, cols=SLOT):
                act.wait_ge(s[SLOT_READY[b]], seen(SLOT_READY[b], 16))
                for c0, c1 in ((0, cols // 2), (cols // 2, cols)):
                    act.activation(slot_hi[b][:, c0:c1], slot[b][:, c0:c1], ACT.Copy).then_inc(s["hi_ready"], 1)

            def rstd_of(target, sums, width, ready="rstd_ready"):
                act.wait_ge(s["ss_done"], seen("ss_done"))
                link(act.activation(target, sums, ACT.Ln, bias=EPS, scale=1.0 / width))
                act.activation(target, target, ACT.Exp, scale=-0.5).then_inc(s[ready], 1)

            def squares_of_slots(final=False):
                for n in range(OUT_SLOTS):
                    if final:
                        act.wait_ge(s["final_ready"], 2 * n + 2)
                    act.wait_ge(s["sum_step"], seen("sum_step"))
                    act.activation(sq[:, n % 2, :], x[:, 2 * n:2 * n + 2, :].rearrange("p a b -> p (a b)"),
                                   ACT.Square).then_inc(s["sq_ready"], 1)
                seen.skip("sum_step", -1)

            def norm(shift=None):
                rstd_of(rstd[:, :], bank[4][:, 0:S], D)
                for k in range(KC):
                    act.wait_ge(s["h_raw"], seen("h_raw"))
                    if shift is None:
                        ins = act.activation(h_hi[:, k, :], h[:, k, :], ACT.Copy)
                    else:
                        ins = act.activation(h_hi[:, k, :], h[:, k, :], ACT.Identity, bias=mod[:, shift + k:shift + k + 1])
                    ins.then_inc(s["h_hi_ready"], 1)
                split_hi(1)

            def shift_of(stack, layer, i):
                return (layer * 9 + 3 * i) * KC if stack else None

            def ffn(stack, layer, i, last_one=False):
                norm(shift_of(stack, layer, i))

                def gate(b, cols):
                    act.wait_ge(s["slot_done"], seen("slot_done"))
                    act.wait_ge(s["act_ready"], seen("act_ready"))
                    act.activation(sil[:, b, :], bank[b][:, 0:S], ACT.Silu).then_inc(s["sil_ready"], 1)
                    split_hi(b, cols)

                with loop(act, seen, FC // 2 - 1, slot_done=2, act_ready=2, slot0_ready=16, slot1_ready=16, act_step=1):
                    link(act.activation(warm[:, 4:5], ones[:, 0:1], ACT.Silu))
                    for b in range(2):
                        gate(b, SLOT)
                for b in range(2):
                    gate(b, HALF_SLOT)
                norm_table()

                def square(j, b):
                    act.wait_ge(s["x_ready"], seen("x_ready"))
                    act.wait_ge(s["sum_step"], seen("sum_step"))
                    act.activation(sq[:, b, 0:S], x[:, bass.ds(j, 1), :].rearrange("p a b -> p (a b)"),
                                   ACT.Square).then_inc(s["sq_ready"], 1)

                with loop(act, seen, KC // 2 - 1, x_ready=2, sum_step=2, slot_done=4, slot0_ready=32, slot1_ready=32) as t:
                    for j in range(2):
                        for b in range(RING):
                            act.wait_ge(s["slot_done"], seen("slot_done"))
                            split_hi(b, HALF_SLOT)
                        square(t * 2 + j, j)
                for b in range(RING):
                    act.wait_ge(s["slot_done"], seen("slot_done"))
                    split_hi(b, HALF_SLOT)
                square(KC - 2, 0)
                act.wait_ge(s["slot_done"], seen("slot_done"))
                if not last_one:
                    split_hi(0)
                square(KC - 1, 1)
                seen.skip("sum_step", -1)
                act.wait_ge(s["slot_done"], seen("slot_done"))

            def project(n, kind="", place=None):
                act.wait_ge(s["slot_done"], seen("slot_done"))
                place = n if place is None else place
                if kind == "g":
                    last = act.activation(gates[:, :, :], bank[n % 2][:, :].rearrange("p (b n) -> p b n", b=TB)[:, :, 0:48],
                                          ACT.Sigmoid)
                elif kind in ("k", "v"):
                    act.wait_ge(s["cmp_summed"], seen("cmp_summed"))
                    last = act.activation(cmp_h[:, n % 2, 0:2 * NCMP], cmp_h[:, n % 2, 0:2 * NCMP], ACT.Gelu_apprx_tanh)
                elif kind == "w":
                    last = act.activation(proj[:, place, :], bank[n % 2][:, :], ACT.Silu)
                else:
                    last = act.activation(proj[:, place, :], bank[n % 2][:, :], ACT.Copy, scale=SCALE if kind == "s" else 1.0)
                last.then_inc(s["proj_ready"], 1)
                split_hi(n % 2)

            def norm_table():
                link(act.activation(warm[:, 4:5], ones[:, 0:1], ACT.Ln))

            def out_projection():
                norm_table()
                for n in range(OUT_SLOTS):
                    act.wait_ge(s["slot_done"], seen("slot_done"))
                    if n < OUT_SLOTS - 1:
                        split_hi(n % 2)
                    act.wait_ge(s["out_added"], seen("out_added"))
                    act.wait_ge(s["sum_step"], seen("sum_step"))
                    act.activation(sq[:, n % 2, :], x[:, 2 * n:2 * n + 2, :].rearrange("p a b -> p (a b)"),
                                   ACT.Square).then_inc(s["sq_ready"], 1)
                seen.skip("sum_step", -1)

            def attention(heads, first_chunk, scores, segments, copies, split, last_slot, beside=None, scale=None):
                def exps(i):
                    act.wait_ge(s["max_ready"], seen("max_ready"))
                    for j, (c, n) in enumerate(segments):
                        k = len(segments)
                        last = act.activation(scores[:, i % 3, c:c + n], scores[:, i % 3, c:c + n], ACT.Exp,
                                              bias=stats[:, i % 2, k + j:k + j + 1],
                                              accum_out=stats[:, i % 2, 2 * k + j:2 * k + j + 1])
                    last.then_inc(s["exp_ready"], 1)

                def copy(i):
                    act.wait_ge(s["pt_done"], seen("pt_done"))
                    if i >= 2:
                        act.wait_ge(s["pv_done"], seen("pv_done"))
                    for dst, src in copies(i):
                        last = act.activation(dst, src, ACT.Copy)
                    last.then_inc(s["pt_copied"], 1)

                def copy_output(i):
                    act.wait_ge(s["pv_done"], seen.value("pv_done", 1 if i < heads - 1 else 2))
                    target = h_hi if split else mix
                    act.activation(target[:, first_chunk + i // 2, :], bank[6 + i // 2 % 2][:, 0:S],
                                   ACT.Copy).then_inc(s["o_copied"], 1)

                for i in range(heads + 2):
                    if i == 0:
                        last_slot()
                    if scale and 1 <= i <= heads:
                        scale(i - 1)
                    if i < heads:
                        exps(i)
                    if 1 <= i <= heads:
                        copy(i - 1)
                    if beside:
                        beside(i)
                    if i >= 2 and i % 2 == 1:
                        copy_output(i - 2)
                seen.skip("pv_done", 2)

            def plain_attention(first_chunk, split, last_slot, beside=None):
                def scale(i):
                    act.wait_ge(s["recip_ready"], seen("recip_ready"))
                    for qt in range(TB):
                        e = att3[:, i % 3, qt * S:qt * S + S]
                        last = act.activation(e, e, ACT.Copy, scale=stats[:, i % 2, 6 + qt:7 + qt])
                    last.then_inc(s["probs_ready"], 1)

                attention(NA_HEADS, first_chunk, att3, [(0, S), (S, S)],
                          lambda i: [(att_pt[:, i % 2, 0:512], bank[4 + i % 2][:, :])], split, last_slot, beside, scale)

            def split_mix(first, count=4):
                act.wait_ge(s["mix_raw"], seen("mix_raw"))
                act.activation(h_hi[:, first:first + count, :], mix[:, first:first + count, :], ACT.Copy
                               ).then_inc(s["mix_hi_ready"], 1)

            def mixer1(layer):
                norm()
                z, e = ge[:, 0, :], ge[:, 1, :]
                for n in range(M1_SLOTS - 1):
                    project(n, {6: "s", 8: "w", 9: "w"}.get(n, ""))
                    if n == 2:
                        act.wait_ge(s["code_done"], seen("code_done"))
                        act.activation(code[:, :], bank[4][0:CODE, 0:S], ACT.Copy).then_inc(s["code_ready"], 1)
                    elif n == 4:
                        act.wait_ge(s["const_ready"], 16 * CONST_LOADS)
                        act.wait_ge(s["logit_done"], seen("logit_done"))
                        for way in range(2):
                            for pair in range(2):
                                c = (way * 2 + pair) * S
                                last = act.activation(z[:, c:c + S], bank[6 + way][:, pair * S:pair * S + S], ACT.Identity,
                                                      bias=b_gate[:, layer, way * 2 + pair:way * 2 + pair + 1])
                        last.then_inc(s["logit_read"], 1)
                        act.wait_ge(s["logit_read"], seen("logit_read"))
                    elif n == 5:
                        link(act.activation(e, z, ACT.Abs))
                    elif n == 6:
                        link(act.activation(e, e, ACT.Exp, scale=-1.0))
                        if layer == 0:
                            act.wait_ge(s["lru_const_ready"], seen("lru_const_ready"))
                            act.activation(lru_c[:, 8:12], lru_c[:, 4:8], ACT.Exp, scale=-1.0).then_inc(s["lru_exp_ready"], 1)
                    elif n == 7:
                        act.activation(e, e, ACT.Ln, bias=1.0).then_inc(s["forget_ready"], 1)

                def decay(i):
                    if i < len(GLA_LEVELS):
                        act.wait_ge(s["diff_ready"], seen("diff_ready"))
                        act.activation(ge[:, i % 2, :], ge[:, i % 2, :], ACT.Exp, scale=1.0 / GLA_TAU).then_inc(s["decay_ready"], 1)

                decay(0)
                plain_attention(0, False, lambda: project(M1_SLOTS - 1), lambda i: decay(i + 1))
                act.wait_ge(s["o_copied"], seen("o_copied", NA_HEADS // 2))
                act.activation(na_sq, mix[:, 0:4, :].rearrange("p a b -> p (a b)"), ACT.Square).then_inc(s["na_sq_ready"], 1)
                rstd_of(rstd[:, :], bank[4][:, 0:S], NA_HEADS * DH)
                split_mix(0)
                act.wait_ge(s["gla_o_done"], seen("gla_o_done"))
                for half in range(2):
                    act.activation(sq[:, half, :], bank[6 + half][:, :], ACT.Square).then_inc(s["gla_sq_ready"], 1)
                for half in range(2):
                    act.wait_ge(s["ss_done"], seen("ss_done"))
                    last = act.activation(gla_rstd[:, half * 512:half * 512 + 512], bank[half][:, :], ACT.Ln, bias=EPS, scale=1.0 / P)
                link(last)
                for half in range(2):
                    v = gla_rstd[:, half * 512:half * 512 + 512]
                    act.activation(v, v, ACT.Exp, scale=-0.5).then_inc(s["gla_rstd_ready"], 1)
                split_mix(4, 2)
                split_mix(6, 2)
                out_projection()

            def mixer2():
                norm(shift_of(1, 0, 1))
                lbf = lb[:, :, :].rearrange("p a b -> p (a b)")
                for n in range(M2_SLOTS - 1):
                    project(n, place=M2_PLACES[n])
                    if n == 5:
                        for c in range(4):
                            act.wait_ge(s["lru_gate_done"], seen("lru_gate_done"))
                            act.activation(lr[:, c, :], lru_bank[c][:, 0:S], ACT.Sigmoid, bias=lru_p[:, 20 + c:21 + c])
                            act.activation(li[:, c, :], lru_bank[c][:, S:2 * S], ACT.Sigmoid, bias=lru_p[:, 24 + c:25 + c]
                                           ).then_inc(s["lru_gate_ready"], 1)
                    elif n == 6:
                        act.wait_ge(s["lru_const_ready"], seen("lru_const_ready"))
                        act.wait_ge(s["lru_gate_ready"], seen("lru_gate_ready", 4))
                        for c in range(4):
                            act.activation(la[:, c, :], lr[:, c, :], ACT.Exp, scale=lru_c[:, 4 + c:5 + c])
                            last = act.activation(lb[:, c, :], lr[:, c, :], ACT.Tanh, scale=lru_c[:, c:c + 1])
                        last.then_inc(s["lru_decay_ready"], 1)
                    elif n == 7:
                        act.wait_ge(s["lru_sq_ready"], seen("lru_sq_ready"))
                        act.activation(lbf, lbf, ACT.Sqrt).then_inc(s["lru_mult_ready"], 1)
                    elif n == 8:
                        act.wait_ge(s["proj_ready"], 2 + LAYERS * M1_SLOTS + 8)
                        act.activation(proj[:, 8:10, :], proj[:, 8:10, :], ACT.Gelu_apprx_tanh).then_inc(s["gelu_ready"], 1)
                plain_attention(4, True, lambda: project(M2_SLOTS - 1, place=M2_PLACES[-1]), lambda i: split_mix(0) if i == 1 else None)
                seen.skip("o_copied", 4)
                out_projection()

            def mixer3():
                norm(shift_of(1, 1, 1))
                for n, kind in enumerate(("", "", "", "", "", "", "k", "v", "")):
                    project(n, kind, M3_PLACES[n])
                    if n == 3:
                        act.wait_ge(s["blocks_raw"], seen("blocks_raw"))
                        act.activation(cmp_hi, cmp_g[:, :, :, :], ACT.Copy).then_inc(s["cmp_hi_ready"], 1)
                    elif n == 8:
                        act.wait_ge(s["cmp_done"], seen("cmp_done"))
                        act.activation(k_cmp[:, 0:2 * NCMP], bank[2][:, 0:2 * NCMP], ACT.Copy)
                        act.activation(v_cmp[0:NCMP, :, :].rearrange("p a b -> p (a b)"), bank[3][0:NCMP, 0:P], ACT.Copy
                                       ).then_inc(s["cmp_ready"], 1)
                segments = [(0, NCMP), (16, P), (16 + P, P), (S + 16, NCMP), (S + 32, S), (2 * S + 32, S)]
                attention(NSA_HEADS, 0, nsa_t, segments,
                          lambda i: [(att_pt[:, i % 2, 0:512], bank[4][:, :])], True,
                          lambda: project(M3_SLOTS - 1, "g"))
                seen.skip("o_copied", 8)
                out_projection()

            act.wait_ge(s["cond_loaded"], 16)
            act.activation(cond[:, :], cond[:, :], ACT.Silu).then_inc(s["cond_ready"], 1)
            act.wait_ge(s["x_loaded"], 16)
            squares_of_slots()
            act.wait_ge(s["sum_step"], seen.value("sum_step", 1))
            norm_table()
            split_hi(0)
            for stack in range(2):
                for layer in range(LAYERS):
                    ffn(stack, layer, 0)
                    if stack == 0:
                        mixer1(layer)
                    elif layer == 0:
                        mixer2()
                    else:
                        mixer3()
                    ffn(stack, layer, 2, stack == 1 and layer == LAYERS - 1)
                rstd_of(rstd[:, :], bank[4][:, 0:S], D)
                if stack == 0:
                    squares_of_slots(final=True)
                    norm_table()

        @block.vector
        def _(dve):
            seen = Seen(sum_step=1, proj_ready=2, out_added=2)

            def link(ins):
                ins.then_inc(s["dve_step"], 1)
                dve.wait_ge(s["dve_step"], seen("dve_step"))

            def split_lo(b, part, cols=SLOT):
                dve.wait_ge(s["hi_ready"], seen("hi_ready"))
                c0, c1 = ((0, cols // 2), (cols // 2, cols))[part]
                ins = dve.tensor_tensor(slot_lo[b][:, c0:c1], slot[b][:, c0:c1], slot_hi[b][:, c0:c1].bitcast(F32), ALU.subtract)
                if part:
                    ins.then_inc(s["lo_ready"], 1)

            def split_both(b, cols=SLOT):
                split_lo(b, 0, cols)
                split_lo(b, 1, cols)

            def add_squares(halves, n):
                dve.wait_ge(s["sq_ready"], seen("sq_ready"))
                dve.wait_ge(s["sum_step"], seen("sum_step"))
                for j in range(halves):
                    ins = dve.tensor_tensor(sqsum[:, :], sqsum[:, :], sq[:, n % 2, j * S:j * S + S], ALU.add)
                    if j < halves - 1:
                        link(ins)
                ins.then_inc(s["sum_step"], 1)

            def clear_sum():
                link(dve.memset(sqsum[:, :], 0.0))

            def sum_slots():
                clear_sum()
                for n in range(OUT_SLOTS - 1):
                    add_squares(2, n)
                seen.skip("sq_ready", 1)

            def final_norm(dst, i, summed=False):
                dve.wait_ge(s["rstd_ready"], seen("rstd_ready"))
                for k in range(KC):
                    dve.scalar_tensor_tensor(out=dst[:, k, :], in0=x[:, k, :], scalar=gains[:, i, k:k + 1],
                                             in1=rstd[:, :], op0=ALU.mult, op1=ALU.mult).then_inc(s["final_ready"], 1)
                    if summed and k == 3:
                        clear_sum()
                    elif summed and k in (5, 7):
                        add_squares(2, (k - 5) // 2)
                if summed:
                    add_squares(2, 2)
                    seen.skip("sq_ready", 1)

            def norm_of(stack, layer, i, group=None):
                dve.wait_ge(s["rstd_ready"], seen("rstd_ready"))
                lag = 2
                for n in range(KC + lag):
                    if n < KC:
                        gain = mod_gain[:, layer, i, n:n + 1] if stack else gains[:, 3 * layer + i, n:n + 1]
                        dve.scalar_tensor_tensor(out=h[:, n, :], in0=x[:, n, :], scalar=gain,
                                                 in1=rstd[:, :], op0=ALU.mult, op1=ALU.mult).then_inc(s["h_raw"], 1)
                    if n >= lag:
                        k = n - lag
                        dve.wait_ge(s["h_hi_ready"], seen("h_hi_ready"))
                        hi = h_hi[:, k, :].bitcast(F32)
                        if stack:
                            c = (layer * 9 + 3 * i) * KC + k
                            ins = dve.scalar_tensor_tensor(out=h_lo[:, k, :], in0=h[:, k, :], scalar=mod[:, c:c + 1],
                                                           in1=hi, op0=ALU.add, op1=ALU.subtract)
                        else:
                            ins = dve.tensor_tensor(h_lo[:, k, :], h[:, k, :], hi, ALU.subtract)
                        ins.then_inc(s["h_ready"], 1)
                split_both(1)
                if group is not None:
                    mod_group(group)

            def mod_group(group):
                c = group * MOD_GROUP
                dve.wait_ge(s["mod_done"], seen("mod_done"))
                link(dve.tensor_tensor(mod[:, c:c + MOD_GROUP], bank[5][:, 0:MOD_GROUP], mod_b[:, c:c + MOD_GROUP], ALU.add))

            def ffn(stack, layer, i, group, last_one=False):
                norm_of(stack, layer, i, group)
                if stack == layer == i == 0:
                    dve.wait_ge(s["mask_loaded"], 16)
                    link(dve.tensor_copy(gla_mask[:, :, :].rearrange("p a b -> p (a b)"), wide_mask))
                seen.skip("slot_done", FC)

                def hidden(c, b, cols):
                    dve.wait_ge(s["sil_ready"], seen("sil_ready"))
                    dve.tensor_tensor(act_f[:, b, :], sil[:, b, :], bank[b][:, S:2 * S], ALU.mult).then_inc(s["dve_step"], 1)
                    value = seen("dve_step")
                    split_lo(b, 0, cols)
                    dve.wait_ge(s["dve_step"], value)
                    hi, lo = (v[:, bass.ds(c, 1), :].rearrange("p a b -> p (a b)") for v in (act_hi, act_lo))
                    dve.tensor_copy(hi, act_f[:, b, :]).then_inc(s["dve_step"], 1)
                    value = seen("dve_step")
                    split_lo(b, 1, cols)
                    dve.wait_ge(s["dve_step"], value)
                    dve.tensor_tensor(lo, act_f[:, b, :], hi.bitcast(F32), ALU.subtract).then_inc(s["act_ready"], 1)

                with loop(dve, seen, FC // 2 - 1, sil_ready=2, dve_step=4, hi_ready=4) as t:
                    for b in range(2):
                        hidden(t * 2 + b, b, SLOT)
                for b in range(2):
                    hidden(FC - 2 + b, b, HALF_SLOT)
                clear_sum()

                def residual(j, bk):
                    dve.wait_ge(s["slot_done"], seen("slot_done", 2))
                    xj = x[:, bass.ds(j, 1), :].rearrange("p a b -> p (a b)")
                    half = 0.5 if stack == 0 else mod_gate[:, layer, i, bass.ds(j, 1)]
                    dve.scalar_tensor_tensor(out=xj, in0=bank[2 + bk][:, 0:S], scalar=half, in1=xj,
                                             op0=ALU.mult, op1=ALU.add).then_inc(s["x_ready"], 1)

                with loop(dve, seen, KC // 2 - 1, slot_done=4, sq_ready=2, sum_step=2, hi_ready=8) as t:
                    for j in range(2):
                        split_both(0, HALF_SLOT)
                        residual(t * 2 + j, j)
                        split_both(1, HALF_SLOT)
                        add_squares(1, j)
                split_both(0, HALF_SLOT)
                residual(KC - 2, 0)
                split_both(1, HALF_SLOT)
                add_squares(1, 0)
                if not last_one:
                    split_both(0)
                residual(KC - 1, 1)
                seen.skip("sq_ready", 1)

            def split_mix(first, count=4):
                dve.wait_ge(s["mix_hi_ready"], seen("mix_hi_ready"))
                for k in range(first, first + count):
                    dve.tensor_tensor(h_lo[:, k, :], mix[:, k, :], h_hi[:, k, :].bitcast(F32), ALU.subtract
                                      ).then_inc(s["mix_split"], 1)

            def two(v):
                return v.rearrange("p (a b) -> p a b", a=2)

            def split_output(chunk, i):
                dve.wait_ge(s["o_copied"], seen("o_copied"))
                dve.tensor_tensor(h_lo[:, chunk, :], bank[6 + i // 2 % 2][:, 0:S], h_hi[:, chunk, :].bitcast(F32),
                                  ALU.subtract).then_inc(s["o_split"], 1)

            def out_projection(stack, layer):
                clear_sum()
                for n in range(OUT_SLOTS):
                    dve.wait_ge(s["slot_done"], seen("slot_done"))
                    for j in range(2):
                        k = 2 * n + j
                        y = bank[2 + n % 2][:, j * S:j * S + S]
                        if stack == 0:
                            ins = dve.tensor_tensor(x[:, k, :], y, x[:, k, :], ALU.add)
                        else:
                            ins = dve.scalar_tensor_tensor(out=x[:, k, :], in0=y, scalar=mod_gate[:, layer, 1, k:k + 1],
                                                           in1=x[:, k, :], op0=ALU.mult, op1=ALU.add)
                    ins.then_inc(s["out_added"], 1)
                    if n < OUT_SLOTS - 1:
                        split_both(n % 2)
                        add_squares(2, n)
                seen.skip("sq_ready", 1)

            def attention(bias, last_slot, first_chunk=None, first_steps=None, last_steps=None):
                def scores(i):
                    b, T = i % 2, att3[:, i % 3, :]
                    dve.wait_ge(s["score_done"], seen("score_done"))
                    if i >= 3:
                        dve.wait_ge(s["pt_done"], seen("pt_done"))
                    dve.scalar_tensor_tensor(out=T, in0=bank[2 + b][:, :], scalar=SCALE,
                                             in1=bias(i), op0=ALU.mult, op1=ALU.add).then_inc(s["score_read"], 1)
                    dve.wait_ge(s["score_read"], seen("score_read"))
                    dve.tensor_reduce(out=stats[:, b, 2:4], in_=two(T), axis=AXX, op=ALU.max, negate=True
                                      ).then_inc(s["max_ready"], 1)

                def invert(i):
                    b = i % 2
                    dve.wait_ge(s["exp_ready"], seen("exp_ready"))
                    dve.reciprocal(stats[:, b, 6:8], stats[:, b, 4:6]).then_inc(s["recip_ready"], 1)

                for i in range(NA_HEADS + 3):
                    if i == 0:
                        last_slot()
                    if 1 <= i <= NA_HEADS:
                        invert(i - 1)
                    if i < NA_HEADS:
                        scores(i)
                    if first_steps:
                        first_steps(i)
                    if first_chunk is not None and i >= 4 and i % 2 == 0:
                        split_output(first_chunk + (i - 4) // 2, i - 4)
                    if last_steps:
                        last_steps(i)
                if first_chunk is None:
                    seen.skip("o_copied", NA_HEADS // 2)
                seen.skip("pt_done", 3)
                seen.skip("pv_done", NA_HEADS)

            def level_halves(way, n, pick):
                return way.rearrange("p (b two t) -> p b two t", two=2, t=n // 2)[:, :, pick, :]

            lam, sp8, ns8 = lru_p[:, 28:32], lru_c[:, 0:4], lru_c[:, 4:8]
            u, z, z2, p, d = (lru_c[:, 8 + 4 * i:12 + 4 * i] for i in range(5))

            def lru_magnitude():
                link(dve.tensor_scalar(ns8, lam, -1.0, None, ALU.mult))
                dve.tensor_tensor(ns8, ns8, lam, ALU.max).then_inc(s["lru_const_ready"], 1)

            def lru_softplus():
                dve.wait_ge(s["lru_exp_ready"], seen("lru_exp_ready"))
                link(dve.tensor_scalar(d, u, 2.0, None, ALU.add))
                link(dve.reciprocal(d, d))
                link(dve.tensor_tensor(z, u, d, ALU.mult))
                link(dve.tensor_tensor(z2, z, z, ALU.mult))
                link(dve.tensor_scalar(p, z2, 1.0 / 17, 1.0 / 15, ALU.mult, ALU.add))
                for k in (13, 11, 9, 7, 5, 3, 1):
                    link(dve.tensor_tensor(p, p, z2, ALU.mult))
                    link(dve.tensor_scalar(p, p, 1.0 / k, None, ALU.add))
                link(dve.tensor_tensor(p, p, z, ALU.mult))
                link(dve.tensor_scalar(p, p, 2.0, None, ALU.mult))
                link(dve.tensor_scalar(d, lam, -1.0, 0.0, ALU.mult, ALU.max))
                link(dve.tensor_tensor(p, p, d, ALU.add))
                dve.tensor_scalar(sp8, p, 8.0, None, ALU.mult)
                dve.tensor_scalar(ns8, p, -8.0, None, ALU.mult).then_inc(s["lru_const_ready"], 1)

            def mixer1(layer):
                dve.wait_ge(s["const_ready"], 16 * CONST_LOADS)
                norm_of(0, layer, 1, 3 * layer)
                if layer == 0:
                    lru_magnitude()
                bf, bb = gb[:, 0, :], gb[:, 1, :]
                qk_all = proj[:, 6:8, :].rearrange("p a b -> p (a b)")

                def diffs(i):
                    n = GLA_LEVELS[i]
                    shape = [P, 512 // n, n // 2]
                    f0, f1, b0, b1 = (level_halves(w, n, j) for w in (bf, bb) for j in (0, 1))
                    fm = f0[:, :, n // 2 - 1:n // 2].to_broadcast(shape)
                    bm = b1[:, :, 0:1].to_broadcast(shape)
                    q0, q1, k0, k1 = (level_halves(ge[:, i % 2, w * 512:w * 512 + 512], n, j) for w in (0, 1) for j in (0, 1))
                    dve.tensor_tensor(q1, f1, fm, ALU.subtract)
                    dve.tensor_tensor(q0, b0, bm, ALU.subtract)
                    dve.tensor_tensor(k0, fm, f0, ALU.subtract)
                    dve.tensor_tensor(k1, bm, b1, ALU.subtract).then_inc(s["diff_ready"], 1)

                def products(i):
                    dve.wait_ge(s["decay_ready"], seen("decay_ready"))
                    dve.tensor_tensor(ge[:, i % 2, :], ge[:, i % 2, :], qk_all, ALU.mult).then_inc(s["qk_ready"], 1)

                def read(i):
                    dve.wait_ge(s["level_done"], seen("level_done"))
                    for odd in range(2):
                        src = bank[odd][:, :].rearrange("p (a b n) -> p a b n", a=2, b=2)
                        dst = ga[:, odd::2, 1:3, :] if i == 0 else ga[:, odd::2, 0::3, :]
                        if i < 2:
                            last = dve.tensor_copy(dst, src)
                        else:
                            m = gla_mask[:, i - 2, :].unsqueeze(1).unsqueeze(1).to_broadcast([P, 2, 2, P])
                            last = dve.copy_predicated(dst, m, src)
                    last.then_inc(s["level_read"], 1)
                    dve.wait_ge(s["level_read"], seen("level_read"))

                def before_scale(i):
                    if i < len(GLA_LEVELS):
                        products(i)

                def after_scale(i):
                    if 1 <= i <= len(GLA_LEVELS) + 1:
                        read(i - 1)
                    if i + 1 < len(GLA_LEVELS):
                        diffs(i + 1)

                seen.skip("slot_done", M1_SLOTS)
                for n in range(M1_SLOTS - 1):
                    split_both(n % 2)
                    if n == 8:
                        dve.wait_ge(s["forget_ready"], seen("forget_ready"))
                        link(dve.scalar_tensor_tensor(out=ge[:, 0, :], in0=ge[:, 0, :], scalar=0.0, in1=ge[:, 1, :],
                                                      op0=ALU.min, op1=ALU.subtract))
                    elif n == 9:
                        for pair in range(2):
                            c, back = pair * S, 512 + pair * S
                            dve.tensor_tensor_scan(gb[:, 0, c:c + S], ones[:, :], ge[:, 0, c:c + S], 0.0, ALU.mult, ALU.add)
                            last = dve.tensor_tensor_scan(gb[:, 1, c:c + S][:, ::-1], ones[:, :], ge[:, 0, back:back + S][:, ::-1],
                                                          0.0, ALU.mult, ALU.add)
                        link(last)
                    elif n == 10:
                        diffs(0)
                dve.wait_ge(s["bias_masked"], seen("bias_masked", NA_HEADS * TB))

                def last_slot():
                    split_both((M1_SLOTS - 1) % 2)
                    dve.wait_ge(s["proj_ready"], seen("proj_ready", M1_SLOTS))

                attention(lambda i: na_bias[:, i, :], last_slot, None, before_scale, after_scale)
                dve.wait_ge(s["rstd_ready"], seen("rstd_ready"))
                for k in range(4):
                    last = dve.scalar_tensor_tensor(out=mix[:, k, :], in0=mix[:, k, :], scalar=na_gain[:, layer, k:k + 1],
                                                    in1=rstd[:, :], op0=ALU.mult, op1=ALU.mult)
                last.then_inc(s["mix_raw"], 1)
                split_mix(0)
                if layer == 0:
                    lru_softplus()
                for half in range(2):
                    m = mix[:, 4 + 2 * half:6 + 2 * half, :].rearrange("p a b -> p (a b)")
                    dve.wait_ge(s["gla_rstd_ready"], seen("gla_rstd_ready"))
                    link(dve.scalar_tensor_tensor(out=m, in0=bank[6 + half][:, :], scalar=gla_gain[:, layer:layer + 1],
                                                  in1=gla_rstd[:, half * 512:half * 512 + 512], op0=ALU.mult, op1=ALU.mult))
                    dve.tensor_tensor(m, m, proj[:, 8 + half, :], ALU.mult).then_inc(s["mix_raw"], 1)
                split_mix(4, 2)
                split_mix(6, 2)
                out_projection(0, layer)

            def both(v):
                return v.unsqueeze(1).to_broadcast([P, 2, v.shape[1]])

            def rotate(dst, plain, turned, tmp):
                dve.wait_ge(s["rot_done"], seen("rot_done"))
                link(dve.tensor_tensor(two(tmp), two(plain), both(rope_cos[:, :]), ALU.mult))
                dve.tensor_tensor(two(dst), two(turned), both(rope_sin[:, :]), ALU.mult).then_inc(s["rot_read"], 1)
                dve.wait_ge(s["rot_read"], seen("rot_read"))
                dve.tensor_tensor(dst, dst, tmp, ALU.add).then_inc(s["rope_ready"], 1)
                dve.wait_ge(s["rope_ready"], seen("rope_ready"))

            def mixer2():
                norm_of(1, 0, 1)
                seen.skip("slot_done", M2_SLOTS)
                flat = lambda v: v[:, :, :].rearrange("p a b -> p (a b)")
                xl = proj[:, 6:8, :].rearrange("p a (b t) -> p (a b) t", b=2)

                def convolve(back):
                    for c in range(4):
                        if back == 0:
                            last = dve.tensor_scalar(xc[:, c, :], xl[:, c, :], lru_p[:, 4 * c + 3:4 * c + 4],
                                                     lru_p[:, 16 + c:17 + c], ALU.mult, ALU.add)
                        else:
                            last = dve.scalar_tensor_tensor(out=xc[:, c, back:S], in0=xl[:, c, 0:S - back],
                                                            scalar=lru_p[:, 4 * c + 3 - back:4 * c + 4 - back],
                                                            in1=xc[:, c, back:S], op0=ALU.mult, op1=ALU.add)
                    last.then_inc(s["conv_step"], 1)
                    dve.wait_ge(s["conv_step"], seen("conv_step"))

                for n in range(M2_SLOTS - 1):
                    split_both(n % 2)
                    if n == 2:
                        dve.wait_ge(s["proj_ready"], seen.value("proj_ready", 2))
                        convolve(0)
                        convolve(1)
                    elif n == 3:
                        convolve(2)
                        convolve(3)
                    elif n == 5:
                        for i in range(2):
                            rotate(proj[:, i, :], proj[:, i, :], bank[4 + i][:, :], att_t[:, 0, 0:512])
                    elif n == 6:
                        dve.wait_ge(s["lru_decay_ready"], seen("lru_decay_ready"))
                        link(dve.tensor_tensor(flat(lg), flat(la), flat(la), ALU.mult))
                        dve.scalar_tensor_tensor(out=flat(lb), in0=flat(lg), scalar=1.0, in1=flat(lb),
                                                 op0=ALU.add, op1=ALU.mult).then_inc(s["lru_sq_ready"], 1)
                    elif n == 7:
                        dve.wait_ge(s["lru_in_ready"], seen("lru_in_ready"))
                        dve.wait_ge(s["lru_mult_ready"], seen("lru_mult_ready"))
                        link(dve.tensor_tensor(flat(lb), flat(lb), flat(li), ALU.mult))
                        for c in range(4):
                            last = dve.tensor_tensor_scan(xc[:, c, :], la[:, c, :], lb[:, c, :], 0.0, ALU.mult, ALU.add)
                        last.then_inc(s["lru_scanned"], 1)
                    elif n == 8:
                        for i in range(2):
                            rotate(proj[:, 2 + i, :], proj[:, 2 + i, :], bank[4 + i][:, :], att_t[:, 0, 0:512])

                def last_slot():
                    split_both((M2_SLOTS - 1) % 2)
                    dve.wait_ge(s["proj_ready"], seen("proj_ready", M2_SLOTS))

                def recurrence_output(i):
                    if i == 2:
                        split_mix(0)

                attention(lambda i: causal[:, :, :].rearrange("p a b -> p (a b)"), last_slot, 4, recurrence_output)
                out_projection(1, 0)

            def mixer3():
                norm_of(1, 1, 1)
                done = seen.value("slot_done")
                seen.skip("slot_done", M3_SLOTS)

                def gather_blocks():
                    dve.wait_ge(s["cmp_dup_done"], seen("cmp_dup_done", 2))
                    for g in range(NSA_GROUPS):
                        for kv in range(2):
                            for half in range(2):
                                p0 = DH * half
                                src = bank[2 + g][p0:p0 + DH, kv * S:kv * S + S].rearrange("p (i c two) -> p c i two", i=16, two=2)
                                for cb in range(2):
                                    dst = cmp_g[p0:p0 + DH, kv, 8 * cb:8 * cb + 8, g * NCMP:g * NCMP + NCMP]
                                    pos = cmp_pos[p0:p0 + DH, kv, 8 * cb:8 * cb + 8].unsqueeze(2).to_broadcast([DH, 8, NCMP])
                                    last = dve.tensor_tensor(dst, src[:, :, cb:cb + NCMP, half], pos, ALU.add)
                    last.then_inc(s["blocks_raw"], 1)

                for n in range(M3_SLOTS - 1):
                    if n in (6, 7):
                        dve.wait_ge(s["slot_done"], done + n + 1)
                        dve.tensor_copy(cmp_h[:, n - 6, 0:2 * NCMP], bank[n - 6][:, 0:2 * NCMP]).then_inc(s["dve_step"], 1)
                        dve.wait_ge(s["dve_step"], seen("dve_step"))
                        dve.tensor_tensor(cmp_h[:, n - 6, 0:2 * NCMP], cmp_h[:, n - 6, 0:2 * NCMP],
                                          bank[n - 6][:, 2 * NCMP:4 * NCMP], ALU.add).then_inc(s["cmp_summed"], 1)
                    split_both(n % 2)
                    if n == 2:
                        gather_blocks()
                    elif n == 3:
                        dve.wait_ge(s["cmp_hi_ready"], seen("cmp_hi_ready"))
                        dve.tensor_tensor(cmp_lo, cmp_g[:, :, :, :], cmp_hi.bitcast(F32), ALU.subtract
                                          ).then_inc(s["blocks_ready"], 1)
                    elif n == 4:
                        for g in range(NSA_GROUPS):
                            rotate(k_rope[:, g, :], bank[4 + 2 * g][:, :], bank[5 + 2 * g][:, :], rope_tmp[:, :])
                    elif n in (6, 8):
                        for i in range(2):
                            q = n - 6 + i
                            rotate(q_rope[:, q, :], proj[:, q, :], bank[4 + i][:, :], rope_tmp[:, :])

                def cmp_cols(v):
                    return v[:, 0:2 * (S + 16)].rearrange("p (a b) -> p a b", a=2)[:, :, 0:NCMP]

                def scores(i):
                    b = i % 2
                    T, big, small = nsa_t[:, i % 3, :], bank[b], bank[2 + b]
                    dve.wait_ge(s["score_done"], seen("score_done"))
                    early, late = T[:, 16:16 + S], T[:, S + 32:S + 32 + 512]
                    dve.scalar_tensor_tensor(out=two(late), in0=two(big[:, :]), scalar=SCALE, in1=both(causal[:, 1, :]),
                                             op0=ALU.mult, op1=ALU.add)
                    dve.scalar_tensor_tensor(out=two(early), in0=two(small[:, 0:S]), scalar=SCALE, in1=both(causal[:, 0, 0:P]),
                                             op0=ALU.mult, op1=ALU.add)
                    dve.scalar_tensor_tensor(out=cmp_cols(T), in0=two(small[:, S:S + 32])[:, :, 0:NCMP], scalar=SCALE,
                                             in1=cmp_bias[:, :, 0:NCMP], op0=ALU.mult, op1=ALU.add).then_inc(s["score_read"], 1)
                    dve.wait_ge(s["score_read"], seen("score_read"))
                    dve.tensor_reduce(out=stats[:, b, 10:12], in_=two(late), axis=AXX, op=ALU.max, negate=True)
                    dve.tensor_reduce(out=stats[:, b, 7:9], in_=two(early), axis=AXX, op=ALU.max, negate=True)
                    dve.tensor_reduce(out=two(stats[:, b, 6:12])[:, :, 0], in_=cmp_cols(T), axis=AXX, op=ALU.max, negate=True
                                      ).then_inc(s["max_ready"], 1)

                def scale(i):
                    b = i % 2
                    dve.wait_ge(s["exp_ready"], seen("exp_ready"))
                    link(dve.reciprocal(stats[:, b, 18:24], stats[:, b, 12:18]))
                    link(dve.tensor_tensor(two(stats[:, b, 18:24]), two(stats[:, b, 18:24]), gates[:, :, 3 * i:3 * i + 3], ALU.mult))
                    for qt in range(TB):
                        f = stats[:, b, 18 + 3 * qt:21 + 3 * qt]
                        c0 = qt * (S + 16)
                        e = nsa_t[:, i % 3, c0:c0 + NCMP]
                        dve.scalar_tensor_tensor(out=e, in0=e, scalar=f[:, 0:1], in1=cmp_keep[:, qt, 0:NCMP],
                                                 op0=ALU.mult, op1=ALU.mult)
                        n = (P, S)[qt]
                        for br in range(2):
                            e = nsa_t[:, i % 3, c0 + 16 + br * n:c0 + 16 + br * n + n]
                            last = dve.tensor_scalar(e, e, f[:, 1 + br:2 + br], None, ALU.mult)
                    last.then_inc(s["probs_ready"], 1)

                def copy(i):
                    dve.wait_ge(s["pt_done"], seen("pt_done"))
                    if i >= 2:
                        dve.wait_ge(s["pv_done"], seen("pv_done"))
                    dve.tensor_copy(att_pt[:, i % 2, 512:768], bank[5][:, 0:S])
                    dve.tensor_copy(att_pt[0:NCMP, i % 2, 768:1024], bank[5][0:NCMP, S:2 * S]).then_inc(s["pt_half_copied"], 1)

                for i in range(NSA_HEADS + 3):
                    if i == 0:
                        split_both((M3_SLOTS - 1) % 2)
                        dve.wait_ge(s["proj_ready"], seen("proj_ready", M3_SLOTS))
                    if i < NSA_HEADS:
                        scores(i)
                    if 2 <= i < NSA_HEADS + 2:
                        copy(i - 2)
                    if i >= 4 and i % 2 == 0:
                        split_output((i - 4) // 2, i - 4)
                    if 1 <= i <= NSA_HEADS:
                        scale(i - 1)
                seen.skip("pv_done", 2)
                out_projection(1, 1)

            dve.memset(ones[:, :], 1.0).then_inc(s["sum_step"], 2)
            dve.memset(warm[:, 0:1], 1.0).then_inc(s["act_ready"], 2)
            dve.memset(warm[:, 1:2], 1.0).then_inc(s["x_ready"], 2)
            dve.memset(warm[:, 2:3], 1.0).then_inc(s["out_added"], 2)
            dve.memset(warm[:, 3:4], 1.0).then_inc(s["proj_ready"], 2)
            dve.memset(warm[:, 5:6], 1.0).then_inc(s["lo_ready"], 2)
            sum_slots()
            split_both(0)
            dve.wait_ge(s["gains_loaded"], 16)
            for stack in range(2):
                for layer in range(LAYERS):
                    ffn(stack, layer, 0, 3 * layer - 1 if stack == 0 and layer else None)
                    if stack == 0:
                        mixer1(layer)
                    elif layer == 0:
                        mixer2()
                    else:
                        mixer3()
                    ffn(stack, layer, 2, 3 * layer + 1 if stack == 0 else None, stack == 1 and layer == LAYERS - 1)
                if stack == 0:
                    final_norm(x, G_FINAL1, summed=True)
                    mod_group(MOD_GROUPS - 1)
                    for l in range(LAYERS):
                        for i in range(3):
                            c = (l * 9 + 3 * i) * KC
                            dve.scalar_tensor_tensor(out=mod_gain[:, l, i, :], in0=mod[:, c + KC:c + 2 * KC], scalar=1.0,
                                                     in1=gains[:, G_NORM2 + 3 * l + i, :], op0=ALU.add, op1=ALU.mult)
                            last = dve.tensor_scalar(mod_gate[:, l, i, :], mod[:, c + 2 * KC:c + 3 * KC],
                                                     1.0 if i == 1 else 0.5, None, ALU.mult)
                    link(last)
                else:
                    final_norm(h, G_FINAL2)


def constants():
    f = np.float32
    d = np.arange(P) % DH
    half = DH // 8
    freqs = f(500000.0) ** (-np.arange(half, dtype=f) * f(2.0) / f(DH // 4))
    ang = np.arange(S, dtype=f)[None, :] * freqs.astype(f)[d % half][:, None]
    turned = (d < 2 * half)[:, None]
    cos, sin = np.where(turned, np.cos(ang), f(1)).astype(f), np.where(turned, np.sin(ang), f(0)).astype(f)
    rot = np.zeros((P, P), f)
    for o in range(P):
        if o % DH < half:
            rot[o + half, o] = -1
        elif o % DH < 2 * half:
            rot[o - half, o] = 1
    pick = [np.zeros((P, P), f) for _ in range(2)]
    for g in range(2):
        for o in range(P):
            pick[g][g * DH + o % DH, o] = 1
    mats = np.stack([rot, pick[0], pick[1], pick[0] @ rot, pick[1] @ rot], axis=1)
    q = np.arange(TB)[None, :, None] * P + np.arange(P)[:, None, None]
    causal = np.where(np.arange(S)[None, None, :] <= q, f(0), f(NEG))
    seen = np.arange(16)[None, None, :] * CMP_STRIDE + CMP_LEN - 1 <= q
    col = np.arange(P) % GRID_W
    start = np.clip(col - WIN_W // 2, 0, GRID_W - WIN_W)[:, None]
    kc = np.arange(GRID_W)[None, :]
    inside = (kc >= start) & (kc < start + WIN_W)
    na = np.repeat(np.where(inside, f(0), f(NEG))[:, None, :], ROWS, axis=1)
    i, j = np.arange(P)[:, None], np.arange(P)[None, :]
    masks = [(i // n == j // n) for n in GLA_LEVELS[2:] + [1]]
    return {
        "ident": np.eye(P, dtype=f), "rope_cos": cos, "rope_sin": sin, "mats": mats.astype(f),
        "causal": causal.astype(f), "cmp_bias": np.where(seen, f(0), f(NEG)).astype(f),
        "cmp_keep": seen.astype(f), "na_mask": na.astype(f),
        "gla_mask": np.stack(masks, axis=1).astype(np.uint32).reshape(P, 7 * P),
    }


def units(w):
    n = w.shape[1] // P
    return w.reshape(KC, P, n // 2, 2, P).transpose(2, 1, 3, 0, 4)


def gate_up(wg, wu):
    pair = [w.reshape(KC, P, FC, P) for w in (wg, wu)]
    return np.stack(pair, axis=0).transpose(3, 2, 0, 1, 4)


def per_partition(v):
    v = v.reshape(v.shape[:-1] + (v.shape[-1] // P, P))
    return np.moveaxis(v, -1, 0)


def lay_out(i):
    a = dict(constants())
    f = np.float32
    a["x"] = i["x"][0].T.reshape(KC, P, S).transpose(1, 0, 2)
    slots = np.zeros((TOTAL_SLOTS, P, 2, KC, P), f)
    wd = np.empty((FFNS * KC * 2, P, HF, P), f)
    n = m = 0

    def put(block):
        nonlocal n
        slots[n:n + len(block)] = block
        n += len(block)

    def put_down(w):
        nonlocal m
        wd[m:m + 2 * KC] = w.reshape(2, HF, P, KC, P).transpose(3, 0, 2, 1, 4).reshape(2 * KC, P, HF, P)
        m += 2 * KC

    for l in range(LAYERS):
        put(gate_up(i["ffn1_wg"][l], i["ffn1_wu"][l]))
        put_down(i["ffn1_wd"][l])
        w = i["w_in"][l]
        q, k, v, gq, gk, gv, gr = (w[:, c:c + m_] for c, m_ in ((0, 512), (512, 512), (1024, 512), (1536, 256),
                                                              (1792, 256), (2048, 512), (2560, 512)))
        for part in (q, k, v, gq, gk, gr, gv, i["w_out"][l]):
            put(units(part))
        put(gate_up(i["ffn2_wg"][l], i["ffn2_wu"][l]))
        put_down(i["ffn2_wd"][l])
    for l in range(LAYERS):
        for j in range(2):
            w1 = i["ffn_w1_2"][l, j]
            put(gate_up(w1[:, :FF], w1[:, FF:]))
            put_down(i["ffn_w2_2"][l, j])
            if j:
                continue
            if l == 0:
                w = i["mix0_in_w_2"][0]
                xl, gl, q, k, v = (w[:, 512 * c:512 * c + 512] for c in range(5))
                for part in (xl, q, k, gl, v, i["mix0_out_w_2"][0]):
                    put(units(part))
            else:
                w = i["mix1_in_w_2"][0]
                kc, vc, ks, vs, kw, vw = (w[:, D + P * c:D + P * c + P] for c in range(6))
                for pair in ((kc, vc), (ks, kw)):
                    put(units(np.concatenate(pair, axis=1)))
                put(units(w[:, :D]))
                for kv in range(2):
                    w1 = i["cmp_w1_2"][0, kv].reshape(CMP_PAIRS, P, P).transpose(1, 0, 2)
                    slots[n].reshape(P, CMP_PAIRS, P)[:] = w1
                    n += 1
                put(units(np.concatenate((vs, vw), axis=1)))
                gate = np.zeros((D, 2 * P), f)
                gate[:, :48] = w[:, D + 6 * P:]
                put(units(gate))
                put(units(i["mix1_out_w_2"][0]))
    assert n == TOTAL_SLOTS and m == FFNS * KC * 2
    a["slots"], a["wd"] = slots.reshape(TOTAL_SLOTS, P, SLOT), wd.reshape(-1, P, HALF_SLOT)
    rpb = i["na_rpb"][:, :, WIN_H - ROWS:WIN_H + ROWS - 1]
    padded = np.zeros(rpb.shape[:3] + (2 * GRID_W - 1,), f)
    padded[..., GRID_W - WIN_W:GRID_W + WIN_W - 1] = rpb
    rows = np.stack([padded[..., GRID_W - 1 - c:2 * GRID_W - 1 - c] for c in range(GRID_W)], axis=3)
    bias = np.stack([rows[:, :, ROWS - 1 - r:2 * ROWS - 1 - r] for r in range(ROWS)], axis=1)
    bias = bias.reshape(LAYERS, TB, ROWS // TB, NA_HEADS, ROWS, GRID_W, GRID_W).transpose(0, 2, 5, 3, 1, 4, 6)
    a["na_bias"] = bias.reshape(LAYERS, P, NA_HEADS, TB * S)
    a["mod_w"] = i["mod_w_2"].reshape(LAYERS, KC, P, 9 * KC, P).transpose(0, 3, 2, 1, 4).reshape(MOD_CHUNKS, P, KC, P)
    a["mod_b"] = per_partition(i["mod_b_2"]).reshape(P, MOD_CHUNKS)
    a["cond"] = per_partition(i["c_2"][0])
    norms = [i[k][l] for l in range(LAYERS) for k in ("ffn1_norm", "mix_norm", "ffn2_norm")]
    norms += [i["final_norm"]] + [i["norm_g_2"][l, j] for l in range(LAYERS) for j in range(3)] + [i["final_norm_g_2"]]
    a["gains"] = per_partition(np.stack(norms))
    a["na_gain"] = per_partition(i["na_gain"])
    a["gla_gain"] = i["gla_gain"].T
    code = np.zeros((LAYERS, KC, P, CODE), f)
    wg = np.zeros((CODE, LAYERS, 256), f)
    for way, key in enumerate(("w_gate_f", "w_gate_b")):
        c = 3072 + GLA_RANK * way
        code[..., 32 * way:32 * way + GLA_RANK] = i["w_in"][:, :, c:c + GLA_RANK].reshape(LAYERS, KC, P, GLA_RANK)
        wg[32 * way:32 * way + GLA_RANK] = i[key].transpose(1, 0, 2)
    a["w_code"] = code.transpose(2, 0, 1, 3)
    a["w_gate"] = wg
    a["b_gate"] = np.concatenate([per_partition(i["b_gate_f"]), per_partition(i["b_gate_b"])], axis=2)

    def block_diagonal(w):
        full = np.zeros((2, DH, 4, 2, DH), f)
        for j in range(2):
            full[j, :, :, j] = w.reshape(4, 2, DH, DH)[:, j].transpose(1, 0, 2)
        return full.reshape(P, 4, P)

    a["lru_w"] = np.stack([block_diagonal(i["lru_wa_2"][0]), block_diagonal(i["lru_wx_2"][0])], axis=1)
    taps = i["lru_conv_w_2"][0].reshape(4, 4, P).transpose(2, 1, 0).reshape(P, 16)
    a["lru_p"] = np.concatenate([taps] + [per_partition(v.reshape(-1)) for v in (
        i["lru_conv_b_2"][0], i["lru_ba_2"][0], i["lru_bx_2"][0], i["lru_lambda_2"][0])], axis=1)
    a["cmp_pos"] = i["cmp_pos_2"][0].reshape(2, CMP_PAIRS, 2, DH).transpose(2, 3, 0, 1).reshape(P, 2, CMP_PAIRS)
    w2 = i["cmp_w2_2"][0]
    v2 = np.zeros((P, P), f)
    v2[:, :DH] = w2[1]
    a["cmp_w2"] = np.stack([np.concatenate([w2[0], w2[0]], axis=1), v2], axis=1)
    return {k: np.ascontiguousarray(v) for k, v in a.items()}


def kernel(**inputs):
    import concourse.bacc as _bacc
    from concourse.bass_utils import run_bass_kernel_spmd as _run

    arrays = lay_out({k: np.asarray(v) for k, v in inputs.items()})
    nc = _bacc.Bacc("TRN2", target_bir_lowering=False, num_devices=1)
    args = {k: nc.dram_tensor(f"in_{k}_dram", v.shape, mybir.dt.from_np(v.dtype), kind="ExternalInput").ap()
            for k, v in arrays.items()}
    out = nc.dram_tensor("out_0_dram", (P, KC, S), F32, kind="ExternalOutput").ap()
    build_program(nc, args, out)
    r = _run(nc, [{f"in_{k}_dram": v for k, v in arrays.items()}], core_ids=[0])
    got = r.results[0]["out_0_dram"]
    return got.transpose(1, 0, 2).reshape(1, D, S).transpose(0, 2, 1)
```
